# Optimizing a Trainium2 kernel written in Bass

```python
import math
import jax, jax.numpy as jnp
from jax import lax
import numpy as np

D_MODEL = 1024
BATCH = 1
SEQ = 512
DEPTH = 2

HEAD_DIM = 64
N_DIFF_HEADS = 6
DIFF_QK_DIM = HEAD_DIM // 2
N_GQA_HEADS = 6
N_GQA_KV_HEADS = 2
GQA_GROUP = N_GQA_HEADS // N_GQA_KV_HEADS
N_MEM_HEADS = 4
N_MEM = 256
GRID_W = 64
Q_BLOCK = 128
ROPE_THETA = 10000.0
NORM_EPS = 1e-6

DIFF_W = N_DIFF_HEADS * HEAD_DIM
GQA_W = N_GQA_HEADS * HEAD_DIM
GQA_KV_W = N_GQA_KV_HEADS * HEAD_DIM
MEM_W = N_MEM_HEADS * HEAD_DIM
D_MIX = DIFF_W + GQA_W + MEM_W
IN_SIZES = [DIFF_W, DIFF_W, DIFF_W, DIFF_W, GQA_W, GQA_KV_W, GQA_KV_W, GQA_W, MEM_W, MEM_W]
D_IN = sum(IN_SIZES)
IN_OFFSETS = [int(v) for v in np.cumsum(IN_SIZES)[:-1]]


def rms_norm(x, g):
    xf = x.astype(jnp.float32)
    y = xf * lax.rsqrt(jnp.mean(xf * xf, axis=-1, keepdims=True) + NORM_EPS)
    return (y * g.astype(jnp.float32)).astype(x.dtype)

def rope_tables(pos, dim):
    inv = ROPE_THETA ** (-jnp.arange(0, dim, 2, dtype=jnp.float32) / dim)
    ang = pos.astype(jnp.float32)[:, None] * inv[None, :]
    return jnp.cos(ang), jnp.sin(ang)

def apply_rope(x, cos, sin):
    xf = x.astype(jnp.float32)
    half = xf.shape[-1] // 2
    x1, x2 = xf[..., :half], xf[..., half:]
    return jnp.concatenate([x1 * cos - x2 * sin, x2 * cos + x1 * sin], axis=-1).astype(x.dtype)

def apply_axial_rope(x, row_cs, col_cs):
    half = x.shape[-1] // 2
    return jnp.concatenate([apply_rope(x[..., :half], *row_cs),
                            apply_rope(x[..., half:], *col_cs)], axis=-1)

def diff_attention(q1, q2, k1, k2, v, lam):
    B, H, S, d = q1.shape
    nb = S // Q_BLOCK
    scale = d ** -0.5

    def blockify(q):
        return jnp.moveaxis(q.reshape(B, H, nb, Q_BLOCK, d), 2, 0)

    def one(qs):
        a, b = qs
        s1 = jnp.einsum('bhqd,bhkd->bhqk', a, k1).astype(jnp.float32) * scale
        s2 = jnp.einsum('bhqd,bhkd->bhqk', b, k2).astype(jnp.float32) * scale
        p = jax.nn.softmax(s1, axis=-1) - lam * jax.nn.softmax(s2, axis=-1)
        return jnp.einsum('bhqk,bhke->bhqe', p.astype(v.dtype), v)

    o = lax.map(one, (blockify(q1), blockify(q2)))
    return jnp.moveaxis(o, 0, 2).reshape(B, H, S, v.shape[-1])

def gqa_attention(q, k, v):
    B, Hk, G, S, d = q.shape
    nb = S // Q_BLOCK
    scale = d ** -0.5
    qb = jnp.moveaxis(q.reshape(B, Hk, G, nb, Q_BLOCK, d), 3, 0)

    def one(qblk):
        s = jnp.einsum('bhgqd,bhkd->bhgqk', qblk, k).astype(jnp.float32) * scale
        p = jax.nn.softmax(s, axis=-1)
        return jnp.einsum('bhgqk,bhkd->bhgqd', p.astype(v.dtype), v)

    o = lax.map(one, qb)
    return jnp.moveaxis(o, 0, 3).reshape(B, Hk, G, S, d)

def first_inputs(seed: int = 0) -> dict:
    key = jax.random.key(seed)
    ks = jax.random.split(key, 14)
    f32 = jnp.float32
    n = jax.random.normal
    return {
        "x": n(ks[0], (BATCH, SEQ, D_MODEL), f32),
        "mem": n(ks[1], (BATCH, N_MEM, D_MODEL), f32),
        "pre_norm": 1.0 + 0.02 * n(ks[2], (DEPTH, D_MODEL), f32),
        "w_in": n(ks[3], (DEPTH, D_MODEL, D_IN), f32) * D_MODEL ** -0.5,
        "diff_lambda": 0.1 * n(ks[4], (DEPTH, 4, DIFF_QK_DIM), f32),
        "diff_subln": 1.0 + 0.02 * n(ks[5], (DEPTH, HEAD_DIM), f32),
        "gqa_q_norm": 1.0 + 0.02 * n(ks[6], (DEPTH, HEAD_DIM), f32),
        "gqa_k_norm": 1.0 + 0.02 * n(ks[7], (DEPTH, HEAD_DIM), f32),
        "mem_norm": 1.0 + 0.02 * n(ks[8], (DEPTH, D_MODEL), f32),
        "w_mem_kv": n(ks[9], (DEPTH, D_MODEL, 2 * MEM_W), f32) * D_MODEL ** -0.5,
        "w_out": n(ks[10], (DEPTH, D_MIX, D_MODEL), f32) * D_MIX ** -0.5,
        "post_norm": 1.0 + 0.02 * n(ks[11], (DEPTH, D_MODEL), f32),
    }

def first_block(x, mem, pre_norm, w_in, diff_lambda, diff_subln, gqa_q_norm, gqa_k_norm,
              mem_norm, w_mem_kv, w_out, post_norm):
    B, S, _ = x.shape
    M = mem.shape[1]
    ROWS = S // GRID_W
    t = jnp.arange(S, dtype=jnp.int32)
    row = jnp.repeat(jnp.arange(ROWS, dtype=jnp.int32), GRID_W)
    col = jnp.tile(jnp.arange(GRID_W, dtype=jnp.int32), ROWS)
    lin_cs = rope_tables(t, DIFF_QK_DIM)
    row_cs = rope_tables(row, HEAD_DIM // 2)
    col_cs = rope_tables(col, HEAD_DIM // 2)

    for l in range(DEPTH):
        lambda_init = 0.8 - 0.6 * math.exp(-0.3 * l)
        h = rms_norm(x, pre_norm[l])
        proj = h @ w_in[l]
        (dq, dk, dv, dgate, gq, gk, gv, ggate, mq, mgate) = jnp.split(proj, IN_OFFSETS, axis=-1)

        dq = apply_rope(dq.reshape(B, S, N_DIFF_HEADS, 2, DIFF_QK_DIM).transpose(0, 2, 3, 1, 4), *lin_cs)
        dk = apply_rope(dk.reshape(B, S, N_DIFF_HEADS, 2, DIFF_QK_DIM).transpose(0, 2, 3, 1, 4), *lin_cs)
        dv = dv.reshape(B, S, N_DIFF_HEADS, HEAD_DIM).transpose(0, 2, 1, 3)
        lp = diff_lambda[l].astype(jnp.float32)
        lam = jnp.exp(jnp.sum(lp[0] * lp[1])) - jnp.exp(jnp.sum(lp[2] * lp[3])) + lambda_init
        oa = diff_attention(dq[:, :, 0], dq[:, :, 1], dk[:, :, 0], dk[:, :, 1], dv, lam)
        oa = rms_norm(oa, diff_subln[l]) * (1.0 - lambda_init)
        oa = oa.transpose(0, 2, 1, 3).reshape(B, S, DIFF_W) * jax.nn.silu(dgate)

        gq = rms_norm(gq.reshape(B, S, N_GQA_HEADS, HEAD_DIM).transpose(0, 2, 1, 3), gqa_q_norm[l])
        gq = apply_axial_rope(gq, row_cs, col_cs).reshape(B, N_GQA_KV_HEADS, GQA_GROUP, S, HEAD_DIM)
        gk = rms_norm(gk.reshape(B, S, N_GQA_KV_HEADS, HEAD_DIM).transpose(0, 2, 1, 3), gqa_k_norm[l])
        gk = apply_axial_rope(gk, row_cs, col_cs)
        gv = gv.reshape(B, S, N_GQA_KV_HEADS, HEAD_DIM).transpose(0, 2, 1, 3)
        ob = gqa_attention(gq, gk, gv).reshape(B, N_GQA_HEADS, S, HEAD_DIM)
        ob = ob.transpose(0, 2, 1, 3).reshape(B, S, GQA_W) * jax.nn.silu(ggate)

        mkv = rms_norm(mem, mem_norm[l]) @ w_mem_kv[l]
        mk, mv = jnp.split(mkv, 2, axis=-1)
        mk = mk.reshape(B, M, N_MEM_HEADS, HEAD_DIM).transpose(0, 2, 1, 3)
        mv = mv.reshape(B, M, N_MEM_HEADS, HEAD_DIM).transpose(0, 2, 1, 3)
        mq = mq.reshape(B, S, N_MEM_HEADS, HEAD_DIM).transpose(0, 2, 1, 3)
        sm = jnp.einsum('bhsd,bhmd->bhsm', mq, mk).astype(jnp.float32) * HEAD_DIM ** -0.5
        pm = jax.nn.softmax(sm, axis=-1)
        om = jnp.einsum('bhsm,bhmd->bhsd', pm.astype(mv.dtype), mv)
        om = om.transpose(0, 2, 1, 3).reshape(B, S, MEM_W) * jax.nn.silu(mgate)

        y = jnp.concatenate([oa, ob, om], axis=-1) @ w_out[l]
        x = x + rms_norm(y, post_norm[l])
    return x


D_MIX_2 = D_MODEL
ATT_HEAD_DIM = 64
ATT_WIDTH = D_MIX_2 // 2
ATT_HEADS = ATT_WIDTH // ATT_HEAD_DIM
DILATED_GROUPS = ((128, 1), (512, 4), (2048, 16))
ROPE_THETA_2 = 500000.0
ROPE_DIM = ATT_HEAD_DIM // 4
MLSTM_WIDTH = D_MIX_2 - ATT_WIDTH
MLSTM_HEADS = 4
MLSTM_HEAD_DIM = MLSTM_WIDTH // MLSTM_HEADS
MLSTM_CHUNK = 64
CONV_WIDTH = 5
N_GATES = 4
IN_WIDTH = 3 * ATT_WIDTH + 4 * MLSTM_WIDTH + N_GATES * MLSTM_HEADS
D_FF = ((8 * D_MODEL // 3 + 127) // 128) * 128
N_NORMS = 6
NEG_BIG = -1e30


def rms_norm_2(x, gain):
    xf = x.astype(jnp.float32)
    y = xf * lax.rsqrt(jnp.mean(xf * xf, axis=-1, keepdims=True) + NORM_EPS)
    return (y * gain).astype(x.dtype)

def swiglu(h, w_in, w_out):
    gu = h @ w_in
    g, u = jnp.split(gu, 2, axis=-1)
    return (jax.nn.silu(g) * u) @ w_out

def split_heads(t, n_heads):
    b, s, w = t.shape
    return t.reshape(b, s, n_heads, w // n_heads).transpose(0, 2, 1, 3)

def merge_heads(t):
    b, h, s, dh = t.shape
    return t.transpose(0, 2, 1, 3).reshape(b, s, h * dh)

def partial_rotary(t, positions):
    half = ROPE_DIM // 2
    inv_freq = ROPE_THETA_2 ** (-jnp.arange(half, dtype=jnp.float32) / half)
    ang = positions.astype(jnp.float32)[:, None] * inv_freq[None, :]
    cos, sin = jnp.cos(ang), jnp.sin(ang)
    t1 = t[..., :half].astype(jnp.float32)
    t2 = t[..., half:ROPE_DIM].astype(jnp.float32)
    rot = jnp.concatenate([t1 * cos - t2 * sin, t2 * cos + t1 * sin], axis=-1).astype(t.dtype)
    return jnp.concatenate([rot, t[..., ROPE_DIM:]], axis=-1)

def dilated_window_attention(q, k, v, window, dilation):
    b, h, s, dh = q.shape
    n_side = (window // 2) // dilation
    blk = n_side
    unit = dilation * blk
    s_pad = -(-s // unit) * unit
    n_blk = s_pad // unit
    sub_len = s_pad // dilation

    def to_blocks(t):
        t = jnp.pad(t, ((0, 0), (0, 0), (0, s_pad - s), (0, 0)))
        t = t.reshape(b, h, sub_len, dilation, dh).transpose(0, 1, 3, 2, 4)
        return t.reshape(b, h, dilation, n_blk, blk, dh)

    def neighbours(t):
        tp = jnp.pad(t, ((0, 0), (0, 0), (0, 0), (1, 1), (0, 0), (0, 0)))
        return jnp.concatenate([tp[:, :, :, :-2], tp[:, :, :, 1:-1], tp[:, :, :, 2:]], axis=4)

    qb = to_blocks(q)
    kn = neighbours(to_blocks(k))
    vn = neighbours(to_blocks(v))

    r = jnp.arange(dilation)[:, None, None, None]
    bi = jnp.arange(n_blk)[None, :, None, None]
    qi = jnp.arange(blk)[None, None, :, None]
    kj = jnp.arange(3 * blk)[None, None, None, :]
    m_q = bi * blk + qi
    m_k = bi * blk - blk + kj
    valid = (m_k >= 0) & (m_k * dilation + r < s) & (jnp.abs(m_q - m_k) <= n_side)

    scores = jnp.einsum('bhrnid,bhrnjd->bhrnij', qb, kn).astype(jnp.float32)
    scores = jnp.where(valid, scores, NEG_BIG)
    lse = jax.nn.logsumexp(scores, axis=-1)
    p = jnp.exp(scores - lse[..., None])
    out = jnp.einsum('bhrnij,bhrnjd->bhrnid', p, vn.astype(jnp.float32))

    def from_blocks(t):
        rest = t.shape[5:]
        t = t.reshape((b, h, dilation, sub_len) + rest)
        t = jnp.moveaxis(t, 2, 3).reshape((b, h, s_pad) + rest)
        return t[:, :, :s]

    return from_blocks(out), from_blocks(lse)

def dilated_attention_mixture(q, k, v):
    outs, lses = [], []
    for window, dilation in DILATED_GROUPS:
        o, l = dilated_window_attention(q, k, v, window, dilation)
        outs.append(o)
        lses.append(l)
    weights = jax.nn.softmax(jnp.stack(lses, axis=0), axis=0)
    return jnp.sum(weights[..., None] * jnp.stack(outs, axis=0), axis=0)

def mlstm_direction(q, k, v, i_pre, f_pre):
    b, h, s, dh = q.shape
    n_chunks = s // MLSTM_CHUNK
    log_f = jax.nn.log_sigmoid(f_pre)
    tril = jnp.tril(jnp.ones((MLSTM_CHUNK, MLSTM_CHUNK), dtype=bool))

    def chunks(t):
        return jnp.moveaxis(t.reshape((b, h, n_chunks, MLSTM_CHUNK) + t.shape[3:]), 2, 0)

    def step(carry, inp):
        c_mat, n_vec, m_prev = carry
        qc, kc, vc, ic, lfc = inp
        cum = jnp.cumsum(lfc, axis=-1)
        decay = cum[..., :, None] - cum[..., None, :] + ic[..., None, :]
        decay = jnp.where(tril, decay, -jnp.inf)
        inter = cum + m_prev[..., None]
        m_t = jnp.maximum(inter, jnp.max(decay, axis=-1))
        w_intra = jnp.exp(decay - m_t[..., None])
        w_inter = jnp.exp(inter - m_t)
        qk = jnp.einsum('bhtd,bhsd->bhts', qc, kc) * w_intra
        num = (jnp.einsum('bhts,bhse->bhte', qk, vc)
               + w_inter[..., None] * jnp.einsum('bhed,bhtd->bhte', c_mat, qc))
        den = jnp.sum(qk, axis=-1) + w_inter * jnp.einsum('bhd,bhtd->bht', n_vec, qc)
        h_out = num / jnp.maximum(jnp.abs(den), jnp.exp(-m_t))[..., None]
        total = cum[..., -1]
        w_src = total[..., None] - cum + ic
        m_new = jnp.maximum(total + m_prev, jnp.max(w_src, axis=-1))
        carry_scale = jnp.exp(total + m_prev - m_new)
        w_src = jnp.exp(w_src - m_new[..., None])
        c_new = carry_scale[..., None, None] * c_mat + jnp.einsum('bhs,bhse,bhsd->bhed', w_src, vc, kc)
        n_new = carry_scale[..., None] * n_vec + jnp.einsum('bhs,bhsd->bhd', w_src, kc)
        return (c_new, n_new, m_new), h_out

    init = (jnp.zeros((b, h, dh, dh), jnp.float32),
            jnp.zeros((b, h, dh), jnp.float32),
            jnp.full((b, h), NEG_BIG, jnp.float32))
    _, hs = lax.scan(step, init, (chunks(q), chunks(k), chunks(v), chunks(i_pre), chunks(log_f)))
    return jnp.moveaxis(hs, 0, 2).reshape(b, h, s, dh)

def token_mixer(h, w_in, conv_w, conv_b, gate_bias, mlstm_norm_gain, w_out):
    b, s, _ = h.shape
    proj = h @ w_in
    sizes = [ATT_WIDTH] * 3 + [MLSTM_WIDTH] * 4 + [N_GATES * MLSTM_HEADS]
    cuts = np.cumsum(sizes)[:-1].tolist()
    aq, ak, av, mq, mk, mv, mo, mg = jnp.split(proj, cuts, axis=-1)

    positions = jnp.arange(s)
    aq = partial_rotary(split_heads(aq, ATT_HEADS), positions) * (ATT_HEAD_DIM ** -0.5)
    ak = partial_rotary(split_heads(ak, ATT_HEADS), positions)
    av = split_heads(av, ATT_HEADS)
    attn_out = merge_heads(dilated_attention_mixture(aq, ak, av))

    qk = jnp.concatenate([mq, mk], axis=-1)
    qk = lax.conv_general_dilated(qk, conv_w.reshape(CONV_WIDTH, 1, 2 * MLSTM_WIDTH).astype(qk.dtype),
                                  window_strides=(1,), padding='SAME',
                                  dimension_numbers=('NWC', 'WIO', 'NWC'),
                                  feature_group_count=2 * MLSTM_WIDTH)
    qk = jax.nn.silu(qk + conv_b)
    mq, mk = jnp.split(qk, 2, axis=-1)
    mq = split_heads(mq, MLSTM_HEADS).astype(jnp.float32)
    mk = split_heads(mk, MLSTM_HEADS).astype(jnp.float32) * (MLSTM_HEAD_DIM ** -0.5)
    mv = split_heads(mv, MLSTM_HEADS).astype(jnp.float32)
    gates = mg.astype(jnp.float32).reshape(b, s, N_GATES, MLSTM_HEADS) + gate_bias
    gates = gates.transpose(2, 0, 3, 1)
    h_fwd = mlstm_direction(mq, mk, mv, gates[0], gates[1])
    flip = lambda t: jnp.flip(t, axis=2)
    h_bwd = flip(mlstm_direction(flip(mq), flip(mk), flip(mv), flip(gates[2]), flip(gates[3])))
    cell = h_fwd + h_bwd
    cell = cell * lax.rsqrt(jnp.mean(cell * cell, axis=-1, keepdims=True) + NORM_EPS)
    mlstm_out = jax.nn.sigmoid(mo.astype(jnp.float32)) * (merge_heads(cell) * mlstm_norm_gain)

    merged = jnp.concatenate([attn_out, mlstm_out], axis=-1).astype(h.dtype)
    return merged @ w_out

def second_inputs(seed: int = 0) -> dict:
    key = jax.random.key(seed)
    ks = jax.random.split(key, 12)
    f32 = jnp.float32
    x = jax.random.normal(ks[0], (BATCH, SEQ, D_MODEL), f32)
    norm_gain = 1.0 + 0.05 * jax.random.normal(ks[1], (DEPTH, N_NORMS, D_MODEL), f32)
    ffn_w_in = jax.random.normal(ks[2], (DEPTH, 2, D_MODEL, 2 * D_FF), f32) * D_MODEL ** -0.5
    ffn_w_out = jax.random.normal(ks[3], (DEPTH, 2, D_FF, D_MODEL), f32) * D_FF ** -0.5
    mix_w_in = jax.random.normal(ks[4], (DEPTH, D_MODEL, IN_WIDTH), f32) * D_MODEL ** -0.5
    conv_w = jax.random.normal(ks[5], (DEPTH, CONV_WIDTH, 2 * MLSTM_WIDTH), f32) * CONV_WIDTH ** -0.5
    conv_b = 0.01 * jax.random.normal(ks[6], (DEPTH, 2 * MLSTM_WIDTH), f32)
    i_bias = 0.1 * jax.random.normal(ks[7], (DEPTH, 2, MLSTM_HEADS), f32)
    f_bias = (jnp.linspace(3.0, 6.0, MLSTM_HEADS, dtype=f32)[None, None, :]
              + 0.1 * jax.random.normal(ks[8], (DEPTH, 2, MLSTM_HEADS), f32))
    gate_bias = jnp.stack([i_bias[:, 0], f_bias[:, 0], i_bias[:, 1], f_bias[:, 1]], axis=1)
    mlstm_norm_gain = 1.0 + 0.05 * jax.random.normal(ks[9], (DEPTH, MLSTM_WIDTH), f32)
    mix_w_out = jax.random.normal(ks[10], (DEPTH, D_MIX_2, D_MODEL), f32) * D_MIX_2 ** -0.5
    return {"x": x, "norm_gain": norm_gain, "ffn_w_in": ffn_w_in, "ffn_w_out": ffn_w_out,
            "mix_w_in": mix_w_in, "conv_w": conv_w, "conv_b": conv_b, "gate_bias": gate_bias,
            "mlstm_norm_gain": mlstm_norm_gain, "mix_w_out": mix_w_out}

def second_block(x, norm_gain, ffn_w_in, ffn_w_out, mix_w_in, conv_w, conv_b, gate_bias,
              mlstm_norm_gain, mix_w_out):
    for layer in range(DEPTH):
        g = norm_gain[layer]
        h = swiglu(rms_norm_2(x, g[0]), ffn_w_in[layer, 0], ffn_w_out[layer, 0])
        x = x + 0.5 * rms_norm_2(h, g[1])
        h = token_mixer(rms_norm_2(x, g[2]), mix_w_in[layer], conv_w[layer], conv_b[layer],
                        gate_bias[layer], mlstm_norm_gain[layer], mix_w_out[layer])
        x = x + rms_norm_2(h, g[3])
        h = swiglu(rms_norm_2(x, g[4]), ffn_w_in[layer, 1], ffn_w_out[layer, 1])
        x = x + 0.5 * rms_norm_2(h, g[5])
    return x


def setup_inputs(seed=0):
    out = dict(first_inputs(seed))
    for name, value in second_inputs(seed + 1).items():
        if name != "x":
            out[name + "_2"] = value
    return out


def reference(
    x, mem, pre_norm, w_in, diff_lambda, diff_subln, gqa_q_norm, gqa_k_norm, mem_norm, w_mem_kv,
    w_out, post_norm, norm_gain_2, ffn_w_in_2, ffn_w_out_2, mix_w_in_2, conv_w_2, conv_b_2,
    gate_bias_2, mlstm_norm_gain_2, mix_w_out_2,
):
    x = first_block(
        x, mem, pre_norm, w_in, diff_lambda, diff_subln, gqa_q_norm, gqa_k_norm, mem_norm,
        w_mem_kv, w_out, post_norm,
    )
    return second_block(
        x, norm_gain_2, ffn_w_in_2, ffn_w_out_2, mix_w_in_2, conv_w_2, conv_b_2, gate_bias_2,
        mlstm_norm_gain_2, mix_w_out_2,
    )


_drawn_inputs = setup_inputs


def setup_inputs(seed=0):
    import zlib

    import numpy as np

    out = dict(_drawn_inputs(seed))
    spreads = {}
    factors = {'gqa_q_norm': 8.0,
     'gqa_k_norm': 8.0,
     'mem_norm': 8.0,
     'conv_b_2': 8.0,
     'diff_lambda': 3.504,
     'diff_subln': 6.342}
    for name, (base, spread) in spreads.items():
        noise = np.random.default_rng([zlib.crc32(name.encode()), seed]).standard_normal(out[name].shape)
        drawn = base * np.exp(spread * noise) if base else spread * noise
        out[name] = __import__('jax').numpy.asarray(drawn.astype(out[name].dtype))
    for name, factor in factors.items():
        out[name] = (out[name] * factor).astype(out[name].dtype)
    return out
```

```python
import math
from contextlib import ExitStack, contextmanager

import numpy as np

import concourse.bass as bass
from concourse import mybir

F32 = mybir.dt.float32
F32R = mybir.dt.float32r
BF16 = mybir.dt.bfloat16
ALU = mybir.AluOpType
ACT = mybir.ActivationFunctionType
AX = mybir.AxisListType

P = 128
S = 512
D = 1024
NT = S // P
NC = D // P
DEPTH = 2
EPS = 1e-6
TILE = 2048
HD = 64
N_DIFF, N_GQA, N_MEMH = 6, 6, 4
N_MEM = 256
FC = 22
MH = 4
CONV = 5
NEG = -1e30

B1_KV, B1_PROJ, B1_OUT, B1_TILES = 0, 2, 14, 18
B2_IN1, B2_OUT1, B2_QK, B2_CONV, B2_ROW, B2_MIXOUT, B2_IN2, B2_OUT2, B2_TILES = 0, 22, 33, 37, 41, 47, 51, 73, 84

AT_X = 16512
AT_HH = AT_X + 16384
AT_HL = AT_HH + 16384
AT_RAW = AT_HL + 16384
AT_WHI = AT_RAW + 16384
AT_WLO = AT_WHI + 16384
AT_GBC = AT_WLO + 16384
AT_SMALL = AT_GBC + 4096
AT_R = AT_SMALL + 8000
END = 229344


class Chain:

    def __init__(self, eng, sem):
        self.eng, self.sem, self.n = eng, sem, 0

    def __call__(self, ins):
        ins.then_inc(self.sem, 1)
        self.n += 1
        self.eng.wait_ge(self.sem, self.n)


def build(nc, a):
    with ExitStack() as ctx:
        def at(name, shape, offset, dt=F32):
            size = int(np.prod(shape[1:])) * (2 if dt == BF16 else 4)
            assert offset % 32 == 0 and offset + size <= END, (name, offset + size)
            return nc.alloc_sbuf_tensor_at(name, shape, dt, offset=offset)

        X = at("X", [P, NT, D], AT_X)
        hTh = at("hTh", [P, NC, S], AT_HH, F32R)
        hTl = at("hTl", [P, NC, S], AT_HL, F32R)
        raw = at("raw", [P, 2, TILE], AT_RAW)
        whi = at("whi", [P, 2, TILE], AT_WHI, F32R)
        wlo = at("wlo", [P, 2, TILE], AT_WLO, F32R)
        gbc = at("gbc", [P, D], AT_GBC)

        small_at = [AT_SMALL]

        def small(name, shape, dt=F32):
            t = at(name, shape, small_at[0], dt)
            small_at[0] += -(-int(np.prod(shape[1:])) * (2 if dt == BF16 else 4) // 32) * 32
            assert small_at[0] <= AT_R, name
            return t

        ident = small("ident", [P, P])
        junk_ffn = at("junk_ffn", [P, NT, D], AT_HH, BF16)
        junk_mix = at("junk_mix", [P, NT, D], AT_R + 16384, BF16)
        junk_mem = at("junk_mem", [P, 2, D], AT_R + 77824)
        junk_head = small("junk_head", [P, MH, P], BF16)
        halfneg = small("halfneg", [P, 1])
        gcol = small("gcol", [P, 6, NC])
        sums = small("sums", [P, 4 * NT])
        rinv = small("rinv", [P, 4 * NT])
        ysum = small("ysum", [P, 3 * NT])
        yinv = small("yinv", [P, 3 * NT])
        negmax = small("negmax", [P, 2, 2])
        rowmax = small("rowmax", [P, 2, 1])
        esum = small("esum", [P, 2, 2])
        erec = small("erec", [P, 4, 2])
        lamc = small("lamc", [P, 2])
        lam = small("lam", [P, 8])
        hsum = small("hsum", [P, NT, 8])
        hinv = small("hinv", [P, NT, 8])
        oinv = small("oinv", [P, NT, 8])
        osum = small("osum", [P, NT, 8])
        gate_bias = small("gate_bias", [P, 16])
        gates = small("gates", [P, NT, 2, 2, MH])
        gtmp = small("gtmp", [P, NT, 2, MH])
        gexp = small("gexp", [P, NT, 2, MH])
        logf = small("logf", [P, NT, 2, MH])
        cum = small("cum", [P, NT, 2, MH])
        acol = small("acol", [P, NT, 2, MH])
        mmax = small("mmax", [P, NT, 2, MH])
        nmmax = small("nmmax", [P, NT, 2, MH])
        mexp = small("mexp", [P, NT, 2, MH])
        den = small("den", [P, NT, 2, MH])
        dtmp = small("dtmp", [P, NT, 2, MH])
        drec = small("drec", [P, NT, 2, MH])
        gate_raw = small("gate_raw", [P, NC, 16])
        gate_hi = small("gate_hi", [P, NC, 16], F32R)
        gate_lo = small("gate_lo", [P, NC, 16], F32R)
        upto = small("upto", [P, 2, P])
        ones = small("ones", [P, 1])
        conv_w = small("conv_w", [P, 8, CONV])
        conv_b = small("conv_b", [P, 8])
        rot_cos = small("rot_cos", [P, NT, 8])
        rot_sin = small("rot_sin", [P, NT, 8])

        ps = ctx.enter_context(nc.psum_tensor("ps", [P, 8, 512], F32))

        names = []

        def sem(name):
            s = ctx.enter_context(nc.semaphore(name))
            names.append(s)
            return s

        raw_in = [sem("raw_in0"), sem("raw_in1")]
        hi_ready, lo_ready = sem("hi_ready"), sem("lo_ready")
        w_used = sem("w_used")
        par = sem("par")
        par2 = sem("par2")
        gain_in = sem("gain_in")
        sq_done, r_done, xn_done = sem("sq_done"), sem("r_done"), sem("xn_done")
        tr_done, th_done, tl_done = sem("tr_done"), sem("th_done"), sem("tl_done")
        y_done, ysq_done, yr_done, ysc_done, x_done = (sem("y_done"), sem("ysq_done"), sem("yr_done"),
                                                       sem("ysc_done"), sem("x_done"))
        proj_done = sem("proj_done")
        ev_a, ev_v = sem("ev_a"), sem("ev_v")
        s_done, mx_done, ex_done, nm_done, t_done, pt_done, pv_done, o_done = (
            sem("s_done"), sem("mx_done"), sem("ex_done"), sem("nm_done"), sem("t_done"),
            sem("pt_done"), sem("pv_done"), sem("o_done"))
        dchain, pchain, achain = sem("dchain"), sem("pchain"), sem("achain")
        q_ready = sem("q_ready")
        qt_done, qte_a, qte_v = sem("qt_done"), sem("qte_a"), sem("qte_v")
        g_v, g_p, g_a = sem("g_v"), sem("g_p"), sem("g_a")
        o_ready = sem("o_ready")
        io = sem("io")
        gu_done, silu_done, gated, acth_done, actl_done = (sem("gu_done"), sem("silu_done"), sem("gated"),
                                                          sem("acth_done"), sem("actl_done"))
        pad_done, cv_done, cs_done = sem("pad_done"), sem("cv_done"), sem("cs_done")
        m1_done, m2_done, ms_done, mt_done, mpt_done, mg_done, mpv_done = (
            sem("m1_done"), sem("m2_done"), sem("ms_done"), sem("mt_done"), sem("mpt_done"), sem("mg_done"),
            sem("mpv_done"))
        mw_done, mr_done = sem("mw_done"), sem("mr_done")
        sm_t, sm_e = sem("sm_t"), sem("sm_e")
        cs_mm, mw2_done, mixpar, ab_a, ab_v, one_done = (sem("cs_mm"), sem("mw2_done"), sem("mixpar"), sem("ab_a"),
                                                         sem("ab_v"), sem("one_done"))
        nums = [s.num for s in names]
        assert nums == list(range(nums[0], nums[0] + len(nums)))

        def stream(sp, weights, layer, tiles):
            for T in range(2):
                sp.dma_start(raw[:, T, :], weights[bass.ds(layer * tiles + T, 1)].rearrange("a p n -> (a p) n")
                             ).then_inc(raw_in[T], 16)
            with sp.Fori(1, tiles // 2) as i:
                for slot in range(2):
                    sp.wait_ge(lo_ready, i * 2 + (slot - 1))
                    sp.dma_start(raw[:, slot, :],
                                 weights[bass.ds(layer * tiles + i * 2 + slot, 1)].rearrange("a p n -> (a p) n")
                                 ).then_inc(raw_in[slot], 16)

        def hi_part(act, T, i=0):
            act.wait_ge(raw_in[T % 2], 16 * (T // 2 + 1) + i * 16)
            if T >= 2:
                act.wait_ge(w_used, T - 1 + i * 2)
            nc.scalar.activation(whi[:, T % 2, :], raw[:, T % 2, :], ACT.Copy).then_inc(hi_ready, 1)

        def lo_part(dve, T, i=0):
            dve.wait_ge(hi_ready, T + 1 + i * 2)
            nc.vector.tensor_tensor(wlo[:, T % 2, :], raw[:, T % 2, :], whi[:, T % 2, :].bitcast(F32),
                                    ALU.subtract).then_inc(lo_ready, 1)

        def three(out, l_hi, l_lo, r_hi, r_lo, start, stop):
            nc.tensor.matmul(out, l_hi, r_hi, start=start, stop=False)
            nc.tensor.matmul(out, l_hi, r_lo, start=False, stop=False)
            return nc.tensor.matmul(out, l_lo, r_hi, start=False, stop=stop)

        def moving(T):
            return (whi[:, T % 2, :].rearrange("p (b n) -> p b n", n=512),
                    wlo[:, T % 2, :].rearrange("p (b n) -> p b n", n=512))

        def stationary(T):
            return (whi[:, T % 2, :].rearrange("p (c k n) -> p c k n", c=2, k=NC),
                    wlo[:, T % 2, :].rearrange("p (c k n) -> p c k n", c=2, k=NC))

        XN = at("XN", [P, NT, D], AT_R)

        def prenorm_act(act, n):
            for t in range(NT):
                if n:
                    act.wait_ge(x_done, NT * (n - 1) + t + 1)
                nc.scalar.activation(XN[:, t, :], X[:, t, :], ACT.Square,
                                     accum_out=sums[:, NT * n + t:NT * n + t + 1]).then_inc(sq_done, 1)

        def prenorm_pool(pool, chain, n):
            for t in range(NT):
                c = slice(NT * n + t, NT * n + t + 1)
                pool.wait_ge(sq_done, NT * n + t + 1)
                chain(nc.gpsimd.tensor_scalar(sums[:, c], sums[:, c], 1.0 / D, EPS, ALU.mult, ALU.add))
                nc.gpsimd.tensor_tensor(rinv[:, c], sums[:, c], halfneg[:], ALU.pow).then_inc(r_done, 1)

        def prenorm_dve(dve, n):
            for t in range(NT):
                dve.wait_ge(r_done, NT * n + t + 1)
                nc.vector.tensor_scalar(XN[:, t, :], X[:, t, :], rinv[:, NT * n + t:NT * n + t + 1], None,
                                        ALU.mult).then_inc(xn_done, 1)

        def turn_pe(pe, m, source, ready):
            for c in range(NC):
                for t in range(NT):
                    if c == 0:
                        pe.wait_ge(*ready(t))
                    last = nc.tensor.transpose(ps[:, c, t * P:(t + 1) * P], source[:, t, c * P:(c + 1) * P],
                                               ident[:])
                last.then_inc(tr_done, 1)

        def turn_act(act, m, gain):
            for c in range(NC):
                act.wait_ge(tr_done, NC * m + c + 1)
                nc.scalar.activation(hTh[:, c, :], ps[:, c, :], ACT.Copy,
                                     scale=gcol[:, gain, c:c + 1] if gain is not None else 1.0
                                     ).then_inc(th_done, 1)

        def turn_dve(dve, m, gain):
            for c in range(NC):
                dve.wait_ge(th_done, NC * m + c + 1)
                nc.vector.scalar_tensor_tensor(
                    hTl[:, c, :], ps[:, c, :], gcol[:, gain, c:c + 1] if gain is not None else 1.0,
                    hTh[:, c, :].bitcast(F32), ALU.mult, ALU.subtract).then_inc(tl_done, 1)

        YT = at("YT", [P, 2, D], AT_R + 94208)

        def y_of(t):
            return ps[:, 2 * t:2 * t + 2, :]

        def out_pe(pe, T0, nk, hi, lo):
            for T in range(T0, T0 + 2 * nk // 4):
                w_hi, w_lo = moving(T)
                pe.wait_ge(lo_ready, T + 1)
                final = T == T0 + 2 * nk // 4 - 1
                for t in range(NT):
                    for b in range(4):
                        half, k = divmod(4 * (T - T0) + b, nk)
                        last = three(ps[:, 2 * t + half, :], hi[:, k, t * P:(t + 1) * P],
                                     lo[:, k, t * P:(t + 1) * P], w_hi[:, b, :], w_lo[:, b, :],
                                     start=k == 0, stop=k == nk - 1)
                    if final and t < NT - 1:
                        last.then_inc(y_done, 1)
                last.then_inc(w_used, 1)

        def postnorm_act(act, n, T_last, junk):
            for t in range(NT):
                if t < NT - 1:
                    act.wait_ge(y_done, (NT - 1) * n + t + 1)
                else:
                    act.wait_ge(w_used, T_last + 1)
                nc.scalar.activation(junk[:, t, :].rearrange("p (h n) -> p h n", h=2), y_of(t), ACT.Square,
                                     accum_out=ysum[:, NT * n + t:NT * n + t + 1]).then_inc(ysq_done, 1)

        def postnorm_pool(pool, chain, n, factor):
            for t in range(NT):
                c = slice(NT * n + t, NT * n + t + 1)
                pool.wait_ge(ysq_done, NT * n + t + 1)
                chain(nc.gpsimd.tensor_scalar(ysum[:, c], ysum[:, c], 1.0 / D, EPS, ALU.mult, ALU.add))
                if factor == 1.0:
                    nc.gpsimd.tensor_tensor(yinv[:, c], ysum[:, c], halfneg[:], ALU.pow).then_inc(yr_done, 1)
                else:
                    chain(nc.gpsimd.tensor_tensor(yinv[:, c], ysum[:, c], halfneg[:], ALU.pow))
                    nc.gpsimd.tensor_scalar(yinv[:, c], yinv[:, c], factor, None, ALU.mult).then_inc(yr_done, 1)
                if t:
                    add_residual(pool, n, t - 1)
            add_residual(pool, n, NT - 1)

        def add_residual(pool, n, t):
            pool.wait_ge(ysc_done, NT * n + t + 1)
            nc.gpsimd.tensor_tensor(X[:, t, :], X[:, t, :], YT[:, t % 2, :], ALU.add).then_inc(x_done, 1)

        def postnorm_dve(dve, n):
            dve.wait_ge(gain_in, 16 * (n + 1))
            for t in range(NT):
                dve.wait_ge(yr_done, NT * n + t + 1)
                if t >= 2:
                    dve.wait_ge(x_done, NT * n + t - 1)
                nc.vector.scalar_tensor_tensor(
                    YT[:, t % 2, :].rearrange("p (h n) -> p h n", h=2), y_of(t),
                    yinv[:, NT * n + t:NT * n + t + 1], gbc[:].rearrange("p (h n) -> p h n", h=2),
                    ALU.mult, ALU.mult).then_inc(ysc_done, 1)

        def project_pe(pe, T0, b, banks):
            for half in range(2):
                T = T0 + half
                w_hi, w_lo = moving(T)
                pe.wait_ge(lo_ready, T + 1)
                for t in range(NT):
                    for kk in range(4):
                        k = 4 * half + kk
                        last = three(ps[:, banks + t, :], hTh[:, k, t * P:(t + 1) * P],
                                     hTl[:, k, t * P:(t + 1) * P], w_hi[:, kk, :], w_lo[:, kk, :],
                                     start=k == 0, stop=k == NC - 1)
                    if t == NT - 1:
                        last.then_inc(w_used, 1)
                    elif half == 1:
                        last.then_inc(proj_done, 1)

        def projected(eng, T0, b, t):
            if t == NT - 1:
                eng.wait_ge(w_used, T0 + 2)
            else:
                eng.wait_ge(proj_done, (NT - 1) * b + t + 1)

        E = at("E", [P, 2, 2, S], AT_R + 77824)
        G = at("G", [P, 2, S], AT_R + 86016)
        PT = at("PT", [P, 2, 4, P], AT_R + 90112)
        MS = at("MS", [P, 2, S], AT_R + 94208)

        def probs(u, unit):
            return G[:, u % 2, :] if unit["kind"] in ("diff", "dilated") else E[:, u % 2, 0, :]

        def attend_pe(pe, units):
            for s in range(len(units) + 2):
                if s < len(units):
                    for j, (q, k) in enumerate(units[s]["scores"]):
                        last = nc.tensor.matmul(ps[:, 2 * (s % 2) + j, 0:units[s]["keys"]], q, k,
                                                start=True, stop=True)
                    last.then_inc(s_done, 1)
                if 1 <= s <= len(units):
                    u = s - 1
                    if units[u]["kind"] == "diff":
                        pe.wait_ge(nm_done, u + 1)
                    else:
                        pe.wait_ge(ex_done, u + 1)
                    pr = probs(u, units[u])
                    for b in range(units[u]["keys"] // P):
                        last = nc.tensor.transpose(ps[:, 4 + u % 2, b * P:(b + 1) * P],
                                                   pr[:, b * P:(b + 1) * P], ident[:])
                    last.then_inc(t_done, 1)
                if s >= 2:
                    u = s - 2
                    pe.wait_ge(pt_done, u + 1)
                    if u >= 2:
                        pe.wait_ge(o_done, u - 1)
                    nb = units[u]["keys"] // P
                    for b in range(nb):
                        last = nc.tensor.matmul(ps[:, 6 + u % 2, 0:HD], PT[:, u % 2, b, :], units[u]["v"][b],
                                                start=b == 0, stop=b == nb - 1)
                    last.then_inc(pv_done, 1)

        def attend_act(act, units):
            for s in range(len(units) + 1):
                if s < len(units):
                    act.wait_ge(mx_done, s + 1)
                    for j in range(len(units[s]["scores"])):
                        n = units[s]["keys"]
                        src = MS[:, s % 2, 0:n] if units[s]["kind"] == "dilated" else ps[:, 2 * (s % 2) + j, 0:n]
                        dst = G[:, s % 2, :] if units[s]["kind"] == "dilated" else E[:, s % 2, j, 0:n]
                        last = nc.scalar.activation(dst, src, ACT.Exp,
                                                    bias=negmax[:, s % 2, j:j + 1],
                                                    accum_out=esum[:, s % 2, j:j + 1])
                    last.then_inc(ex_done, 1)
                if s >= 1:
                    u = s - 1
                    n = units[u]["keys"]
                    act.wait_ge(t_done, u + 1)
                    nc.scalar.copy(PT[:, u % 2, 0:n // P, :].rearrange("p b n -> p (b n)"),
                                   ps[:, 4 + u % 2, 0:n]).then_inc(pt_done, 1)

        def attend_dve(dve, chain, units, bias_of=None):
            for s in range(len(units) + 2):
                if s < len(units):
                    un, n = units[s], units[s]["keys"]
                    dve.wait_ge(s_done, s + 1)
                    if un["kind"] == "dilated":
                        chain(nc.vector.tensor_tensor_reduce(
                            out=MS[:, s % 2, :], in0=ps[:, 2 * (s % 2), :], in1=un["bias"], scale=1.0,
                            scalar=-3.0e38, op0=ALU.add, op1=ALU.max, accum_out=rowmax[:, s % 2, :]))
                        nc.vector.tensor_scalar(negmax[:, s % 2, 0:1], rowmax[:, s % 2, :], -1.0, None,
                                                ALU.mult).then_inc(mx_done, 1)
                    else:
                        js = len(un["scores"])
                        nc.vector.tensor_reduce(negmax[:, s % 2, 0:js], ps[:, 2 * (s % 2):2 * (s % 2) + js, 0:n],
                                                AX.X, ALU.max, negate=True).then_inc(mx_done, 1)
                if 1 <= s <= len(units):
                    u = s - 1
                    dve.wait_ge(ex_done, u + 1)
                    if units[u]["kind"] == "diff":
                        r = erec[:, u % 4, :]
                        chain(nc.vector.reciprocal(r, esum[:, u % 2, :]))
                        chain(nc.vector.tensor_scalar(r[:, 1:2], r[:, 1:2], lam[:, 5:6], None, ALU.mult))
                        chain(nc.vector.tensor_scalar(G[:, u % 2, :], E[:, u % 2, 1, :], r[:, 1:2], None, ALU.mult))
                        nc.vector.scalar_tensor_tensor(G[:, u % 2, :], E[:, u % 2, 0, :], r[:, 0:1], G[:, u % 2, :],
                                                       ALU.mult, ALU.add).then_inc(nm_done, 1)
                    else:
                        nc.vector.reciprocal(erec[:, u % 4, 0:1], esum[:, u % 2, 0:1]).then_inc(nm_done, 1)
                if s >= 2:
                    u = s - 2
                    dve.wait_ge(pv_done, u + 1)
                    if units[u]["kind"] == "diff":
                        nc.vector.tensor_copy(units[u]["out"], ps[:, 6 + u % 2, 0:HD]).then_inc(o_done, 1)
                    else:
                        dve.wait_ge(nm_done, u + 1)
                        nc.vector.tensor_scalar(units[u]["out"], ps[:, 6 + u % 2, 0:HD], erec[:, u % 4, 0:1], None,
                                                ALU.mult).then_inc(o_done, 1)

        with nc.Block() as block:
            @block.sync
            def _(sp):
                sp.dma_start(X[:], a["x"].rearrange("b (t p) d -> p (b t) d", p=P)).then_inc(io, 16)
                sp.dma_start(ident[:], a["identity"]).then_inc(io, 16)
                sp.wait_ge(io, 32)

            @block.gpsimd
            def _(pool):
                nc.gpsimd.memset(halfneg[:], -0.5)

        def next_round():
            nc.sync.sem_clear(range(nums[0], nums[-1] + 1))
            nc.all_engine_barrier()

        @contextmanager
        def layers():
            with nc.Fori(0, DEPTH) as layer:
                with nc.Block() as block:
                    yield layer, block
                next_round()

        next_round()

        P1 = at("P1", [P, NT, 3072], AT_R)
        QT = at("QT", [P, 12, S], AT_R + 49152)
        memX = at("memX", [P, 2, D], AT_R + 49152)
        memTh = at("memTh", [P, NC, N_MEM], AT_R + 49152 + 8192, F32R)
        memTl = at("memTl", [P, NC, N_MEM], AT_R + 49152 + 16384, F32R)
        mkT = at("mkT", [P, 2, N_MEM], AT_R + 73728)
        mv = at("mv", [P, 2, N_MEM], AT_R + 75776)
        lin_cos = at("lin_cos", [P, NT, 16], AT_R + 98304)
        lin_sin = at("lin_sin", [P, NT, 16], AT_R + 98560)
        ax_cos = at("ax_cos", [P, NT, 2, 16], AT_R + 98816)
        ax_sin = at("ax_sin", [P, NT, 2, 16], AT_R + 99328)
        qk_gain = at("qk_gain", [P, 2, HD], AT_R + 99840)
        subln = at("subln", [P, HD], AT_R + 100352)
        lamin = at("lamin", [P, 4, 32], AT_R + 100608)
        lamt = at("lamt", [P, 2, 32], AT_R + 101120)
        rA = at("rA", [P, 768], AT_R + 77824)
        rB = at("rB", [P, 768], AT_R + 77824 + 3072)
        par_all = 16 * 12

        def scores1():
            units = []
            for t in range(NT):
                tk = slice(t * P, (t + 1) * P)
                for h in range(N_DIFF):
                    sc = []
                    for j in range(2):
                        c, r = divmod(2 * h + j, 4)
                        rows = slice(32 * r, 32 * r + 32)
                        sc.append((QT[rows, c, tk], QT[rows, 3 + c, :]))
                    units.append(dict(kind="diff", t=t, keys=S, scores=sc, out=P1[:, t, HD * h:HD * (h + 1)],
                                      v=[P1[:, b, 1536 + HD * h:1536 + HD * (h + 1)] for b in range(NT)]))
                for h in range(N_GQA):
                    kv, c = divmod(h, 3)
                    rows = slice(HD * kv, HD * kv + HD)
                    o = 384 + HD * h
                    units.append(dict(kind="gqa", t=t, keys=S, scores=[(QT[rows, 6 + c, tk], QT[rows, 9, :])],
                                      out=P1[:, t, o:o + HD],
                                      v=[P1[:, b, 1920 + HD * kv:1920 + HD * (kv + 1)] for b in range(NT)]))
                for h in range(N_MEMH):
                    c, r = divmod(h, 2)
                    rows = slice(HD * r, HD * r + HD)
                    o = 768 + HD * h
                    units.append(dict(kind="mem", t=t, keys=N_MEM, scores=[(QT[rows, 10 + c, tk], mkT[rows, c, :])],
                                      out=P1[:, t, o:o + HD],
                                      v=[mv[:, b, HD * h:HD * (h + 1)] for b in range(2)]))
            return units

        units1 = scores1()
        scale1 = [32 ** -0.5] * 3 + [None] * 3 + [0.125] * 3 + [None] + [0.125] * 2

        with layers() as (layer, block):
            one = lambda name: a[name][bass.ds(layer, 1)]

            @block.sync
            def _(sp):
                sp.dma_start(memX[:], a["mem"].rearrange("b (t p) d -> p (b t) d", p=P)).then_inc(par, 16)
                for i, name in enumerate(("pre_norm", "mem_norm")):
                    sp.dma_start(gcol[:, i, :], one(name).rearrange("a p c -> (a p) c")).then_inc(par, 16)
                for dst, name in ((lin_cos, "lin_cos"), (lin_sin, "lin_sin")):
                    sp.dma_start(dst[:], a[name]).then_inc(par, 16)
                for dst, name in ((ax_cos, "ax_cos"), (ax_sin, "ax_sin")):
                    sp.dma_start(dst[:], a[name]).then_inc(par, 16)
                for dst, name in ((qk_gain[:, 0, :], "gqa_q_norm"), (qk_gain[:, 1, :], "gqa_k_norm"),
                                  (subln[:], "diff_subln")):
                    sp.dma_start(dst, one(name).to_broadcast([P, HD])).then_inc(par, 16)
                sp.dma_start(lamin[:].rearrange("p a b -> p (a b)"),
                             one("diff_lambda").to_broadcast([P, 128])).then_inc(par, 16)
                sp.dma_start(lamc[:], one("lambda_init").to_broadcast([P, 2])).then_inc(par, 16)
                sp.dma_start(gbc[:], one("post_norm").to_broadcast([P, D])).then_inc(gain_in, 16)
                stream(sp, a["w1"], layer, B1_TILES)

            @block.tensor
            def _(pe):
                pe.wait_ge(g_v, 2)
                for c in range(NC):
                    for t in range(2):
                        last = nc.tensor.transpose(ps[:, c, t * P:(t + 1) * P], memX[:, t, c * P:(c + 1) * P],
                                                   ident[:])
                    last.then_inc(sm_t, 1)
                w_hi, w_lo = stationary(0)
                pe.wait_ge(mw_done, NC)
                pe.wait_ge(lo_ready, 1)
                for c in range(2):
                    for k in range(NC):
                        last = three(ps[:, c, 0:N_MEM], w_hi[:, c, k, :], w_lo[:, c, k, :],
                                     memTh[:, k, :], memTl[:, k, :], k == 0, k == NC - 1)
                    last.then_inc(sm_t if c == 0 else w_used, 1)
                v_hi = whi[:, 1, :].rearrange("p (k n) -> p k n", k=NC)
                v_lo = wlo[:, 1, :].rearrange("p (k n) -> p k n", k=NC)
                pe.wait_ge(lo_ready, 2)
                for t in range(2):
                    for k in range(NC):
                        last = three(ps[:, 2 + t, 0:N_MEM], memTh[:, k, t * P:(t + 1) * P],
                                     memTl[:, k, t * P:(t + 1) * P], v_hi[:, k, :], v_lo[:, k, :],
                                     k == 0, k == NC - 1)
                    last.then_inc(sm_t if t == 0 else w_used, 1)
                pe.wait_ge(sm_e, NC + 4)
                turn_pe(pe, 0, XN, lambda t: (xn_done, t + 1))
                pe.wait_ge(tl_done, NC)
                for b in range(6):
                    if b >= 2:
                        pe.wait_ge(ev_a, 2 * (b - 1))
                        pe.wait_ge(ev_v, 2 * (b - 1))
                    project_pe(pe, B1_PROJ + 2 * b, b, 4 * (b % 2))
                pe.wait_ge(ev_a, 8 + 8)
                pe.wait_ge(q_ready, NT)
                for c in range(12):
                    if c >= 8:
                        pe.wait_ge(qte_v if c % 2 else qte_a, (c - 8) // 2 + 1)
                    for t in range(NT):
                        last = nc.tensor.transpose(ps[:, c % 8, t * P:(t + 1) * P], P1[:, t, c * P:(c + 1) * P],
                                                   ident[:])
                    last.then_inc(qt_done, 1)
                pe.wait_ge(qte_a, 6)
                pe.wait_ge(qte_v, 6)
                attend_pe(pe, units1)
                turn_pe(pe, 1, P1, lambda t: (o_ready, t + 1))
                pe.wait_ge(tl_done, 2 * NC)
                out_pe(pe, B1_OUT, NC, hTh, hTl)

            @block.scalar
            def _(act):
                act.wait_ge(par, par_all)
                for t in range(2):
                    nc.scalar.activation(junk_mem[:, t, :], memX[:, t, :], ACT.Square,
                                         accum_out=osum[:, t, 0:1]).then_inc(g_a, 1)
                prenorm_act(act, 0)
                act.wait_ge(g_v, 3)
                nc.scalar.activation(lam[:, 2:4], lam[:, 0:2], ACT.Exp).then_inc(g_a, 1)
                hi_part(act, 0)
                hi_part(act, 1)
                for c in range(NC):
                    act.wait_ge(sm_t, c + 1)
                    nc.scalar.activation(memTh[:, c, :], ps[:, c, 0:N_MEM], ACT.Copy,
                                         scale=gcol[:, 1, c:c + 1]).then_inc(sm_e, 1)
                for c in range(2):
                    act.wait_ge(*((sm_t, NC + 1), (w_used, 1))[c])
                    nc.scalar.copy(mkT[:, c, :], ps[:, c, 0:N_MEM]).then_inc(sm_e, 1)
                hi_part(act, 2)
                for t in range(2):
                    act.wait_ge(*((sm_t, NC + 2), (w_used, 2))[t])
                    nc.scalar.copy(mv[:, t, :], ps[:, 2 + t, 0:N_MEM]).then_inc(sm_e, 1)
                hi_part(act, 3)
                turn_act(act, 0, 0)
                for b in range(6):
                    hi_part(act, B1_PROJ + 2 * b + 2)
                    for t in range(NT):
                        if b >= 4:
                            projected(act, B1_PROJ + 2 * b, b, t)
                            nc.scalar.activation(P1[:, t, 512 * b:512 * (b + 1)], ps[:, 4 * (b % 2) + t, :],
                                                 ACT.Silu).then_inc(ev_a, 1)
                        elif t % 2 == 0:
                            projected(act, B1_PROJ + 2 * b, b, t)
                            nc.scalar.copy(P1[:, t, 512 * b:512 * (b + 1)], ps[:, 4 * (b % 2) + t, :]
                                           ).then_inc(ev_a, 1)
                    hi_part(act, B1_PROJ + 2 * b + 3)
                for c in range(0, 12, 2):
                    act.wait_ge(qt_done, c + 1)
                    nc.scalar.activation(QT[:, c, :], ps[:, c % 8, :], ACT.Copy, scale=scale1[c] or 1.0
                                         ).then_inc(qte_a, 1)
                attend_act(act, units1)
                turn_act(act, 1, None)
                for T in range(B1_OUT + 2, B1_TILES):
                    hi_part(act, T)
                postnorm_act(act, 0, B1_TILES - 1, junk_mix)

            @block.vector
            def _(dve):
                chain = Chain(dve, dchain)
                for t in range(2):
                    dve.wait_ge(g_p, t + 1)
                    nc.vector.tensor_scalar(memX[:, t, :], memX[:, t, :], oinv[:, t, 0:1], None, ALU.mult
                                            ).then_inc(g_v, 1)
                dve.wait_ge(par, par_all)
                for j in range(2):
                    chain(nc.vector.tensor_tensor_reduce(
                        out=lamt[:, j, :], in0=lamin[:, 2 * j, :], in1=lamin[:, 2 * j + 1, :], scale=1.0, scalar=0.0,
                        op0=ALU.mult, op1=ALU.add, accum_out=lam[:, j:j + 1]))
                nc.vector.tensor_scalar(subln[:], subln[:], lamc[:, 1:2], None, ALU.mult).then_inc(g_v, 1)
                dve.wait_ge(g_a, 3)
                chain(nc.vector.tensor_tensor(lam[:, 4:5], lam[:, 3:4], lam[:, 2:3], ALU.subtract))
                chain(nc.vector.tensor_tensor(lam[:, 5:6], lam[:, 4:5], lamc[:, 0:1], ALU.subtract))
                prenorm_dve(dve, 0)
                lo_part(dve, 0)
                lo_part(dve, 1)
                for c in range(NC):
                    dve.wait_ge(sm_e, c + 1)
                    nc.vector.scalar_tensor_tensor(memTl[:, c, :], ps[:, c, 0:N_MEM], gcol[:, 1, c:c + 1],
                                                   memTh[:, c, :].bitcast(F32), ALU.mult, ALU.subtract
                                                   ).then_inc(mw_done, 1)
                lo_part(dve, 2)
                lo_part(dve, 3)
                turn_dve(dve, 0, 0)

                def rotate(x, n, cos, sin, out_inc=None):
                    A = rA[:, 0:32 * n].rearrange("p (n r d) -> p n r d", r=2, d=16)
                    B = rB[:, 0:32 * n].rearrange("p (n r d) -> p n r d", r=2, d=16)
                    xs = x.rearrange("p n (r d) -> p n r d", r=2)
                    c4 = cos.unsqueeze(1).unsqueeze(1).to_broadcast([P, n, 2, 16])
                    s3 = sin.unsqueeze(1).to_broadcast([P, n, 16])
                    nc.vector.tensor_tensor(A, xs, c4, ALU.mult)
                    nc.vector.scalar_tensor_tensor(B[:, :, 0, :], xs[:, :, 1, :], -1.0, s3, ALU.mult, ALU.mult)
                    chain(nc.vector.tensor_tensor(B[:, :, 1, :], xs[:, :, 0, :], s3, ALU.mult))
                    return nc.vector.tensor_tensor(x, A.rearrange("p n r d -> p n (r d)"),
                                                   B.rearrange("p n r d -> p n (r d)"), ALU.add)

                def rope(t):
                    gq = P1[:, t, 768:1280].rearrange("p (h d) -> p h d", d=HD)
                    sq = rA[:, 0:512].rearrange("p (h d) -> p h d", d=HD)
                    chain(nc.vector.tensor_tensor(sq, gq, gq, ALU.mult))
                    nc.vector.tensor_reduce(hsum[:, t, :], sq, AX.X, ALU.add).then_inc(g_v, 1)
                    dve.wait_ge(g_v, 3 + t + 1)
                    chain(rotate(P1[:, t, 0:768].rearrange("p (n d) -> p n d", d=32), 24, lin_cos[:, t, :],
                                 lin_sin[:, t, :]))
                    dve.wait_ge(g_p, 2 + t + 1)
                    chain(nc.vector.tensor_tensor(gq, gq, hinv[:, t, :].unsqueeze(2).to_broadcast([P, 8, HD]),
                                                  ALU.mult))
                    nc.vector.tensor_tensor(gq[:, 0:6, :], gq[:, 0:6, :],
                                            qk_gain[:, 0:1, :].to_broadcast([P, 6, HD]), ALU.mult)
                    chain(nc.vector.tensor_tensor(gq[:, 6:8, :], gq[:, 6:8, :],
                                                  qk_gain[:, 1:2, :].to_broadcast([P, 2, HD]), ALU.mult))
                    for axis in range(2):
                        last = rotate(gq[:, :, 32 * axis:32 * axis + 32], 8, ax_cos[:, t, axis, :],
                                      ax_sin[:, t, axis, :])
                        if axis == 0:
                            chain(last)
                    last.then_inc(q_ready, 1)
                    dve.wait_ge(q_ready, t + 1)

                for b in range(6):
                    lo_part(dve, B1_PROJ + 2 * b + 2)
                    if b < 4:
                        for t in (1, 3):
                            projected(dve, B1_PROJ + 2 * b, b, t)
                            nc.vector.tensor_copy(P1[:, t, 512 * b:512 * (b + 1)], ps[:, 4 * (b % 2) + t, :]
                                                  ).then_inc(ev_v, 1)
                    lo_part(dve, B1_PROJ + 2 * b + 3)
                    if b == 3:
                        dve.wait_ge(ev_a, 6)
                        dve.wait_ge(ev_v, 6)
                    if b in (3, 4):
                        rope(2 * (b - 3))
                        rope(2 * (b - 3) + 1)
                for c in range(1, 12, 2):
                    dve.wait_ge(qt_done, c + 1)
                    nc.vector.tensor_scalar(QT[:, c, :], ps[:, c % 8, :], scale1[c] or 1.0, None, ALU.mult
                                            ).then_inc(qte_v, 1)
                attend_dve(dve, chain, units1)
                dve.wait_ge(o_done, len(units1))
                for t in range(NT):
                    oa = P1[:, t, 0:384].rearrange("p (h d) -> p h d", d=HD)
                    sq = rA[:, 0:384].rearrange("p (h d) -> p h d", d=HD)
                    chain(nc.vector.tensor_tensor(sq, oa, oa, ALU.mult))
                    nc.vector.tensor_reduce(osum[:, t, 0:6], sq, AX.X, ALU.add).then_inc(g_v, 1)
                    dve.wait_ge(g_v, 3 + NT + t + 1)
                for t in range(NT):
                    oa = P1[:, t, 0:384].rearrange("p (h d) -> p h d", d=HD)
                    dve.wait_ge(g_p, 2 + NT + t + 1)
                    chain(nc.vector.tensor_tensor(oa, oa, oinv[:, t, 0:6].unsqueeze(2).to_broadcast([P, 6, HD]),
                                                  ALU.mult))
                    chain(nc.vector.tensor_tensor(oa, oa, subln[:].unsqueeze(1).to_broadcast([P, 6, HD]), ALU.mult))
                    nc.vector.tensor_tensor(P1[:, t, 0:D], P1[:, t, 0:D], P1[:, t, 2048:3072], ALU.mult
                                            ).then_inc(o_ready, 1)
                turn_dve(dve, 1, None)
                for T in range(B1_OUT + 2, B1_TILES):
                    lo_part(dve, T)
                postnorm_dve(dve, 0)

            @block.gpsimd
            def _(pool):
                chain = Chain(pool, pchain)

                def inverse_root(src, dst, width, n, done):
                    chain(nc.gpsimd.tensor_scalar(src, src, 1.0 / width, EPS, ALU.mult, ALU.add))
                    nc.gpsimd.tensor_tensor(dst, src, halfneg[:].to_broadcast([P, n]), ALU.pow).then_inc(done, 1)

                for t in range(2):
                    pool.wait_ge(g_a, t + 1)
                    inverse_root(osum[:, t, 0:1], oinv[:, t, 0:1], D, 1, g_p)
                prenorm_pool(pool, chain, 0)
                for t in range(NT):
                    pool.wait_ge(g_v, 3 + t + 1)
                    inverse_root(hsum[:, t, :], hinv[:, t, :], HD, 8, g_p)
                for t in range(NT):
                    pool.wait_ge(g_v, 3 + NT + t + 1)
                    inverse_root(osum[:, t, 0:6], oinv[:, t, 0:6], HD, 6, g_p)
                postnorm_pool(pool, chain, 0, 1.0)

        P2 = at("P2", [P, NT, 2560], AT_R)
        MQK = at("MQK", [P, 8, S], AT_R + 40960)
        QT2 = at("QT2", [P, 8, S], AT_R + 57344)
        AB = at("AB", [P, 8, S], AT_R + 57344)
        masks = at("masks", [P, 2, S], AT_R + 73728)
        BM = at("BM", [P, NT, S], AT_R + 77824)
        acc = at("acc", [P, 2, S], AT_R + 86016)
        mgain = at("mgain", [P, S], AT_R + 94208)
        pad = at("pad", [P, 2, S + 4], AT_R + 98304)
        rt = at("rt", [P, 2, 3, 128], AT_R + 90112)
        SW = at("SW", [P, 2, MH, 640], AT_R + 77824)
        PT2 = at("PT2", [P, 2, NT, P], AT_R + 98304)
        aT = at("aT", [P, S], AT_R + 98304)
        acth = at("acth", [P, FC, S], AT_R, F32R)
        actl = at("actl", [P, FC, S], AT_R + 45056, F32R)
        sil = at("sil", [P, 2, S], AT_R + 90112)
        afull = at("afull", [P, 2, S], AT_R + 94208)
        par2_all = 16 * 8

        units2 = []
        for t in range(NT):
            for h in range(8):
                c, r = divmod(h, 2)
                rows = slice(HD * r, HD * r + HD)
                units2.append(dict(kind="dilated", t=t, keys=S, bias=BM[:, t, :],
                                   scores=[(QT2[rows, c, t * P:(t + 1) * P], QT2[rows, 4 + c, :])],
                                   out=P2[:, t, HD * h:HD * (h + 1)],
                                   v=[P2[:, b, 1024 + HD * h:1024 + HD * (h + 1)] for b in range(NT)]))

        def ffn_pe(pe, f, m, T_in, T_out):
            pe.wait_ge(tl_done, NC * (m + 1))
            with pe.Fori(0, FC // 2) as i:
                for p in range(2):
                    w_hi, w_lo = stationary(T_in + p)
                    pe.wait_ge(lo_ready, T_in + p + 1 + i * 2)
                    pe.wait_ge(gated, FC * f + p + 1 + i * 2)
                    for c in range(2):
                        for k in range(NC):
                            last = three(ps[:, 4 + 2 * p + c, :], w_hi[:, c, k, :], w_lo[:, c, k, :],
                                         hTh[:, k, :], hTl[:, k, :], k == 0, k == NC - 1)
                    last.then_inc(w_used, 1)
            pe.wait_ge(actl_done, FC * (f + 1))
            out_pe(pe, T_out, FC, acth, actl)

        def ffn_act(act, f, T_in, T_out):
            with act.Fori(0, FC // 2) as i:
                for p in range(2):
                    act.wait_ge(w_used, T_in + p + 1 + i * 2)
                    nc.scalar.activation(sil[:, p, :], ps[:, 4 + 2 * p, :], ACT.Silu).then_inc(silu_done, 1)
                    hi_part(act, T_in + p + 2, i)
                    act.wait_ge(gated, FC * f + p + 3 + i * 2)
                    nc.scalar.copy(acth[:, bass.ds(i * 2 + p, 1), :].rearrange("p a n -> p (a n)"), afull[:, p, :]
                                   ).then_inc(acth_done, 1)
            for T in range(T_out + 2, min(T_out + 13, B2_TILES)):
                hi_part(act, T)

        def ffn_dve(dve, f, T_in, T_out):
            with dve.Fori(0, FC // 2) as i:
                for p in range(2):
                    dve.wait_ge(silu_done, FC * f + p + 1 + i * 2)
                    nc.vector.tensor_tensor(afull[:, p, :], sil[:, p, :], ps[:, 5 + 2 * p, :], ALU.mult
                                            ).then_inc(gated, 1)
                    lo_part(dve, T_in + p + 2, i)
                    dve.wait_ge(acth_done, FC * f + p + 1 + i * 2)
                    j = bass.ds(i * 2 + p, 1)
                    nc.vector.tensor_tensor(actl[:, j, :].rearrange("p a n -> p (a n)"), afull[:, p, :],
                                            acth[:, j, :].rearrange("p a n -> p (a n)").bitcast(F32),
                                            ALU.subtract).then_inc(actl_done, 1)
            for T in range(T_out + 2, min(T_out + 13, B2_TILES)):
                lo_part(dve, T)

        def seg(t, d):
            wf = (t + 1) * P
            return (slice(0, wf), slice(0, wf)) if d == 0 else (slice(wf, 640), slice(t * P, S))

        ROW = [(B2_QK, 0), (B2_QK + 2, 4), (B2_ROW, 0), (B2_ROW + 2, 4), (B2_ROW + 4, 0)]

        with layers() as (layer, block):
            one = lambda name: a[name][bass.ds(layer, 1)]

            def gain_row(j):
                return a["norm_gain_rows"][bass.ds(layer * 6 + j, 1)].to_broadcast([P, D])

            @block.sync
            def _(sp):
                sp.dma_start(gcol[:].rearrange("p a c -> p (a c)"), one("norm_gain").rearrange("a p c -> (a p) c")
                             ).then_inc(par2, 16)
                sp.dma_start(gate_raw[:].rearrange("p a c -> p (a c)"), one("w_gate").rearrange("a p c -> (a p) c")
                             ).then_inc(par2, 16)
                sp.dma_start(gate_bias[:], one("gate_bias").to_broadcast([P, 16])).then_inc(par2, 16)
                sp.dma_start(conv_w[:].rearrange("p a c -> p (a c)"), one("conv_w").rearrange("a p c -> (a p) c")
                             ).then_inc(par2, 16)
                sp.dma_start(conv_b[:], one("conv_b").rearrange("a p c -> (a p) c")).then_inc(par2, 16)
                sp.dma_start(rot_cos[:], a["rot_cos"]).then_inc(par2, 16)
                sp.dma_start(rot_sin[:], a["rot_sin"]).then_inc(par2, 16)
                sp.dma_start(upto[:], a["upto"]).then_inc(par2, 16)
                sp.dma_start(gbc[:], gain_row(1)).then_inc(gain_in, 16)
                stream(sp, a["w2"], layer, B2_TILES)

            @block.tensor
            def _(pe):
                turn_pe(pe, 0, XN, lambda t: (xn_done, t + 1))
                ffn_pe(pe, 0, 0, B2_IN1, B2_OUT1)
                turn_pe(pe, 1, XN, lambda t: (xn_done, NT + t + 1))
                pe.wait_ge(tl_done, 2 * NC)
                pe.wait_ge(mw_done, 1)
                for t in range(NT):
                    for k in range(NC):
                        last = three(ps[:, 7, 16 * t:16 * (t + 1)], hTh[:, k, t * P:(t + 1) * P],
                                     hTl[:, k, t * P:(t + 1) * P], gate_hi[:, k, :], gate_lo[:, k, :],
                                     k == 0, k == NC - 1)
                last.then_inc(sm_t, 1)
                project_pe(pe, *ROW[0][:1], 0, ROW[0][1])
                pe.wait_ge(g_v, 1)
                project_pe(pe, ROW[1][0], 1, ROW[1][1])
                for c in range(8):
                    T = B2_CONV + c // 2
                    if c % 4 == 0:
                        pe.wait_ge(ev_a, 2 * (c // 4 + 1))
                        pe.wait_ge(ev_v, 2 * (c // 4 + 1))
                    w_hi, w_lo = stationary(T)
                    pe.wait_ge(lo_ready, T + 1)
                    for k in range(NC):
                        last = three(ps[:, c, :], w_hi[:, c % 2, k, :], w_lo[:, c % 2, k, :], hTh[:, k, :],
                                     hTl[:, k, :], k == 0, k == NC - 1)
                    last.then_inc(w_used if c % 2 else cs_mm, 1)
                for b in (2, 3, 4):
                    if b == 4:
                        pe.wait_ge(ev_a, 6)
                        pe.wait_ge(ev_v, 6)
                    else:
                        pe.wait_ge(pad_done, 4 * (b - 1))
                    project_pe(pe, ROW[b][0], b, ROW[b][1])
                pe.wait_ge(ev_a, 8)
                pe.wait_ge(ev_v, 8)
                pe.wait_ge(g_v, 3)
                for t in range(NT):
                    for d in range(2):
                        others = range(t) if d == 0 else range(t + 1, NT)
                        out = ps[:, 4, 8 * t + 4 * d:8 * t + 4 * d + 4]
                        last = nc.tensor.matmul(out, upto[:, d, :], logf[:, t, d, :], start=True, stop=not len(others))
                        for o in others:
                            last = nc.tensor.matmul(out, ones[:].to_broadcast([P, P]), logf[:, o, d, :],
                                                    start=False, stop=o == others[-1])
                last.then_inc(sm_t, 1)
                pe.wait_ge(g_v, 4)
                pe.wait_ge(q_ready, NT)
                pe.wait_ge(ev_a, 12)
                for c in range(8):
                    for t in range(NT):
                        last = nc.tensor.transpose(ps[:, c, t * P:(t + 1) * P], P2[:, t, c * P:(c + 1) * P], ident[:])
                    last.then_inc(qt_done, 1)
                pe.wait_ge(qte_a, 4)
                pe.wait_ge(qte_v, 4)
                attend_pe(pe, units2)
                pe.wait_ge(o_done, len(units2))
                for t in range(NT):
                    last = nc.tensor.transpose(ps[0:8, 0, t * P:(t + 1) * P],
                                               acol[:, t, :, :].rearrange("p d h -> p (d h)"), ident[:])
                last.then_inc(sm_t, 1)
                pe.wait_ge(sm_e, 1)
                for r in range(8):
                    nc.tensor.matmul(ps[:, r, :], ident[0:8, r:r + 1].to_broadcast([8, P]), aT[0:8, :],
                                     start=True, stop=True).then_inc(sm_t, 1)
                pe.wait_ge(ab_a, 4)
                pe.wait_ge(ab_v, 4)

                def similar(t):
                    for h in range(MH):
                        if t:
                            pe.wait_ge(m2_done, MH * (t - 1) + h + 1)
                        nc.tensor.matmul(ps[:, h, :], MQK[:, h, t * P:(t + 1) * P], MQK[:, MH + h, :],
                                         start=True, stop=True).then_inc(ms_done, 1)

                def values(t, h):
                    pe.wait_ge(mpt_done, MH * t + h + 1)
                    for b in range(NT):
                        last = nc.tensor.matmul(ps[:, 6 + t % 2, h * P:(h + 1) * P], PT2[:, h % 2, b, :],
                                                P2[:, b, 1536 + h * P:1536 + (h + 1) * P],
                                                start=b == 0, stop=b == NT - 1)
                    if h == MH - 1:
                        last.then_inc(mpv_done, 1)

                pe.wait_ge(cs_done, 8)
                similar(0)
                for t in range(NT):
                    if t + 1 < NT:
                        similar(t + 1)
                    if t >= 2:
                        pe.wait_ge(o_ready, t - 1)
                    for h in range(MH):
                        pe.wait_ge(mg_done, MH * t + h + 1)
                        for b in range(NT):
                            col = b * P if b <= t else (b + 1) * P
                            last = nc.tensor.transpose(ps[:, 4 + h % 2, b * P:(b + 1) * P],
                                                       SW[:, t % 2, h, col:col + P], ident[:])
                        last.then_inc(mt_done, 1)
                        if h:
                            values(t, h - 1)
                    values(t, MH - 1)
                turn_pe(pe, 2, P2, lambda t: (o_ready, t + 1))
                pe.wait_ge(tl_done, 3 * NC)
                out_pe(pe, B2_MIXOUT, NC, hTh, hTl)
                turn_pe(pe, 3, XN, lambda t: (xn_done, 2 * NT + t + 1))
                ffn_pe(pe, 1, 3, B2_IN2, B2_OUT2)

            @block.scalar
            def _(act):
                prenorm_act(act, 0)
                act.wait_ge(par2, par2_all)
                hi_part(act, 0)
                hi_part(act, 1)
                turn_act(act, 0, 0)
                ffn_act(act, 0, B2_IN1, B2_OUT1)
                postnorm_act(act, 0, B2_OUT1 + 10, junk_ffn)
                nc.scalar.copy(gate_hi[:], gate_raw[:]).then_inc(mr_done, 1)
                prenorm_act(act, 1)
                act.dma_start(gbc[:], gain_row(3)).then_inc(gain_in, 16)
                act.dma_start(BM[:], a["group_bias"]).then_inc(mixpar, 16)
                act.dma_start(masks[:], a["causal"]).then_inc(mixpar, 16)
                act.dma_start(mgain[:], one("mlstm_gain").to_broadcast([P, S])).then_inc(mixpar, 16)
                turn_act(act, 1, 2)

                def evacuate(b):
                    T0, bank = ROW[b]
                    for t in (0, 2):
                        projected(act, T0, b, t)
                        nc.scalar.copy(P2[:, t, 512 * b:512 * (b + 1)], ps[:, bank + t, :]).then_inc(ev_a, 1)

                def conv_silu(c):
                    act.wait_ge(cv_done, c + 1)
                    nc.scalar.activation(MQK[:, c, :], acc[:, c % 2, :], ACT.Silu, bias=conv_b[:, c:c + 1]
                                         ).then_inc(cs_done, 1)

                for b in (0, 1):
                    hi_part(act, ROW[b][0] + 2)
                    if b == 0:
                        act.wait_ge(g_v, 2)
                        nc.scalar.activation(gexp[:], gtmp[:], ACT.Exp).then_inc(g_a, 1)
                        act.wait_ge(g_a, 1)
                        nc.scalar.activation(gexp[:], gexp[:], ACT.Ln, bias=1.0).then_inc(g_a, 1)
                    evacuate(b)
                    hi_part(act, ROW[b][0] + 3)
                act.wait_ge(g_p, 1)
                for c in range(8):
                    T = B2_CONV + c // 2
                    if c % 2:
                        hi_part(act, T + 2)
                        act.wait_ge(w_used, T + 1)
                    else:
                        act.wait_ge(cs_mm, c // 2 + 1)
                    if c >= 2:
                        act.wait_ge(cv_done, c - 1)
                    nc.scalar.copy(pad[:, c % 2, 2:S + 2], ps[:, c, :]).then_inc(pad_done, 1)
                    if c:
                        conv_silu(c - 1)
                conv_silu(7)
                for b in (2, 3, 4):
                    hi_part(act, ROW[b][0] + 2)
                    if b < 4:
                        evacuate(b)
                    else:
                        for t in range(NT):
                            projected(act, ROW[b][0], b, t)
                            nc.scalar.activation(P2[:, t, 512 * b:512 * (b + 1)], ps[:, ROW[b][1] + t, :],
                                                 ACT.Sigmoid).then_inc(ev_a, 1)
                    hi_part(act, ROW[b][0] + 3)
                for c in range(0, 8, 2):
                    act.wait_ge(qt_done, c + 1)
                    nc.scalar.activation(QT2[:, c, :], ps[:, c, :], ACT.Copy, scale=0.125 if c < 4 else 1.0
                                         ).then_inc(qte_a, 1)
                attend_act(act, units2)
                act.wait_ge(sm_t, 3)
                nc.scalar.copy(aT[0:8, :], ps[0:8, 0, :]).then_inc(sm_e, 1)
                for r in range(0, 8, 2):
                    act.wait_ge(sm_t, 3 + r + 1)
                    nc.scalar.copy(AB[:, r, :], ps[:, r, :]).then_inc(ab_a, 1)

                def weights(t):
                    act.wait_ge(m1_done, t + 1)
                    for h in range(MH):
                        for d in range(2):
                            w = SW[:, t % 2, h, seg(t, d)[0]]
                            nc.scalar.activation(w, w, ACT.Exp, bias=nmmax[:, t, d, h:h + 1])
                    nc.scalar.activation(mexp[:, t, :, :], dtmp[:, t, :, :], ACT.Exp).then_inc(mw2_done, 1)

                def cell_squares(t):
                    act.wait_ge(mpv_done, t + 1)
                    for h in range(MH):
                        last = nc.scalar.activation(junk_head[:, h, :], ps[:, 6 + t % 2, h * P:(h + 1) * P], ACT.Square,
                                                    accum_out=osum[:, t, h:h + 1])
                    last.then_inc(g_a, 1)

                weights(0)
                for t in range(NT):
                    for h in range(MH):
                        act.wait_ge(mt_done, MH * t + h + 1)
                        nc.scalar.copy(PT2[:, h % 2, :, :].rearrange("p b n -> p (b n)"), ps[:, 4 + h % 2, :]
                                       ).then_inc(mpt_done, 1)
                        if h == 1 and t + 1 < NT:
                            weights(t + 1)
                    cell_squares(t)
                turn_act(act, 2, None)
                for T in range(B2_MIXOUT + 2, B2_MIXOUT + 6):
                    hi_part(act, T)
                postnorm_act(act, 1, B2_MIXOUT + 3, junk_mix)
                prenorm_act(act, 2)
                act.dma_start(gbc[:], gain_row(5)).then_inc(gain_in, 16)
                turn_act(act, 3, 4)
                ffn_act(act, 1, B2_IN2, B2_OUT2)
                postnorm_act(act, 2, B2_TILES - 1, junk_ffn)

            @block.vector
            def _(dve):
                chain = Chain(dve, dchain)
                nc.vector.memset(ones[:], 1.0).then_inc(one_done, 1)
                prenorm_dve(dve, 0)
                lo_part(dve, 0)
                lo_part(dve, 1)
                turn_dve(dve, 0, 0)
                dve.sem_inc(gated, 2)
                ffn_dve(dve, 0, B2_IN1, B2_OUT1)
                postnorm_dve(dve, 0)
                dve.wait_ge(mr_done, 1)
                nc.vector.tensor_tensor(gate_lo[:], gate_raw[:], gate_hi[:].bitcast(F32), ALU.subtract
                                        ).then_inc(mw_done, 1)
                prenorm_dve(dve, 1)
                turn_dve(dve, 1, 2)
                dve.wait_ge(sm_t, 1)
                nc.vector.tensor_tensor(gates[:].rearrange("p t d g h -> p t (d g h)"),
                                        ps[:, 7, 0:64].rearrange("p (t g) -> p t g", t=NT),
                                        gate_bias[:].unsqueeze(1).to_broadcast([P, NT, 16]), ALU.add).then_inc(g_v, 1)
                dve.wait_ge(g_v, 1)
                f = gates[:, :, :, 1, :]
                chain(nc.vector.tensor_scalar(gtmp[:], f, -1.0, None, ALU.mult))
                nc.vector.tensor_tensor(gtmp[:], gtmp[:], f, ALU.min).then_inc(g_v, 1)

                def evacuate(b):
                    T0, bank = ROW[b]
                    for t in (1, 3):
                        projected(dve, T0, b, t)
                        nc.vector.tensor_copy(P2[:, t, 512 * b:512 * (b + 1)], ps[:, bank + t, :]).then_inc(ev_v, 1)

                def rotary(t):
                    x = P2[:, t, 0:1024].rearrange("p (n d) -> p n d", d=HD)
                    x1, x2 = x[:, :, 0:8], x[:, :, 8:16]
                    c3 = rot_cos[:, t, :].unsqueeze(1).to_broadcast([P, 16, 8])
                    s3 = rot_sin[:, t, :].unsqueeze(1).to_broadcast([P, 16, 8])
                    A, B, C = (rt[:, t % 2, j, :].rearrange("p (n d) -> p n d", d=8) for j in range(3))
                    nc.vector.tensor_tensor(A, x1, s3, ALU.mult)
                    nc.vector.tensor_tensor(B, x2, s3, ALU.mult)
                    chain(nc.vector.tensor_tensor(C, x2, c3, ALU.mult))
                    chain(nc.vector.tensor_tensor(x1, x1, c3, ALU.mult))
                    nc.vector.tensor_tensor(x2, C, A, ALU.add)
                    nc.vector.tensor_tensor(x1, x1, B, ALU.subtract).then_inc(q_ready, 1)

                def convolve(c):
                    dve.wait_ge(pad_done, c + 1)
                    if c >= 2:
                        dve.wait_ge(cs_done, c - 1)
                    o, x = acc[:, c % 2, :], pad[:, c % 2, :]
                    chain(nc.vector.tensor_scalar(o, x[:, 0:S], conv_w[:, c, 0:1], None, ALU.mult))
                    for w in range(1, CONV):
                        ins = nc.vector.scalar_tensor_tensor(o, x[:, w:w + S], conv_w[:, c, w:w + 1], o,
                                                             ALU.mult, ALU.add)
                        if w < CONV - 1:
                            chain(ins)
                    ins.then_inc(cv_done, 1)

                dve.wait_ge(par2, par2_all)
                for b in (0, 1):
                    lo_part(dve, ROW[b][0] + 2)
                    if b == 0:
                        dve.wait_ge(g_a, 2)
                        nc.vector.scalar_tensor_tensor(logf[:], f, 0.0, gexp[:], ALU.min, ALU.subtract
                                                       ).then_inc(g_v, 1)
                    evacuate(b)
                    lo_part(dve, ROW[b][0] + 3)
                for c in range(8):
                    if c % 2:
                        lo_part(dve, B2_CONV + c // 2 + 2)
                    convolve(c)
                for b in (2, 3, 4):
                    lo_part(dve, ROW[b][0] + 2)
                    if b < 4:
                        evacuate(b)
                    if b == 2:
                        dve.wait_ge(ev_a, 4)
                        dve.wait_ge(ev_v, 4)
                        for t in range(NT):
                            rotary(t)
                    lo_part(dve, ROW[b][0] + 3)
                dve.wait_ge(sm_t, 2)
                nc.vector.tensor_copy(cum[:].rearrange("p t d h -> p (t d h)"), ps[:, 4, 0:32]).then_inc(g_v, 1)
                dve.wait_ge(g_v, 4)
                chain(nc.vector.tensor_tensor(acol[:], gates[:, :, :, 0, :], cum[:], ALU.subtract))
                for c in range(1, 8, 2):
                    dve.wait_ge(qt_done, c + 1)
                    nc.vector.tensor_scalar(QT2[:, c, :], ps[:, c, :], 0.125 if c < 4 else 1.0, None, ALU.mult
                                            ).then_inc(qte_v, 1)
                dve.wait_ge(mixpar, 48)
                dve.wait_ge(g_p, 2)
                attend_dve(dve, chain, units2)
                for r in range(1, 8, 2):
                    dve.wait_ge(sm_t, 3 + r + 1)
                    nc.vector.tensor_copy(AB[:, r, :], ps[:, r, :]).then_inc(ab_v, 1)
                dve.wait_ge(ab_a, 4)
                dve.wait_ge(ab_v, 4)

                def decay(t):
                    for h in range(MH):
                        for d in range(2):
                            dst, src = seg(t, d)
                            mask = masks[:, 0, 384 - P * t:S] if d == 0 else masks[:, 1, 0:S - P * t]
                            last = nc.vector.tensor_tensor_reduce(
                                out=SW[:, t % 2, h, dst], in0=AB[:, MH * d + h, src], in1=mask, scale=1.0,
                                scalar=-3.0e38, op0=ALU.add, op1=ALU.max, accum_out=mmax[:, t, d, h:h + 1])
                    chain(last)
                    chain(nc.vector.tensor_scalar(nmmax[:, t, :, :], mmax[:, t, :, :], -1.0, None, ALU.mult))
                    nc.vector.tensor_tensor(dtmp[:, t, :, :], nmmax[:, t, :, :], cum[:, t, :, :], ALU.subtract
                                            ).then_inc(m1_done, 1)

                def weigh(t):
                    dve.wait_ge(mw2_done, t + 1)
                    for h in range(MH):
                        dve.wait_ge(ms_done, MH * t + h + 1)
                        for d in range(2):
                            dst, src = seg(t, d)
                            w = SW[:, t % 2, h, dst]
                            last = nc.vector.tensor_tensor_reduce(
                                out=w, in0=ps[:, h, src], in1=w, scale=P ** -0.5, scalar=0.0,
                                op0=ALU.mult, op1=ALU.add, accum_out=den[:, t, d, h:h + 1])
                        last.then_inc(m2_done, 1)
                    dve.wait_ge(m2_done, MH * (t + 1))
                    chain(nc.vector.tensor_scalar(drec[:, t, :, :], den[:, t, :, :], -1.0, None, ALU.mult))
                    chain(nc.vector.tensor_tensor(drec[:, t, :, :], drec[:, t, :, :], den[:, t, :, :], ALU.max))
                    chain(nc.vector.tensor_tensor(drec[:, t, :, :], drec[:, t, :, :], mexp[:, t, :, :], ALU.max))
                    chain(nc.vector.reciprocal(drec[:, t, :, :], drec[:, t, :, :]))
                    for h in range(MH):
                        for d in range(2):
                            w = SW[:, t % 2, h, seg(t, d)[0]]
                            last = nc.vector.tensor_scalar(w, w, drec[:, t, d, h:h + 1], None, ALU.mult)
                        chain(last)
                        w = SW[:, t % 2, h, :]
                        nc.vector.tensor_tensor(w[:, t * P:(t + 1) * P], w[:, t * P:(t + 1) * P],
                                                w[:, (t + 1) * P:(t + 2) * P], ALU.add).then_inc(mg_done, 1)

                def cell(t):
                    dve.wait_ge(g_p, 2 + t + 1)
                    for h in range(MH):
                        o = 512 + h * P
                        last = nc.vector.scalar_tensor_tensor(
                            P2[:, t, o:o + P], ps[:, 6 + t % 2, h * P:(h + 1) * P], oinv[:, t, h:h + 1],
                            P2[:, t, 1536 + o:1536 + o + P], ALU.mult, ALU.mult)
                    last.then_inc(o_ready, 1)

                decay(0)
                for t in range(NT):
                    weigh(t)
                    if t:
                        cell(t - 1)
                    if t + 1 < NT:
                        decay(t + 1)
                cell(NT - 1)
                turn_dve(dve, 2, None)
                for T in range(B2_MIXOUT + 2, B2_MIXOUT + 6):
                    lo_part(dve, T)
                postnorm_dve(dve, 1)
                prenorm_dve(dve, 2)
                turn_dve(dve, 3, 4)
                ffn_dve(dve, 1, B2_IN2, B2_OUT2)
                postnorm_dve(dve, 2)

            @block.gpsimd
            def _(pool):
                chain = Chain(pool, pchain)
                prenorm_pool(pool, chain, 0)
                postnorm_pool(pool, chain, 0, 0.5)
                prenorm_pool(pool, chain, 1)
                pool.wait_ge(x_done, NT)
                nc.gpsimd.memset(pad[:, :, 0:2], 0.0)
                nc.gpsimd.memset(pad[:, :, S + 2:S + 4], 0.0).then_inc(g_p, 1)
                pool.wait_ge(mixpar, 48)
                pool.wait_ge(ev_a, 12)
                for t in range(NT):
                    last = nc.gpsimd.tensor_tensor(P2[:, t, 2048:2560], P2[:, t, 2048:2560], mgain[:], ALU.mult)
                last.then_inc(g_p, 1)
                for t in range(NT):
                    pool.wait_ge(g_a, 2 + t + 1)
                    chain(nc.gpsimd.tensor_scalar(osum[:, t, 0:MH], osum[:, t, 0:MH], 1.0 / P, EPS,
                                                  ALU.mult, ALU.add))
                    nc.gpsimd.tensor_tensor(oinv[:, t, 0:MH], osum[:, t, 0:MH], halfneg[:].to_broadcast([P, MH]),
                                            ALU.pow).then_inc(g_p, 1)
                postnorm_pool(pool, chain, 1, 1.0)
                prenorm_pool(pool, chain, 2)
                postnorm_pool(pool, chain, 2, 0.5)

        with nc.Block() as block:
            @block.sync
            def _(sp):
                sp.dma_start(a["out"].rearrange("b (t p) d -> p (b t) d", p=P), X[:]).then_inc(io, 16)
                sp.wait_ge(io, 16)
    return nc


def moving_tiles(w):
    L, K, N = w.shape
    b = w.reshape(L, K // P, P, N // 512, 512).transpose(0, 3, 1, 2, 4).reshape(L, -1, 4, P, 512)
    return b.transpose(0, 1, 3, 2, 4).reshape(L, -1, P, TILE)


def stationary_tiles(w):
    L, _, n, _ = w.shape
    return w.reshape(L, NC, P, n // 2, 2, P).transpose(0, 3, 2, 4, 1, 5).reshape(L, n // 2, P, TILE)


def rope_tables(pos, dim, theta):
    inv = (np.float32(theta) ** (-np.arange(0, dim, 2, dtype=np.float32) / np.float32(dim))).astype(np.float32)
    ang = pos.astype(np.float32)[:, None] * inv[None, :]
    return np.cos(ang).astype(np.float32), np.sin(ang).astype(np.float32)


def by_token(t):
    return np.ascontiguousarray(np.moveaxis(t.reshape(NT, P, *t.shape[1:]), 0, 1))


def constants():
    pos = np.arange(S)
    c = {"identity": np.eye(P, dtype=np.float32)}
    cos, sin = rope_tables(pos, 32, 10000.0)
    c["lin_cos"], c["lin_sin"] = by_token(cos), by_token(sin)
    rc, rs = rope_tables(pos // 64, 32, 10000.0)
    cc, cs = rope_tables(pos % 64, 32, 10000.0)
    c["ax_cos"], c["ax_sin"] = by_token(np.stack([rc, cc], 1)), by_token(np.stack([rs, cs], 1))
    cos, sin = rope_tables(pos, 16, 500000.0)
    c["rot_cos"], c["rot_sin"] = by_token(cos), by_token(sin)
    gap = np.abs(pos[:, None] - pos[None, :])
    count = sum(((gap % dil == 0) & (gap // dil <= 64)).astype(np.int64) for dil in (1, 4, 16))
    bias = np.where(count > 0, np.log(np.maximum(count, 1)), NEG).astype(np.float32)
    c["group_bias"] = by_token(bias)
    p, s = np.arange(P)[:, None], np.arange(P)[None, :]
    zero = np.zeros((P, 384), np.float32)
    c["causal"] = np.stack([np.concatenate([zero, np.where(s <= p, 0, NEG).astype(np.float32)], 1),
                            np.concatenate([np.where(s >= p, 0, NEG).astype(np.float32), zero], 1)], 1)
    c["upto"] = np.stack([(p <= s).astype(np.float32), (p >= s).astype(np.float32)], 1)
    li = [0.8 - 0.6 * math.exp(-0.3 * l) for l in range(DEPTH)]
    c["lambda_init"] = np.array([[v, 1.0 - v] for v in li], np.float32)
    return c


def lay_out(x, mem, pre_norm, w_in, diff_lambda, diff_subln, gqa_q_norm, gqa_k_norm, mem_norm, w_mem_kv,
            w_out, post_norm, norm_gain_2, ffn_w_in_2, ffn_w_out_2, mix_w_in_2, conv_w_2, conv_b_2,
            gate_bias_2, mlstm_norm_gain_2, mix_w_out_2):
    L = DEPTH
    cut = lambda w, lo, hi: w[:, :, lo:hi]
    gq = cut(w_in, 1536, 1920).reshape(L, D, 2, 3, HD).transpose(0, 1, 3, 2, 4).reshape(L, D, 384)
    proj = np.concatenate([cut(w_in, 0, 768), gq, cut(w_in, 1920, 2048), cut(w_in, 2560, 2816),
                           cut(w_in, 768, 1152), cut(w_in, 2048, 2176), cut(w_in, 1152, 1536),
                           cut(w_in, 2176, 2560), cut(w_in, 2816, 3072)], 2)
    mem_v = cut(w_mem_kv, 256, 512).reshape(L, NC, P, 256).transpose(0, 2, 1, 3).reshape(L, 1, P, TILE)
    w1 = np.concatenate([stationary_tiles(cut(w_mem_kv, 0, 256).reshape(L, D, 2, P)), mem_v,
                         moving_tiles(proj), moving_tiles(w_out)], 1)

    def ffn(i):
        w = ffn_w_in_2[:, i].reshape(L, D, 2, FC, P).transpose(0, 1, 3, 2, 4).reshape(L, D, 2 * FC, P)
        return [stationary_tiles(w), moving_tiles(ffn_w_out_2[:, i])]

    m = mix_w_in_2
    w2 = np.concatenate(ffn(0) + [moving_tiles(cut(m, 0, 1024)),
                                  stationary_tiles(cut(m, 1536, 2560).reshape(L, D, 8, P)),
                                  moving_tiles(np.concatenate([cut(m, 1024, 1536), cut(m, 2560, 3584)], 2)),
                                  moving_tiles(mix_w_out_2)] + ffn(1), 1)
    col = lambda g: g.reshape(L, NC, P).transpose(0, 2, 1)
    arrays = {
        "x": x, "mem": mem, "w1": w1.reshape(-1, P, TILE), "w2": w2.reshape(-1, P, TILE),
        "pre_norm": col(pre_norm), "mem_norm": col(mem_norm), "post_norm": post_norm,
        "diff_lambda": diff_lambda.reshape(L, 128), "diff_subln": diff_subln,
        "gqa_q_norm": gqa_q_norm, "gqa_k_norm": gqa_k_norm,
        "norm_gain": norm_gain_2.reshape(L, 6, NC, P).transpose(0, 3, 1, 2).reshape(L, P, 48),
        "norm_gain_rows": norm_gain_2.reshape(L * 6, D),
        "w_gate": cut(m, 3584, 3600).reshape(L, NC, P, 16).transpose(0, 2, 1, 3).reshape(L, P, 128),
        "gate_bias": gate_bias_2.reshape(L, 16),
        "conv_w": conv_w_2.reshape(L, CONV, 8, P).transpose(0, 3, 2, 1).reshape(L, P, 40),
        "conv_b": conv_b_2.reshape(L, 8, P).transpose(0, 2, 1),
        "mlstm_gain": mlstm_norm_gain_2,
    }
    return {k: np.ascontiguousarray(v) for k, v in {**arrays, **constants()}.items()}


def kernel(**inputs):
    import concourse.bacc as bacc
    from concourse.bass_utils import run_bass_kernel_spmd

    arrays = lay_out(**{k: np.asarray(v) for k, v in inputs.items()})
    nc = bacc.Bacc("TRN2", target_bir_lowering=False, num_devices=1)
    aps = {k: nc.dram_tensor(f"in_{k}", v.shape, F32, kind="ExternalInput").ap() for k, v in arrays.items()}
    aps["out"] = nc.dram_tensor("out", (1, S, D), F32, kind="ExternalOutput").ap()
    build(nc, aps)
    r = run_bass_kernel_spmd(nc, [{f"in_{k}": v for k, v in arrays.items()}], core_ids=[0])
    return r.results[0]["out"]
```

```python
import math
from contextlib import ExitStack, contextmanager

import numpy as np

import concourse.bass as bass
from concourse import mybir

F32 = mybir.dt.float32
F32R = mybir.dt.float32r
BF16 = mybir.dt.bfloat16
ALU = mybir.AluOpType
ACT = mybir.ActivationFunctionType
AX = mybir.AxisListType

P = 128
S = 512
D = 1024
NT = S // P
NC = D // P
DEPTH = 2
EPS = 1e-6
TILE = 2048
HD = 64
N_DIFF, N_GQA, N_MEMH = 6, 6, 4
N_MEM = 256
FC = 22
MH = 4
CONV = 5
NEG = -1e30

B1_PROJ, B1_KV, B1_OUT, B1_TILES = 0, 12, 14, 18
B2_IN1, B2_OUT1, B2_QK, B2_CONV, B2_ROW, B2_MIXOUT, B2_IN2, B2_OUT2, B2_TILES = 0, 22, 33, 37, 41, 47, 51, 73, 84

AT_X = 16512
AT_HH = AT_X + 16384
AT_HL = AT_HH + 16384
AT_RAW = AT_HL + 16384
AT_WHI = AT_RAW + 16384
AT_WLO = AT_WHI + 16384
AT_GBC = AT_WLO + 16384
AT_SMALL = AT_GBC + 4096
AT_R = AT_SMALL + 8000
END = 229344


class Chain:

    def __init__(self, eng, sem):
        self.eng, self.sem, self.n = eng, sem, 0

    def __call__(self, ins):
        ins.then_inc(self.sem, 1)
        self.n += 1
        self.eng.wait_ge(self.sem, self.n)


def build(nc, a):
    with ExitStack() as ctx:
        def at(name, shape, offset, dt=F32):
            size = int(np.prod(shape[1:])) * (2 if dt == BF16 else 4)
            assert offset % 32 == 0 and offset + size <= END, (name, offset + size)
            return nc.alloc_sbuf_tensor_at(name, shape, dt, offset=offset)

        X = at("X", [P, NT, D], AT_X)
        hTh = at("hTh", [P, NC, S], AT_HH, F32R)
        hTl = at("hTl", [P, NC, S], AT_HL, F32R)
        raw = at("raw", [P, 2, TILE], AT_RAW)
        whi = at("whi", [P, 2, TILE], AT_WHI, F32R)
        wlo = at("wlo", [P, 2, TILE], AT_WLO, F32R)
        gbc = at("gbc", [P, D], AT_GBC)

        small_at = [AT_SMALL]

        def small(name, shape, dt=F32):
            t = at(name, shape, small_at[0], dt)
            small_at[0] += -(-int(np.prod(shape[1:])) * (2 if dt == BF16 else 4) // 32) * 32
            assert small_at[0] <= AT_R, name
            return t

        ident = small("ident", [P, P])
        junk_mem = at("junk_mem", [P, 2, D], AT_R + 77824)
        junk_head = small("junk_head", [P, MH, P], BF16)
        halfneg = small("halfneg", [P, 1])
        gcol = small("gcol", [P, NC])
        sums = small("sums", [P, 4 * NT])
        rinv = small("rinv", [P, 4 * NT])
        ysum = small("ysum", [P, 3 * NT])
        yinv = small("yinv", [P, 3 * NT])
        negmax = small("negmax", [P, 2, 2])
        rowmax = small("rowmax", [P, 2, 1])
        esum = small("esum", [P, 2, 2])
        erec = small("erec", [P, 8, 2])
        otmp = small("otmp", [P, 2, HD])
        lamc = small("lamc", [P, 2])
        lam = small("lam", [P, 8])
        hsum = small("hsum", [P, NT, 8])
        hinv = small("hinv", [P, NT, 8])
        oinv = small("oinv", [P, NT, 8])
        osum = small("osum", [P, NT, 8])
        gate_bias = small("gate_bias", [P, 16])
        gates = small("gates", [P, NT, 2, 2, MH])
        gtmp = small("gtmp", [P, NT, 2, MH])
        gexp = small("gexp", [P, NT, 2, MH])
        logf = small("logf", [P, NT, 2, MH])
        cum = small("cum", [P, NT, 2, MH])
        acol = small("acol", [P, NT, 2, MH])
        mmax = small("mmax", [P, NT, 2, MH])
        nmmax = small("nmmax", [P, NT, 2, MH])
        mexp = small("mexp", [P, NT, 2, MH])
        den = small("den", [P, NT, 2, MH])
        dtmp = small("dtmp", [P, NT, 2, MH])
        drec = small("drec", [P, NT, 2, MH])
        gate_raw = small("gate_raw", [P, NC, 16])
        gate_hi = small("gate_hi", [P, NC, 16], F32R)
        gate_lo = small("gate_lo", [P, NC, 16], F32R)
        upto = small("upto", [P, 2, P])
        ones = small("ones", [P, 1])
        conv_w = small("conv_w", [P, 8, CONV])
        conv_b = small("conv_b", [P, 8])
        rot_cos = small("rot_cos", [P, NT, 8])
        rot_sin = small("rot_sin", [P, NT, 8])

        ps = ctx.enter_context(nc.psum_tensor("ps", [P, 8, 512], F32))

        names = []

        def sem(name):
            s = ctx.enter_context(nc.semaphore(name))
            names.append(s)
            return s

        raw_in = [sem("raw_in0"), sem("raw_in1")]
        hi_ready, lo_ready = sem("hi_ready"), sem("lo_ready")
        w_used = sem("w_used")
        par = sem("par")
        par2 = sem("par2")
        gain_in = sem("gain_in")
        sq_done, r_done, xn_done = sem("sq_done"), sem("r_done"), sem("xn_done")
        tr_done, th_done, tl_done = sem("tr_done"), sem("th_done"), sem("tl_done")
        y_done, ysq_done, yr_done, ysc_done, x_done = (sem("y_done"), sem("ysq_done"), sem("yr_done"),
                                                       sem("ysc_done"), sem("x_done"))
        proj_done = sem("proj_done")
        ev_a, ev_v = sem("ev_a"), sem("ev_v")
        x_in = [sem(f"x_in{t}") for t in range(NT)]
        s_done, mx_done, ex_done, nm_done, t_done, pt_done, ptl_done, pv_done, o_done = (
            sem("s_done"), sem("mx_done"), sem("ex_done"), sem("nm_done"), sem("t_done"),
            sem("pt_done"), sem("ptl_done"), sem("pv_done"), sem("o_done"))
        ot_done = sem("ot_done")
        vh_done, vl_done = sem("vh_done"), sem("vl_done")
        dchain, pchain, achain = sem("dchain"), sem("pchain"), sem("achain")
        q_ready = sem("q_ready")
        qt_done, qte_a, qte_v = sem("qt_done"), sem("qte_a"), sem("qte_v")
        g_v, g_p, g_a = sem("g_v"), sem("g_p"), sem("g_a")
        o_ready = sem("o_ready")
        io = sem("io")
        gu_done, silu_done, gated, acth_done, actl_done = (sem("gu_done"), sem("silu_done"), sem("gated"),
                                                          sem("acth_done"), sem("actl_done"))
        pad_done, cv_done, cs_done = sem("pad_done"), sem("cv_done"), sem("cs_done")
        m1_done, m2_done, ms_done, mt_done, mpt_done, mptl_done, mg_done, mpv_done = (
            sem("m1_done"), sem("m2_done"), sem("ms_done"), sem("mt_done"), sem("mpt_done"), sem("mptl_done"),
            sem("mg_done"), sem("mpv_done"))
        mw_done, mr_done = sem("mw_done"), sem("mr_done")
        sm_t, sm_e = sem("sm_t"), sem("sm_e")
        al_done, cs_mm, mw2_done, mixpar, ab_a, ab_v, one_done = (sem("al_done"), sem("cs_mm"), sem("mw2_done"), sem("mixpar"), sem("ab_a"),
                                                         sem("ab_v"), sem("one_done"))
        nums = [s.num for s in names]
        assert nums == list(range(nums[0], nums[0] + len(nums)))

        def tile_of(T):
            return a["weights"][bass.ds(T, 1)].rearrange("a p n -> (a p) n")

        def stream(sp, base, tiles):
            for slot in range(2):
                sp.sem_inc(raw_in[slot], 16)
            with sp.Fori(1, tiles // 2 + 1) as i:
                for slot in range(2):
                    sp.wait_ge(lo_ready, i * 2 + (slot - 1))
                    sp.dma_start(raw[:, slot, :], tile_of(base + i * 2 + slot)).then_inc(raw_in[slot], 16)

        def hi_part(act, T, i=0):
            act.wait_ge(raw_in[T % 2], 16 * (T // 2 + 1) + i * 16)
            if T >= 2:
                act.wait_ge(w_used, T - 1 + i * 2)
            nc.scalar.activation(whi[:, T % 2, :], raw[:, T % 2, :], ACT.Copy).then_inc(hi_ready, 1)

        def lo_part(dve, T, i=0):
            dve.wait_ge(hi_ready, T + 1 + i * 2)
            nc.vector.tensor_tensor(wlo[:, T % 2, :], raw[:, T % 2, :], whi[:, T % 2, :].bitcast(F32),
                                    ALU.subtract).then_inc(lo_ready, 1)

        def three(out, l_hi, l_lo, r_hi, r_lo, start, stop):
            nc.tensor.matmul(out, l_hi, r_hi, start=start, stop=False)
            nc.tensor.matmul(out, l_hi, r_lo, start=False, stop=False)
            return nc.tensor.matmul(out, l_lo, r_hi, start=False, stop=stop)

        def moving(T):
            return (whi[:, T % 2, :].rearrange("p (b n) -> p b n", n=512),
                    wlo[:, T % 2, :].rearrange("p (b n) -> p b n", n=512))

        def stationary(T):
            return (whi[:, T % 2, :].rearrange("p (c k n) -> p c k n", c=2, k=NC),
                    wlo[:, T % 2, :].rearrange("p (c k n) -> p c k n", c=2, k=NC))

        XN = at("XN", [P, D], AT_R + 90112)
        YT = at("YT", [P, D], AT_R + 94208)
        grow = at("grow", [P, D], AT_R + 98304)

        def halves(ap):
            return ap.rearrange("p (h n) -> p h n", h=2)

        def y_bank(t):
            return (2 * t + 4) % 8

        def y_of(t):
            return ps[:, y_bank(t):y_bank(t) + 2, :]

        def turn_pe(pe, source, t):
            for c in range(NC):
                last = nc.tensor.transpose(ps[:, y_bank(t) + c // 4, (c % 4) * P:(c % 4 + 1) * P],
                                           source[:, c * P:(c + 1) * P], ident[:])
            last.then_inc(tr_done, 1)

        def turned(t):
            return y_of(t).rearrange("p h (c n) -> p (h c) n", c=4)

        def turn_act(act, q, t, pos=None):
            act.wait_ge(tr_done, NT * q + (t if pos is None else pos) + 1)
            nc.scalar.copy(hTh[:, :, t * P:(t + 1) * P], turned(t)).then_inc(th_done, 1)

        def turn_dve(dve, q, t, pos=None):
            dve.wait_ge(th_done, NT * q + (t if pos is None else pos) + 1)
            nc.vector.tensor_tensor(hTl[:, :, t * P:(t + 1) * P], turned(t),
                                    hTh[:, :, t * P:(t + 1) * P].bitcast(F32), ALU.subtract).then_inc(tl_done, 1)

        def square_act(act, n, t):
            nc.scalar.activation(XN[:], X[:, t, :], ACT.Square,
                                 accum_out=sums[:, NT * n + t:NT * n + t + 1]).then_inc(sq_done, 1)

        def root_pool(pool, chain, n, t):
            c = slice(NT * n + t, NT * n + t + 1)
            pool.wait_ge(sq_done, NT * n + t + 1)
            chain(nc.gpsimd.tensor_scalar(sums[:, c], sums[:, c], 1.0 / D, EPS, ALU.mult, ALU.add))
            nc.gpsimd.tensor_tensor(rinv[:, c], sums[:, c], halfneg[:], ALU.pow).then_inc(r_done, 1)

        def norm_dve(dve, n, t):
            dve.wait_ge(r_done, NT * n + t + 1)
            nc.vector.scalar_tensor_tensor(XN[:], X[:, t, :], rinv[:, NT * n + t:NT * n + t + 1], grow[:],
                                           ALU.mult, ALU.mult).then_inc(xn_done, 1)

        def turn_x_pe(pe, n, t):
            pe.wait_ge(xn_done, NT * n + t + 1)
            turn_pe(pe, XN, t)

        def end_pe(pe, n, T0, nk, hi, lo, order, ready):
            T1 = T0 + 2 * nk // 4

            def part(T, t):
                w_hi, w_lo = moving(T)
                for b in range(4):
                    half, k = divmod(4 * (T - T0) + b, nk)
                    last = three(ps[:, y_bank(t) + half, :], hi[:, k, t * P:(t + 1) * P],
                                 lo[:, k, t * P:(t + 1) * P], w_hi[:, b, :], w_lo[:, b, :],
                                 start=k == 0, stop=k == nk - 1)
                return last

            for T in range(T0, T1 - 2):
                pe.wait_ge(lo_ready, T + 1)
                for t in (order if T == T0 else range(NT)):
                    if T == T0:
                        ready(t)
                    last = part(T, t)
                last.then_inc(w_used, 1)
                if T == T0:
                    ready(None)
            pe.wait_ge(lo_ready, T1)
            for t in range(NT):
                first = part(T1 - 2, t)
                last = part(T1 - 1, t)
                if t == NT - 1:
                    first.then_inc(w_used, 1)
                last.then_inc(w_used if t == NT - 1 else y_done, 1)
                if t == 2:
                    turn_x_pe(pe, n, 0)
            for t in range(1, NT):
                turn_x_pe(pe, n, t)

        def end_act(act, n, q, T1):
            for t in range(NT):
                if t < NT - 1:
                    act.wait_ge(y_done, (NT - 1) * n + t + 1)
                else:
                    act.wait_ge(w_used, T1)
                nc.scalar.activation(halves(YT[:]), y_of(t), ACT.Square,
                                     accum_out=ysum[:, NT * n + t:NT * n + t + 1]).then_inc(ysq_done, 1)
                if t:
                    turn_act(act, q, t - 1)
                act.wait_ge(x_done, NT * n + t + 1)
                square_act(act, n, t)
            turn_act(act, q, NT - 1)
            hi_part(act, T1)
            hi_part(act, T1 + 1)

        def end_pool(pool, chain, n, factor):
            for t in range(NT):
                c = slice(NT * n + t, NT * n + t + 1)
                pool.wait_ge(ysq_done, NT * n + t + 1)
                chain(nc.gpsimd.tensor_scalar(ysum[:, c], ysum[:, c], 1.0 / D, EPS, ALU.mult, ALU.add))
                if factor == 1.0:
                    nc.gpsimd.tensor_tensor(yinv[:, c], ysum[:, c], halfneg[:], ALU.pow).then_inc(yr_done, 1)
                else:
                    chain(nc.gpsimd.tensor_tensor(yinv[:, c], ysum[:, c], halfneg[:], ALU.pow))
                    nc.gpsimd.tensor_scalar(yinv[:, c], yinv[:, c], factor, None, ALU.mult).then_inc(yr_done, 1)
                root_pool(pool, chain, n, t)

        def end_dve(dve, chain, n, q, T1):
            dve.wait_ge(gain_in, 32 * (n + 1))
            for t in range(NT):
                dve.wait_ge(yr_done, NT * n + t + 1)
                chain(nc.vector.scalar_tensor_tensor(halves(YT[:]), y_of(t), yinv[:, NT * n + t:NT * n + t + 1],
                                                     halves(gbc[:]), ALU.mult, ALU.mult))
                nc.vector.tensor_tensor(X[:, t, :], X[:, t, :], YT[:], ALU.add).then_inc(x_done, 1)
                if t:
                    turn_dve(dve, q, t - 1)
                norm_dve(dve, n, t)
            turn_dve(dve, q, NT - 1)
            lo_part(dve, T1)
            lo_part(dve, T1 + 1)

        def project_pe(pe, T0, b, banks, turn=None, last_bank=None):
            order = [(half, t) for half in range(2) for t in range(NT)]
            if turn is not None:
                order.sort(key=lambda half_t: half_t[1] == NT - 1)
            for i, (half, t) in enumerate(order):
                T = T0 + half
                w_hi, w_lo = moving(T)
                if t == 0:
                    pe.wait_ge(lo_ready, T + 1)
                if turn is not None and half == 0:
                    pe.wait_ge(tl_done, NT * turn + t + 1)
                if last_bank and (half, t) == (0, NT - 1):
                    last_bank()
                for kk in range(4):
                    k = 4 * half + kk
                    last = three(ps[:, banks + t, :], hTh[:, k, t * P:(t + 1) * P],
                                 hTl[:, k, t * P:(t + 1) * P], w_hi[:, kk, :], w_lo[:, kk, :],
                                 start=k == 0, stop=k == NC - 1)
                if t == NT - 1:
                    last.then_inc(w_used, 1)
                elif half == 1:
                    last.then_inc(proj_done, 1)

        def projected(eng, T0, b, t):
            if t == NT - 1:
                eng.wait_ge(w_used, T0 + 2)
            else:
                eng.wait_ge(proj_done, (NT - 1) * b + t + 1)

        FILL_STEPS, FILL_START = 6, 8
        FILL = {"diff": 5, "gqa": 2, "mem": 3, "dilated": 0}

        def fill(filler, n, bank):
            for _ in range(n):
                nc.tensor.matmul(ps[:, bank, :], *filler, start=True, stop=True)

        def attend_pe(pe, units, buf, v_ready, filler):
            E, MS, PTh, PTl = buf
            for s in range(len(units) + 4):
                if s < FILL_STEPS:
                    fill(filler, FILL_START, 7)
                if s < len(units):
                    if s >= 2:
                        pe.wait_ge(ex_done, s - 1)
                    if s >= FILL_STEPS:
                        fill(filler, FILL[units[s]["kind"]], 2 * (s % 2))
                    for j, (q_hi, q_lo, k_hi, k_lo) in enumerate(units[s]["scores"]):
                        last = three(ps[:, 2 * (s % 2) + j, 0:units[s]["keys"]], q_hi, q_lo, k_hi, k_lo,
                                     start=True, stop=True)
                    last.then_inc(s_done, 1)
                if 0 <= s - 2 < len(units):
                    u = s - 2
                    if units[u]["kind"] == "diff":
                        pe.wait_ge(nm_done, u + 1)
                    else:
                        pe.wait_ge(ex_done, u + 1)
                    if u >= 2:
                        pe.wait_ge(ptl_done, u - 1)
                    for b in range(units[u]["keys"] // P):
                        last = nc.tensor.transpose(ps[:, 4 + u % 2, b * P:(b + 1) * P],
                                                   E[:, u % 3, 0, b * P:(b + 1) * P], ident[:])
                    last.then_inc(t_done, 1)
                if s >= 4:
                    u = s - 4
                    if u == 0:
                        v_ready()
                    pe.wait_ge(ptl_done, u + 1)
                    if u >= 2:
                        pe.wait_ge(o_done, u - 1)
                    nb = units[u]["keys"] // P
                    both = ps[:, 6 + u % 2, 0:2 * HD].rearrange("p (two n) -> p two n", two=2)
                    v = units[u]["v"]
                    for b in range(nb):
                        last = nc.tensor.matmul(both, PTh[:, u % 2, b, :], v[b], start=b == 0, stop=b == nb - 1)
                        if b < nb - 1:
                            nc.tensor.matmul(both[:, 0, :], PTl[:, u % 2, b, :], v[b][:, 0, :], start=False, stop=False)
                        if b == nb - 2:
                            nc.tensor.matmul(both[:, 0, :], PTl[:, u % 2, nb - 1, :], v[nb - 1][:, 0, :],
                                             start=False, stop=False)
                    last.then_inc(pv_done, 1)

        def part_of_pt(PT, u, n):
            return PT[:, u % 2, 0:n // P, :].rearrange("p b n -> p (b n)")

        def attend_act(act, units, buf, beside=None):
            E, MS, PTh, PTl = buf
            for s in range(len(units) + 3):
                if s >= 3:
                    u = s - 3
                    n = units[u]["keys"]
                    act.wait_ge(t_done, u + 1)
                    if u >= 2:
                        act.wait_ge(pv_done, u - 1)
                    nc.scalar.copy(part_of_pt(PTh, u, n), ps[:, 4 + u % 2, 0:n]).then_inc(pt_done, 1)
                if s < len(units):
                    act.wait_ge(mx_done, s + 1)
                    for j in range(len(units[s]["scores"])):
                        n = units[s]["keys"]
                        last = nc.scalar.activation(
                            E[:, s % 3, j, 0:n],
                            MS[:, s % 2, 0:n] if units[s]["kind"] == "dilated" else ps[:, 2 * (s % 2) + j, 0:n],
                            ACT.Exp, bias=negmax[:, s % 2, j:j + 1], accum_out=esum[:, s % 2, j:j + 1])
                    last.then_inc(ex_done, 1)
                if beside:
                    beside(s)

        def attend_dve(dve, chain, units, buf, beside=None, after=None):
            E, MS, PTh, PTl = buf
            for s in range(len(units) + 5):
                if s < len(units):
                    un, n = units[s], units[s]["keys"]
                    dve.wait_ge(s_done, s + 1)
                    if un["kind"] == "dilated":
                        chain(nc.vector.tensor_tensor_reduce(
                            out=MS[:, s % 2, :], in0=ps[:, 2 * (s % 2), :], in1=un["bias"], scale=1.0,
                            scalar=-3.0e38, op0=ALU.add, op1=ALU.max, accum_out=rowmax[:, s % 2, :]))
                        nc.vector.tensor_scalar(negmax[:, s % 2, 0:1], rowmax[:, s % 2, :], -1.0, None,
                                                ALU.mult).then_inc(mx_done, 1)
                    else:
                        js = len(un["scores"])
                        nc.vector.tensor_reduce(negmax[:, s % 2, 0:js], ps[:, 2 * (s % 2):2 * (s % 2) + js, 0:n],
                                                AX.X, ALU.max, negate=True).then_inc(mx_done, 1)
                if 0 <= s - 3 < len(units):
                    u = s - 3
                    n = units[u]["keys"]
                    dve.wait_ge(pt_done, u + 1)
                    nc.vector.tensor_tensor(part_of_pt(PTl, u, n), ps[:, 4 + u % 2, 0:n],
                                            part_of_pt(PTh, u, n).bitcast(F32), ALU.subtract).then_inc(ptl_done, 1)
                if s >= 5:
                    u = s - 5
                    dve.wait_ge(pv_done, u + 1)
                    nc.vector.tensor_scalar(otmp[:, u % 2, :], ps[:, 6 + u % 2, HD:2 * HD], erec[:, u % 8, 0:1], None,
                                            ALU.mult).then_inc(ot_done, 1)
                if 1 <= s <= len(units):
                    u = s - 1
                    dve.wait_ge(ex_done, u + 1)
                    r = erec[:, u % 8, :]
                    if units[u]["kind"] == "diff":
                        chain(nc.vector.reciprocal(r, esum[:, u % 2, :]))
                        chain(nc.vector.tensor_scalar(r[:, 1:2], r[:, 1:2], esum[:, u % 2, 0:1], lam[:, 5:6],
                                                      ALU.mult, ALU.mult))
                        nc.vector.scalar_tensor_tensor(E[:, u % 3, 0, :], E[:, u % 3, 1, :], r[:, 1:2],
                                                       E[:, u % 3, 0, :], ALU.mult, ALU.add).then_inc(nm_done, 1)
                    else:
                        nc.vector.reciprocal(r[:, 0:1], esum[:, u % 2, 0:1]).then_inc(nm_done, 1)
                if s >= 5:
                    u = s - 5
                    dve.wait_ge(ot_done, u + 1)
                    nc.vector.scalar_tensor_tensor(units[u]["out"], ps[:, 6 + u % 2, 0:HD], erec[:, u % 8, 0:1],
                                                   otmp[:, u % 2, :], ALU.mult, ALU.add).then_inc(o_done, 1)
                    if after:
                        after(u)
                if beside:
                    beside(s)

        with nc.Block() as block:
            @block.sync
            def _(sp):
                for t in range(NT):
                    sp.dma_start(X[:, t, :], a["x"][0, t * P:(t + 1) * P, :]).then_inc(x_in[t], 16)
                    if t % 2 == 0:
                        sp.dma_start(raw[:, t // 2, :], a["weights"][t // 2]).then_inc(raw_in[t // 2], 16)

            @block.tensor
            def _(pe):
                pe.wait_ge(par, 32)
                for t in range(NT):
                    turn_x_pe(pe, 0, t)

            @block.scalar
            def _(act):
                act.dma_start(ident[:], a["identity"]).then_inc(par, 16)
                act.dma_start(grow[:], a["next_gain"][0:1].to_broadcast([P, D])).then_inc(par, 16)
                for t in range(NT):
                    if t:
                        turn_act(act, 0, t - 1)
                    act.wait_ge(x_in[t], 16)
                    square_act(act, 0, t)
                turn_act(act, 0, NT - 1)
                for T in range(2):
                    act.wait_ge(raw_in[T], 16)
                    nc.scalar.activation(whi[:, T, :], raw[:, T, :], ACT.Copy).then_inc(hi_ready, 1)

            @block.vector
            def _(dve):
                dve.wait_ge(par, 32)
                for t in range(NT):
                    if t:
                        turn_dve(dve, 0, t - 1)
                    norm_dve(dve, 0, t)
                turn_dve(dve, 0, NT - 1)
                lo_part(dve, 0)
                lo_part(dve, 1)

            @block.gpsimd
            def _(pool):
                chain = Chain(pool, pchain)
                chain(nc.gpsimd.memset(halfneg[:], -0.5))
                for t in range(NT):
                    root_pool(pool, chain, 0, t)

        def next_round():
            nc.sync.sem_clear(range(nums[0], nums[-1] + 1))
            nc.all_engine_barrier()

        @contextmanager
        def layers():
            with nc.Fori(0, DEPTH) as layer:
                with nc.Block() as block:
                    yield layer, block
                next_round()

        next_round()

        P1 = at("P1", [P, NT, 3072], AT_R)
        P1r = at("P1r", [P, NT, 3072], AT_R, F32R)
        QXh = at("QXh", [P, 4, S], AT_R + 57344, F32R)
        QXl = at("QXl", [P, 4, S], AT_R + 65536, F32R)
        memX = at("memX", [P, 2, D], AT_R + 49152)
        memTh = at("memTh", [P, NC, N_MEM], AT_R + 49152 + 8192, F32R)
        memTl = at("memTl", [P, NC, N_MEM], AT_R + 49152 + 16384, F32R)
        mkh = at("mkh", [P, 2, N_MEM], AT_R + 49152, F32R)
        mkl = at("mkl", [P, 2, N_MEM], AT_R + 51200, F32R)
        mv = at("mv", [P, 2, 2, N_MEM], AT_R + 53248, F32R)
        lin_cos = at("lin_cos", [P, NT, 16], AT_R + 86016)
        lin_sin = at("lin_sin", [P, NT, 16], AT_R + 86272)
        ax_cos = at("ax_cos", [P, NT, 2, 16], AT_R + 86528)
        ax_sin = at("ax_sin", [P, NT, 2, 16], AT_R + 87040)
        qk_gain = at("qk_gain", [P, 2, HD], AT_R + 87552)
        subln = at("subln", [P, HD], AT_R + 100352)
        lamin = at("lamin", [P, 4, 32], AT_R + 88064)
        lamt = at("lamt", [P, 2, 32], AT_R + 88576)
        rA = at("rA", [P, 768], AT_R + 77824)
        rB = at("rB", [P, 768], AT_R + 77824 + 3072)
        osq = at("osq", [P, 384], AT_R + 100608)
        buf1 = (at("E1", [P, 3, 2, S], AT_R + 77824), None, at("PTh1", [P, 2, 4, P], AT_R + 90112, F32R),
                at("PTl1", [P, 2, 4, P], AT_R + 94208, F32R))
        BANK1 = [4, 0, 4, 0, 4, 4]

        filler1 = (mkh[:, 0, 0:P], mv[:, 0, :, :].rearrange("p a n -> p (a n)"))

        def turned1(c, rows=slice(0, P), cols=slice(0, S)):
            return (hTh[rows, c, cols], hTl[rows, c, cols]) if c < NC else (QXh[rows, c - NC, cols],
                                                                            QXl[rows, c - NC, cols])

        def values1(b, col):
            return P1r[:, b, 1024:2048].rearrange("p (two n) -> p two n", two=2)[:, :, col - 1536:col - 1536 + HD]
        TURN_ORDER = [0, 2, 1, 3]
        par_all = 16 * 11

        def scores1():
            units = []
            for t in range(NT):
                tk = slice(t * P, (t + 1) * P)
                for h in range(N_DIFF):
                    sc = []
                    for j in range(2):
                        c, r = divmod(2 * h + j, 4)
                        rows = slice(32 * r, 32 * r + 32)
                        sc.append(turned1(c, rows, tk) + turned1(3 + c, rows))
                    units.append(dict(kind="diff", t=t, keys=S, scores=sc, out=P1[:, t, HD * h:HD * (h + 1)],
                                      v=[values1(b, 1536 + HD * h) for b in range(NT)]))
                for h in range(N_GQA):
                    kv, c = divmod(h, 3)
                    rows = slice(HD * kv, HD * kv + HD)
                    o = 384 + HD * h
                    units.append(dict(kind="gqa", t=t, keys=S, scores=[turned1(6 + c, rows, tk) + turned1(9, rows)],
                                      out=P1[:, t, o:o + HD],
                                      v=[values1(b, 1920 + HD * kv) for b in range(NT)]))
                for h in range(N_MEMH):
                    c, r = divmod(h, 2)
                    rows = slice(HD * r, HD * r + HD)
                    o = 768 + HD * h
                    units.append(dict(kind="mem", t=t, keys=N_MEM, out=P1[:, t, o:o + HD],
                                      scores=[turned1(10 + c, rows, tk) + (mkh[rows, c, :], mkl[rows, c, :])],
                                      v=[mv[:, b, :, HD * h:HD * (h + 1)] for b in range(2)]))
            return units

        units1 = scores1()
        scale1 = [32 ** -0.5] * 3 + [None] * 3 + [0.125] * 3 + [None] + [0.125] * 2

        with layers() as (layer, block):
            one = lambda name: a[name][bass.ds(layer, 1)]

            @block.sync
            def _(sp):
                sp.dma_start(memX[:], a["mem"].rearrange("b (t p) d -> p (b t) d", p=P)).then_inc(par, 16)
                sp.dma_start(gcol[:], one("mem_norm").rearrange("a p c -> (a p) c")).then_inc(par, 16)
                for dst, name in ((lin_cos, "lin_cos"), (lin_sin, "lin_sin")):
                    sp.dma_start(dst[:], a[name]).then_inc(par, 16)
                for dst, name in ((ax_cos, "ax_cos"), (ax_sin, "ax_sin")):
                    sp.dma_start(dst[:], a[name]).then_inc(par, 16)
                for dst, name in ((qk_gain[:, 0, :], "gqa_q_norm"), (qk_gain[:, 1, :], "gqa_k_norm"),
                                  (subln[:], "diff_subln")):
                    sp.dma_start(dst, one(name).to_broadcast([P, HD])).then_inc(par, 16)
                sp.dma_start(lamin[:].rearrange("p a b -> p (a b)"),
                             one("diff_lambda").to_broadcast([P, 128])).then_inc(par, 16)
                sp.dma_start(lamc[:], one("lambda_init").to_broadcast([P, 2])).then_inc(par, 16)
                sp.dma_start(gbc[:], a["post_gain"][bass.ds(layer, 1)].to_broadcast([P, D])).then_inc(gain_in, 16)
                stream(sp, layer * B1_TILES, B1_TILES)

            @block.tensor
            def _(pe):
                for b in range(6):
                    if 2 <= b < 5:
                        pe.wait_ge(ev_a, 2 * (b - 1))
                        pe.wait_ge(ev_v, 2 * (b - 1))
                    if b == 5:
                        pe.wait_ge(ev_a, 8)
                        pe.wait_ge(ev_v, 8)
                        pe.wait_ge(g_v, 2)
                        for c in range(NC):
                            for t in range(2):
                                last = nc.tensor.transpose(ps[:, c // 2, (2 * (c % 2) + t) * P:
                                                              (2 * (c % 2) + t + 1) * P],
                                                           memX[:, t, c * P:(c + 1) * P], ident[:])
                            if c % 2:
                                last.then_inc(sm_t, 1)
                        pe.wait_ge(ev_a, 12)
                    project_pe(pe, B1_PROJ + 2 * b, b, BANK1[b])
                w_hi, w_lo = stationary(B1_KV)
                pe.wait_ge(mw_done, NC)
                pe.wait_ge(lo_ready, B1_KV + 1)
                for c in range(2):
                    for k in range(NC):
                        last = three(ps[:, c, 0:N_MEM], w_hi[:, c, k, :], w_lo[:, c, k, :],
                                     memTh[:, k, :], memTl[:, k, :], k == 0, k == NC - 1)
                    last.then_inc(sm_t if c == 0 else w_used, 1)
                v_hi = whi[:, 1, :].rearrange("p (k n) -> p k n", k=NC)
                v_lo = wlo[:, 1, :].rearrange("p (k n) -> p k n", k=NC)
                pe.wait_ge(lo_ready, B1_KV + 2)
                for t in range(2):
                    for k in range(NC):
                        last = three(ps[:, 2 + t, 0:N_MEM], memTh[:, k, t * P:(t + 1) * P],
                                     memTl[:, k, t * P:(t + 1) * P], v_hi[:, k, :], v_lo[:, k, :],
                                     k == 0, k == NC - 1)
                    last.then_inc(sm_t if t == 0 else w_used, 1)
                pe.wait_ge(ev_a, 8 + 8)
                pe.wait_ge(q_ready, NT)
                for c in range(12):
                    if c == 4:
                        pe.wait_ge(mw_done, NC + 4)
                    if c >= 8:
                        pe.wait_ge(qte_v, c - 7)
                    if c >= 4:
                        fill(filler1, 2, (c + 4) % 8)
                    for t in range(NT):
                        last = nc.tensor.transpose(ps[:, (c + 4) % 8, t * P:(t + 1) * P], P1[:, t, c * P:(c + 1) * P],
                                                   ident[:])
                    last.then_inc(qt_done, 1)
                pe.wait_ge(qte_v, 5)
                fill(filler1, 8, 0)
                pe.wait_ge(qte_v, 12)
                attend_pe(pe, units1, buf1, lambda: pe.wait_ge(vl_done, NT), filler1)
                for t in TURN_ORDER:
                    if y_bank(t) == 6:
                        pe.wait_ge(o_done, len(units1))
                    pe.wait_ge(o_ready, t + 1)
                    turn_pe(pe, P1[:, t, 0:D], t)
                end_pe(pe, 0, B1_OUT, NC, hTh, hTl, TURN_ORDER,
                       lambda t: t is not None and pe.wait_ge(tl_done, TURN_ORDER.index(t) + 1))

            @block.scalar
            def _(act):
                act.wait_ge(par, par_all)
                for t in range(2):
                    nc.scalar.activation(junk_mem[:, t, :], memX[:, t, :], ACT.Square,
                                         accum_out=osum[:, t, 0:1]).then_inc(g_a, 1)
                act.wait_ge(g_v, 3)
                nc.scalar.activation(lam[:, 2:4], lam[:, 0:2], ACT.Exp).then_inc(g_a, 1)
                act.sem_inc(hi_ready, 2)
                for b in range(6):
                    hi_part(act, B1_PROJ + 2 * b + 2)
                    for t in range(NT):
                        if b >= 4:
                            projected(act, B1_PROJ + 2 * b, b, t)
                            nc.scalar.activation(P1[:, t, 512 * b:512 * (b + 1)], ps[:, BANK1[b] + t, :],
                                                 ACT.Silu).then_inc(ev_a, 1)
                        elif t % 2 == 0:
                            projected(act, B1_PROJ + 2 * b, b, t)
                            nc.scalar.copy(P1[:, t, 512 * b:512 * (b + 1)], ps[:, BANK1[b] + t, :]
                                           ).then_inc(ev_a, 1)
                    hi_part(act, B1_PROJ + 2 * b + 3)
                    if b == 4:
                        for c in range(NC):
                            act.wait_ge(sm_t, c // 2 + 1)
                            nc.scalar.activation(memTh[:, c, :], ps[:, c // 2, 256 * (c % 2):256 * (c % 2 + 1)],
                                                 ACT.Copy, scale=gcol[:, c:c + 1]).then_inc(sm_e, 1)
                for c in range(2):
                    act.wait_ge(*((sm_t, NC // 2 + 1), (w_used, B1_KV + 1))[c])
                    nc.scalar.copy(mkh[:, c, :], ps[:, c, 0:N_MEM]).then_inc(sm_e, 1)
                hi_part(act, B1_KV + 2)
                for t in range(2):
                    act.wait_ge(*((sm_t, NC // 2 + 2), (w_used, B1_KV + 2))[t])
                    nc.scalar.copy(mv[:, t, 0, :], ps[:, 2 + t, 0:N_MEM]).then_inc(sm_e, 1)
                hi_part(act, B1_KV + 3)
                for c in range(12):
                    act.wait_ge(qt_done, c + 1)
                    nc.scalar.activation(turned1(c)[0], ps[:, (c + 4) % 8, :], ACT.Copy, scale=scale1[c] or 1.0
                                         ).then_inc(qte_a, 1)

                def value_high(s):
                    if s < NT:
                        nc.scalar.copy(P1r[:, s, 1024:1536], P1[:, s, 1536:2048]).then_inc(vh_done, 1)

                attend_act(act, units1, buf1, value_high)
                for pos, t in enumerate(TURN_ORDER):
                    turn_act(act, 0, t, pos)
                act.dma_start(grow[:], a["next_gain"][bass.ds(layer + 1, 1)].to_broadcast([P, D])
                              ).then_inc(gain_in, 16)
                hi_part(act, B1_OUT + 2)
                hi_part(act, B1_OUT + 3)
                end_act(act, 0, 1, B1_TILES)

            @block.vector
            def _(dve):
                chain = Chain(dve, dchain)
                for t in range(2):
                    dve.wait_ge(g_p, t + 1)
                    nc.vector.tensor_scalar(memX[:, t, :], memX[:, t, :], oinv[:, t, 0:1], None, ALU.mult
                                            ).then_inc(g_v, 1)
                dve.wait_ge(par, par_all)
                for j in range(2):
                    chain(nc.vector.tensor_tensor_reduce(
                        out=lamt[:, j, :], in0=lamin[:, 2 * j, :], in1=lamin[:, 2 * j + 1, :], scale=1.0, scalar=0.0,
                        op0=ALU.mult, op1=ALU.add, accum_out=lam[:, j:j + 1]))
                nc.vector.tensor_scalar(subln[:], subln[:], lamc[:, 1:2], None, ALU.mult).then_inc(g_v, 1)
                dve.wait_ge(g_a, 3)
                chain(nc.vector.tensor_tensor(lam[:, 4:5], lam[:, 3:4], lam[:, 2:3], ALU.subtract))
                chain(nc.vector.tensor_tensor(lam[:, 5:6], lam[:, 4:5], lamc[:, 0:1], ALU.subtract))
                dve.sem_inc(lo_ready, 2)

                def rotate(x, n, cos, sin, out_inc=None):
                    A = rA[:, 0:32 * n].rearrange("p (n r d) -> p n r d", r=2, d=16)
                    B = rB[:, 0:32 * n].rearrange("p (n r d) -> p n r d", r=2, d=16)
                    xs = x.rearrange("p n (r d) -> p n r d", r=2)
                    c4 = cos.unsqueeze(1).unsqueeze(1).to_broadcast([P, n, 2, 16])
                    s3 = sin.unsqueeze(1).to_broadcast([P, n, 16])
                    nc.vector.tensor_tensor(A, xs, c4, ALU.mult)
                    nc.vector.scalar_tensor_tensor(B[:, :, 0, :], xs[:, :, 1, :], -1.0, s3, ALU.mult, ALU.mult)
                    chain(nc.vector.tensor_tensor(B[:, :, 1, :], xs[:, :, 0, :], s3, ALU.mult))
                    return nc.vector.tensor_tensor(x, A.rearrange("p n r d -> p n (r d)"),
                                                   B.rearrange("p n r d -> p n (r d)"), ALU.add)

                def rope(t):
                    gq = P1[:, t, 768:1280].rearrange("p (h d) -> p h d", d=HD)
                    sq = rA[:, 0:512].rearrange("p (h d) -> p h d", d=HD)
                    chain(nc.vector.tensor_tensor(sq, gq, gq, ALU.mult))
                    nc.vector.tensor_reduce(hsum[:, t, :], sq, AX.X, ALU.add).then_inc(g_v, 1)
                    dve.wait_ge(g_v, 3 + t + 1)
                    chain(rotate(P1[:, t, 0:768].rearrange("p (n d) -> p n d", d=32), 24, lin_cos[:, t, :],
                                 lin_sin[:, t, :]))
                    dve.wait_ge(g_p, 2 + t + 1)
                    chain(nc.vector.tensor_tensor(gq, gq, hinv[:, t, :].unsqueeze(2).to_broadcast([P, 8, HD]),
                                                  ALU.mult))
                    nc.vector.tensor_tensor(gq[:, 0:6, :], gq[:, 0:6, :],
                                            qk_gain[:, 0:1, :].to_broadcast([P, 6, HD]), ALU.mult)
                    chain(nc.vector.tensor_tensor(gq[:, 6:8, :], gq[:, 6:8, :],
                                                  qk_gain[:, 1:2, :].to_broadcast([P, 2, HD]), ALU.mult))
                    for axis in range(2):
                        last = rotate(gq[:, :, 32 * axis:32 * axis + 32], 8, ax_cos[:, t, axis, :],
                                      ax_sin[:, t, axis, :])
                        if axis == 0:
                            chain(last)
                    last.then_inc(q_ready, 1)
                    dve.wait_ge(q_ready, t + 1)

                for b in range(6):
                    lo_part(dve, B1_PROJ + 2 * b + 2)
                    if b < 4:
                        for t in (1, 3):
                            projected(dve, B1_PROJ + 2 * b, b, t)
                            nc.vector.tensor_copy(P1[:, t, 512 * b:512 * (b + 1)], ps[:, BANK1[b] + t, :]
                                                  ).then_inc(ev_v, 1)
                    lo_part(dve, B1_PROJ + 2 * b + 3)
                    if b == 3:
                        dve.wait_ge(ev_a, 6)
                        dve.wait_ge(ev_v, 6)
                    if b == 4:
                        for c in range(NC):
                            dve.wait_ge(sm_e, c // 2 * 2 + 2)
                            nc.vector.scalar_tensor_tensor(
                                memTl[:, c, :], ps[:, c // 2, 256 * (c % 2):256 * (c % 2 + 1)],
                                gcol[:, c:c + 1], memTh[:, c, :].bitcast(F32), ALU.mult, ALU.subtract
                                ).then_inc(mw_done, 1)
                    if b in (3, 4):
                        rope(2 * (b - 3))
                        rope(2 * (b - 3) + 1)
                for i in range(2):
                    for c in range(2):
                        low, high = (mv[:, c, 1, :], mv[:, c, 0, :]) if i else (mkl[:, c, :], mkh[:, c, :])
                        dve.wait_ge(sm_e, NC + 2 * i + c + 1)
                        nc.vector.tensor_tensor(low, ps[:, 2 * i + c, 0:N_MEM], high.bitcast(F32), ALU.subtract
                                                ).then_inc(mw_done, 1)
                    lo_part(dve, B1_KV + 2 + i)
                for c in range(12):
                    dve.wait_ge(qte_a, c + 1)
                    nc.vector.scalar_tensor_tensor(turned1(c)[1], ps[:, (c + 4) % 8, :], scale1[c] or 1.0,
                                                   turned1(c)[0].bitcast(F32), ALU.mult, ALU.subtract
                                                   ).then_inc(qte_v, 1)

                def value_low(s):
                    if s < NT:
                        dve.wait_ge(vh_done, s + 1)
                        nc.vector.tensor_tensor(P1r[:, s, 1536:2048], P1[:, s, 1536:2048],
                                                P1r[:, s, 1024:1536].bitcast(F32), ALU.subtract).then_inc(vl_done, 1)

                def after(u):
                    t, i = divmod(u, 16)
                    if i == 9:
                        dve.wait_ge(g_p, 6 + t + 1)
                        nc.vector.tensor_reduce(osum[:, t, 0:6], osq[:].rearrange("p (h d) -> p h d", d=HD), AX.X,
                                                ALU.add).then_inc(g_v, 1)

                attend_dve(dve, chain, units1, buf1, value_low, after)
                for pos, t in enumerate(TURN_ORDER):
                    turn_dve(dve, 0, t, pos)
                lo_part(dve, B1_OUT + 2)
                lo_part(dve, B1_OUT + 3)
                end_dve(dve, chain, 0, 1, B1_TILES)

            @block.gpsimd
            def _(pool):
                chain = Chain(pool, pchain)

                def inverse_root(src, dst, width, n, done):
                    chain(nc.gpsimd.tensor_scalar(src, src, 1.0 / width, EPS, ALU.mult, ALU.add))
                    nc.gpsimd.tensor_tensor(dst, src, halfneg[:].to_broadcast([P, n]), ALU.pow).then_inc(done, 1)

                for t in range(2):
                    pool.wait_ge(g_a, t + 1)
                    inverse_root(osum[:, t, 0:1], oinv[:, t, 0:1], D, 1, g_p)
                for t in range(NT):
                    pool.wait_ge(g_v, 3 + t + 1)
                    inverse_root(hsum[:, t, :], hinv[:, t, :], HD, 8, g_p)
                for t in range(NT):
                    oa = P1[:, t, 0:384].rearrange("p (h d) -> p h d", d=HD)
                    pool.wait_ge(o_done, 16 * t + 6)
                    nc.gpsimd.tensor_tensor(osq[:], P1[:, t, 0:384], P1[:, t, 0:384], ALU.mult).then_inc(g_p, 1)
                    pool.wait_ge(g_v, 7 + t + 1)
                    chain(nc.gpsimd.tensor_scalar(osum[:, t, 0:6], osum[:, t, 0:6], 1.0 / HD, EPS,
                                                  ALU.mult, ALU.add))
                    chain(nc.gpsimd.tensor_tensor(oinv[:, t, 0:6], osum[:, t, 0:6], halfneg[:].to_broadcast([P, 6]),
                                                  ALU.pow))
                    chain(nc.gpsimd.tensor_tensor(oa, oa, oinv[:, t, 0:6].unsqueeze(2).to_broadcast([P, 6, HD]),
                                                  ALU.mult))
                    chain(nc.gpsimd.tensor_tensor(oa, oa, subln[:].unsqueeze(1).to_broadcast([P, 6, HD]),
                                                  ALU.mult))
                    pool.wait_ge(o_done, 16 * t + 12)
                    nc.gpsimd.tensor_tensor(P1[:, t, 0:768], P1[:, t, 0:768], P1[:, t, 2048:2816], ALU.mult)
                    pool.wait_ge(o_done, 16 * (t + 1))
                    nc.gpsimd.tensor_tensor(P1[:, t, 768:D], P1[:, t, 768:D], P1[:, t, 2816:3072], ALU.mult
                                            ).then_inc(o_ready, 1)
                end_pool(pool, chain, 0, 1.0)

        P2 = at("P2", [P, NT, 2560], AT_R)
        P2r = at("P2r", [P, NT, 2560], AT_R, F32R)
        MQK = at("MQK", [P, 8, S], AT_R + 40960)
        MQKl = at("MQKl", [P, 8, S], AT_R + 40960, F32R)
        VA = at("VA", [P, NT, 2, 512], AT_R + 57344, F32R)

        filler2 = (VA[:, 0, 0, 0:P], VA[:, 0, 0, :])

        def value_part(b, t, part):
            return VA[:, t, part, :] if b == 2 else P2r[:, t, 1536 - 512 * part:2048 - 512 * part]
        AB = at("AB", [P, 8, S], AT_HH)
        masks = at("masks", [P, 2, S], AT_R + 73728)
        BM = at("BM", [P, NT, S], AT_R + 77824)
        acc = at("acc", [P, 2, S], AT_R + 86016)
        mgain = at("mgain", [P, S], AT_R + 94208)
        pad = at("pad", [P, 2, S + 4], AT_R + 98304)
        rt = at("rt", [P, 2, 3, 128], AT_R + 90112)
        SW = at("SW", [P, 2, MH, 640], AT_R + 77824)
        aTh = at("aTh", [P, S], AT_R + 86016, F32R)
        aTl = at("aTl", [P, S], AT_R + 88064, F32R)
        identr = at("identr", [P, P], AT_R + 90112, F32R)
        PT2h = at("PT2h", [P, 2, NT, P], AT_R + 57344, F32R)
        PT2l = at("PT2l", [P, 2, NT, P], AT_R + 61440, F32R)
        acth = at("acth", [P, FC, S], AT_R, F32R)
        actl = at("actl", [P, FC, S], AT_R + 45056, F32R)
        sil = at("sil", [P, 2, S], AT_R + 90112)
        afull = at("afull", [P, 2, S], AT_R + 94208)
        buf2 = (at("E2", [P, 3, 1, S], AT_R + 86016), at("MS", [P, 2, S], AT_R + 96256),
                at("PTh2", [P, 2, 4, P], AT_R + 92160, F32R), at("PTl2", [P, 2, 4, P], AT_GBC, F32R))
        par2_all = 16 * 7

        units2 = []
        for t in range(NT):
            for h in range(8):
                c, r = divmod(h, 2)
                rows = slice(HD * r, HD * r + HD)
                units2.append(dict(kind="dilated", t=t, keys=S, bias=BM[:, t, :],
                                   scores=[(hTh[rows, c, t * P:(t + 1) * P], hTl[rows, c, t * P:(t + 1) * P],
                                            hTh[rows, 4 + c, :], hTl[rows, 4 + c, :])],
                                   out=P2[:, t, HD * h:HD * (h + 1)],
                                   v=[VA[:, b, :, HD * h:HD * (h + 1)] for b in range(NT)]))

        def ffn_pe(pe, f, n, T_in, T_out, turn=None):
            def pair(T, p, cols=slice(0, S)):
                w_hi, w_lo = stationary(T)
                for c in range(2):
                    for k in range(NC):
                        last = three(ps[:, 4 + 2 * p + c, cols], w_hi[:, c, k, :], w_lo[:, c, k, :],
                                     hTh[:, k, cols], hTl[:, k, cols], k == 0, k == NC - 1)
                return last

            if turn is None:
                first = 0
            else:
                first, early = 1, slice(0, (NT - 1) * P)
                pe.wait_ge(gated, FC * f + 2)
                pe.wait_ge(tl_done, NT * turn + NT - 1)
                for p in range(2):
                    pe.wait_ge(lo_ready, T_in + p + 1)
                    pair(T_in + p, p, early)
                pe.wait_ge(tl_done, NT * turn + NT)
                for p in range(2):
                    pair(T_in + p, p, slice((NT - 1) * P, S)).then_inc(w_used, 1)
            with pe.Fori(first, FC // 2) as i:
                for p in range(2):
                    pe.wait_ge(lo_ready, T_in + p + 1 + i * 2)
                    pe.wait_ge(gated, FC * f + p + 1 + i * 2)
                    pair(T_in + p, p).then_inc(w_used, 1)

            def ready(t):
                if t == 2:
                    pe.wait_ge(actl_done, FC * f + 4)
                elif t == 0:
                    pe.wait_ge(gated, FC * (f + 1) + 2)
                elif t is None:
                    pe.wait_ge(actl_done, FC * (f + 1))

            end_pe(pe, n, T_out, FC, acth, actl, [2, 3, 0, 1], ready)

        def ffn_act(act, f, T_in, T_out):
            with act.Fori(0, FC // 2) as i:
                for p in range(2):
                    act.wait_ge(w_used, T_in + p + 1 + i * 2)
                    nc.scalar.activation(sil[:, p, :], ps[:, 4 + 2 * p, :], ACT.Silu).then_inc(silu_done, 1)
                    hi_part(act, T_in + p + 2, i)
                    act.wait_ge(gated, FC * f + p + 3 + i * 2)
                    nc.scalar.copy(acth[:, bass.ds(i * 2 + p, 1), :].rearrange("p a n -> p (a n)"), afull[:, p, :]
                                   ).then_inc(acth_done, 1)
            for T in range(T_out + 2, T_out + 11):
                hi_part(act, T)

        def ffn_dve(dve, f, T_in, T_out):
            with dve.Fori(0, FC // 2) as i:
                for p in range(2):
                    dve.wait_ge(silu_done, FC * f + p + 1 + i * 2)
                    nc.vector.tensor_tensor(afull[:, p, :], sil[:, p, :], ps[:, 5 + 2 * p, :], ALU.mult
                                            ).then_inc(gated, 1)
                    lo_part(dve, T_in + p + 2, i)
                    dve.wait_ge(acth_done, FC * f + p + 1 + i * 2)
                    j = bass.ds(i * 2 + p, 1)
                    nc.vector.tensor_tensor(actl[:, j, :].rearrange("p a n -> p (a n)"), afull[:, p, :],
                                            acth[:, j, :].rearrange("p a n -> p (a n)").bitcast(F32),
                                            ALU.subtract).then_inc(actl_done, 1)
            for T in range(T_out + 2, T_out + 11):
                lo_part(dve, T)

        def seg(t, d):
            wf = (t + 1) * P
            return (slice(0, wf), slice(0, wf)) if d == 0 else (slice(wf, 640), slice(t * P, S))

        ROW = [(B2_QK, 4), (B2_QK + 2, 0), (B2_ROW, 4), (B2_ROW + 2, 0), (B2_ROW + 4, 4)]

        with layers() as (layer, block):
            one = lambda name: a[name][bass.ds(layer, 1)]

            def gains(eng, n):
                eng.dma_start(gbc[:], a["post_gain"][bass.ds(layer * 3 + (n + 2), 1)].to_broadcast([P, D])
                              ).then_inc(gain_in, 16)
                eng.dma_start(grow[:], a["next_gain"][bass.ds(layer * 3 + (n + 3), 1)].to_broadcast([P, D])
                              ).then_inc(gain_in, 16)

            @block.sync
            def _(sp):
                sp.dma_start(gate_raw[:].rearrange("p a c -> p (a c)"), one("w_gate").rearrange("a p c -> (a p) c")
                             ).then_inc(par2, 16)
                sp.dma_start(gate_bias[:], one("gate_bias").to_broadcast([P, 16])).then_inc(par2, 16)
                sp.dma_start(conv_w[:].rearrange("p a c -> p (a c)"), one("conv_w").rearrange("a p c -> (a p) c")
                             ).then_inc(par2, 16)
                sp.dma_start(conv_b[:], one("conv_b").rearrange("a p c -> (a p) c")).then_inc(par2, 16)
                sp.dma_start(rot_cos[:], a["rot_cos"]).then_inc(par2, 16)
                sp.dma_start(rot_sin[:], a["rot_sin"]).then_inc(par2, 16)
                sp.dma_start(upto[:], a["upto"]).then_inc(par2, 16)
                gains(sp, 0)
                stream(sp, layer * B2_TILES + DEPTH * B1_TILES, B2_TILES)
                for t in range(NT):
                    sp.wait_ge(x_done, 2 * NT + t + 1)
                    sp.dma_start(a["out"][0, t * P:(t + 1) * P, :], X[:, t, :]).then_inc(io, 16)
                sp.wait_ge(io, 16 * NT)

            @block.tensor
            def _(pe):
                ffn_pe(pe, 0, 0, B2_IN1, B2_OUT1)
                project_pe(pe, ROW[0][0], 0, ROW[0][1], turn=0)
                pe.wait_ge(mw_done, 1)
                for t in range(NT):
                    for k in range(NC):
                        last = three(ps[:, 3, 16 * t:16 * (t + 1)], hTh[:, k, t * P:(t + 1) * P],
                                     hTl[:, k, t * P:(t + 1) * P], gate_hi[:, k, :], gate_lo[:, k, :],
                                     k == 0, k == NC - 1)
                last.then_inc(sm_t, 1)
                project_pe(pe, ROW[1][0], 1, ROW[1][1],
                           last_bank=lambda: pe.wait_ge(g_v, 1))
                for c in range(8):
                    T = B2_CONV + c // 2
                    if c % 4 == 0:
                        pe.wait_ge(ev_a, 2 * (c // 4 + 1))
                        pe.wait_ge(ev_v, 2 * (c // 4 + 1))
                    w_hi, w_lo = stationary(T)
                    pe.wait_ge(lo_ready, T + 1)
                    for k in range(NC):
                        last = three(ps[:, (c + 4) % 8, :], w_hi[:, c % 2, k, :], w_lo[:, c % 2, k, :], hTh[:, k, :],
                                     hTl[:, k, :], k == 0, k == NC - 1)
                    last.then_inc(w_used if c % 2 else cs_mm, 1)
                for b in (2, 3, 4):
                    if b == 4:
                        pe.wait_ge(ev_v, 8)
                    else:
                        pe.wait_ge(pad_done, 4 * (b - 1))
                    project_pe(pe, ROW[b][0], b, ROW[b][1])
                pe.wait_ge(ev_v, 12)
                pe.wait_ge(g_v, 3)
                for t in range(NT):
                    for d in range(2):
                        others = range(t) if d == 0 else range(t + 1, NT)
                        out = ps[:, 0, 8 * t + 4 * d:8 * t + 4 * d + 4]
                        last = nc.tensor.matmul(out, upto[:, d, :], logf[:, t, d, :], start=True, stop=not len(others))
                        for o in others:
                            last = nc.tensor.matmul(out, ones[:].to_broadcast([P, P]), logf[:, o, d, :],
                                                    start=False, stop=o == others[-1])
                last.then_inc(sm_t, 1)
                pe.wait_ge(g_v, 4)
                pe.wait_ge(q_ready, NT)
                for c in range(8):
                    if c == 4:
                        pe.wait_ge(ev_a, 16)
                    for t in range(NT):
                        last = nc.tensor.transpose(ps[:, c, t * P:(t + 1) * P], P2[:, t, c * P:(c + 1) * P], ident[:])
                    last.then_inc(qt_done, 1)
                pe.wait_ge(qte_v, 8)
                attend_pe(pe, units2, buf2, lambda: pe.wait_ge(ev_v, 12), filler2)
                pe.wait_ge(o_done, len(units2))
                for t in range(NT):
                    last = nc.tensor.transpose(ps[0:8, 0, t * P:(t + 1) * P],
                                               acol[:, t, :, :].rearrange("p d h -> p (d h)"), ident[:])
                last.then_inc(sm_t, 1)
                pe.wait_ge(al_done, 1)
                for r in range(8):
                    row = identr[0:8, r:r + 1].to_broadcast([8, P])
                    nc.tensor.matmul(ps[:, r, :], row, aTh[0:8, :], start=True, stop=False)
                    nc.tensor.matmul(ps[:, r, :], row, aTl[0:8, :], start=False, stop=True).then_inc(sm_t, 1)
                pe.wait_ge(ab_a, 4)
                pe.wait_ge(ab_v, 4)

                def similar(t):
                    for h in range(MH):
                        if t:
                            pe.wait_ge(m2_done, MH * (t - 1) + h + 1)
                        three(ps[:, h, :], hTl[:, h, t * P:(t + 1) * P], MQKl[:, h, t * P:(t + 1) * P],
                              hTl[:, MH + h, :], MQKl[:, MH + h, :], True, True).then_inc(ms_done, 1)

                def values(t, h):
                    pe.wait_ge(mptl_done, MH * t + h + 1)
                    for b in range(NT):
                        last = three(ps[:, 6 + t % 2, h * P:(h + 1) * P], PT2h[:, h % 2, b, :], PT2l[:, h % 2, b, :],
                                     value_part(3, b, 0)[:, h * P:(h + 1) * P], value_part(3, b, 1)[:, h * P:(h + 1) * P],
                                     start=b == 0, stop=b == NT - 1)
                    if h == MH - 1:
                        last.then_inc(mpv_done, 1)

                pe.wait_ge(vl_done, 8)
                similar(0)
                for t in range(NT):
                    if t + 1 < NT:
                        similar(t + 1)
                    if t >= 2:
                        pe.wait_ge(o_ready, t - 1)
                    for h in range(MH):
                        pe.wait_ge(mg_done, MH * t + h + 1)
                        for b in range(NT):
                            col = b * P if b <= t else (b + 1) * P
                            last = nc.tensor.transpose(ps[:, 4 + h % 2, b * P:(b + 1) * P],
                                                       SW[:, t % 2, h, col:col + P], ident[:])
                        last.then_inc(mt_done, 1)
                        if h:
                            values(t, h - 1)
                    values(t, MH - 1)
                for t in TURN_ORDER:
                    pe.wait_ge(o_ready, NT if y_bank(t) == 6 else t + 1)
                    turn_pe(pe, P2[:, t, 0:D], t)
                end_pe(pe, 1, B2_MIXOUT, NC, hTh, hTl, TURN_ORDER,
                       lambda t: t is not None and pe.wait_ge(tl_done, NT + TURN_ORDER.index(t) + 1))
                ffn_pe(pe, 1, 2, B2_IN2, B2_OUT2, turn=2)

            @block.scalar
            def _(act):
                act.sem_inc(hi_ready, 2)
                act.wait_ge(par2, par2_all)
                nc.scalar.copy(gate_hi[:], gate_raw[:]).then_inc(mr_done, 1)
                ffn_act(act, 0, B2_IN1, B2_OUT1)
                end_act(act, 0, 0, B2_OUT1 + 11)
                act.dma_start(BM[:], a["group_bias"]).then_inc(mixpar, 16)
                act.dma_start(masks[:], a["causal"]).then_inc(mixpar, 16)
                act.dma_start(mgain[:], one("mlstm_gain").to_broadcast([P, S])).then_inc(mixpar, 16)

                def evacuate(b):
                    T0, bank = ROW[b]
                    for t in (0, 2):
                        projected(act, T0, b, t)
                        nc.scalar.copy(P2[:, t, 512 * b:512 * (b + 1)], ps[:, bank + t, :]).then_inc(ev_a, 1)

                def conv_silu(c):
                    act.wait_ge(cv_done, c + 1)
                    nc.scalar.activation(MQK[:, c, :], acc[:, c % 2, :], ACT.Silu, bias=conv_b[:, c:c + 1]
                                         ).then_inc(cs_done, 1)

                for b in (0, 1):
                    hi_part(act, ROW[b][0] + 2)
                    if b == 0:
                        act.wait_ge(g_v, 2)
                        nc.scalar.activation(gexp[:], gtmp[:], ACT.Exp).then_inc(g_a, 1)
                        act.wait_ge(g_a, 1)
                        nc.scalar.activation(gexp[:], gexp[:], ACT.Ln, bias=1.0).then_inc(g_a, 1)
                    evacuate(b)
                    hi_part(act, ROW[b][0] + 3)
                act.wait_ge(g_p, 1)
                for c in range(8):
                    T = B2_CONV + c // 2
                    if c % 2:
                        hi_part(act, T + 2)
                        act.wait_ge(w_used, T + 1)
                    else:
                        act.wait_ge(cs_mm, c // 2 + 1)
                    if c >= 2:
                        act.wait_ge(cv_done, c - 1)
                    nc.scalar.copy(pad[:, c % 2, 2:S + 2], ps[:, (c + 4) % 8, :]).then_inc(pad_done, 1)
                    if c:
                        conv_silu(c - 1)
                conv_silu(7)
                for b in (2, 3, 4):
                    hi_part(act, ROW[b][0] + 2)
                    if b < 4:
                        for t in range(NT):
                            projected(act, ROW[b][0], b, t)
                            nc.scalar.copy(value_part(b, t, 0), ps[:, ROW[b][1] + t, :]).then_inc(ev_a, 1)
                    else:
                        for t in range(NT):
                            projected(act, ROW[b][0], b, t)
                            nc.scalar.activation(P2[:, t, 512 * b:512 * (b + 1)], ps[:, ROW[b][1] + t, :],
                                                 ACT.Sigmoid).then_inc(ev_a, 1)
                    hi_part(act, ROW[b][0] + 3)
                for c in range(8):
                    act.wait_ge(qt_done, c + 1)
                    nc.scalar.activation(hTh[:, c, :], ps[:, c, :], ACT.Copy, scale=0.125 if c < 4 else 1.0
                                         ).then_inc(qte_a, 1)
                attend_act(act, units2, buf2)
                act.wait_ge(sm_t, 3)
                nc.scalar.copy(identr[:], ident[:])
                nc.scalar.copy(aTh[0:8, :], ps[0:8, 0, :]).then_inc(sm_e, 1)
                for c in (0, 4, 1, 5, 2, 6, 3, 7):
                    nc.scalar.copy(hTl[:, c, :], MQK[:, c, :]).then_inc(vh_done, 1)
                for r in range(0, 8, 2):
                    act.wait_ge(sm_t, 3 + r + 1)
                    nc.scalar.copy(AB[:, r, :], ps[:, r, :]).then_inc(ab_a, 1)

                def weights(t):
                    act.wait_ge(m1_done, t + 1)
                    for h in range(MH):
                        for d in range(2):
                            w = SW[:, t % 2, h, seg(t, d)[0]]
                            nc.scalar.activation(w, w, ACT.Exp, bias=nmmax[:, t, d, h:h + 1])
                    nc.scalar.activation(mexp[:, t, :, :], dtmp[:, t, :, :], ACT.Exp).then_inc(mw2_done, 1)

                def cell_squares(t):
                    act.wait_ge(mpv_done, t + 1)
                    for h in range(MH):
                        last = nc.scalar.activation(junk_head[:, h, :], ps[:, 6 + t % 2, h * P:(h + 1) * P], ACT.Square,
                                                    accum_out=osum[:, t, h:h + 1])
                    last.then_inc(g_a, 1)

                weights(0)
                weights(1)
                for t in range(NT):
                    for h in range(MH):
                        act.wait_ge(mt_done, MH * t + h + 1)
                        nc.scalar.copy(PT2h[:, h % 2, :, :].rearrange("p b n -> p (b n)"), ps[:, 4 + h % 2, :]
                                       ).then_inc(mpt_done, 1)
                    if t + 2 < NT:
                        weights(t + 2)
                    cell_squares(t)
                for pos, t in enumerate(TURN_ORDER):
                    turn_act(act, 1, t, pos)
                gains(act, 1)
                hi_part(act, B2_MIXOUT + 2)
                hi_part(act, B2_MIXOUT + 3)
                end_act(act, 1, 2, B2_MIXOUT + 4)
                gains(act, 2)
                ffn_act(act, 1, B2_IN2, B2_OUT2)
                end_act(act, 2, 3, B2_TILES)

            @block.vector
            def _(dve):
                chain = Chain(dve, dchain)
                nc.vector.memset(ones[:], 1.0).then_inc(one_done, 1)
                dve.sem_inc(lo_ready, 2)
                dve.sem_inc(gated, 2)
                dve.wait_ge(mr_done, 1)
                nc.vector.tensor_tensor(gate_lo[:], gate_raw[:], gate_hi[:].bitcast(F32), ALU.subtract
                                        ).then_inc(mw_done, 1)
                ffn_dve(dve, 0, B2_IN1, B2_OUT1)
                end_dve(dve, chain, 0, 0, B2_OUT1 + 11)
                dve.wait_ge(sm_t, 1)
                nc.vector.tensor_tensor(gates[:].rearrange("p t d g h -> p t (d g h)"),
                                        ps[:, 3, 0:64].rearrange("p (t g) -> p t g", t=NT),
                                        gate_bias[:].unsqueeze(1).to_broadcast([P, NT, 16]), ALU.add).then_inc(g_v, 1)
                dve.wait_ge(g_v, 1)
                f = gates[:, :, :, 1, :]
                chain(nc.vector.tensor_scalar(gtmp[:], f, -1.0, None, ALU.mult))
                nc.vector.tensor_tensor(gtmp[:], gtmp[:], f, ALU.min).then_inc(g_v, 1)

                def evacuate(b):
                    T0, bank = ROW[b]
                    for t in (1, 3):
                        projected(dve, T0, b, t)
                        nc.vector.tensor_copy(P2[:, t, 512 * b:512 * (b + 1)], ps[:, bank + t, :]).then_inc(ev_v, 1)

                def rotary(t):
                    x = P2[:, t, 0:1024].rearrange("p (n d) -> p n d", d=HD)
                    x1, x2 = x[:, :, 0:8], x[:, :, 8:16]
                    c3 = rot_cos[:, t, :].unsqueeze(1).to_broadcast([P, 16, 8])
                    s3 = rot_sin[:, t, :].unsqueeze(1).to_broadcast([P, 16, 8])
                    A, B, C = (rt[:, t % 2, j, :].rearrange("p (n d) -> p n d", d=8) for j in range(3))
                    nc.vector.tensor_tensor(A, x1, s3, ALU.mult)
                    nc.vector.tensor_tensor(B, x2, s3, ALU.mult)
                    chain(nc.vector.tensor_tensor(C, x2, c3, ALU.mult))
                    chain(nc.vector.tensor_tensor(x1, x1, c3, ALU.mult))
                    nc.vector.tensor_tensor(x2, C, A, ALU.add)
                    nc.vector.tensor_tensor(x1, x1, B, ALU.subtract).then_inc(q_ready, 1)

                def convolve(c):
                    dve.wait_ge(pad_done, c + 1)
                    if c >= 2:
                        dve.wait_ge(cs_done, c - 1)
                    o, x = acc[:, c % 2, :], pad[:, c % 2, :]
                    chain(nc.vector.tensor_scalar(o, x[:, 0:S], conv_w[:, c, 0:1], None, ALU.mult))
                    for w in range(1, CONV):
                        ins = nc.vector.scalar_tensor_tensor(o, x[:, w:w + S], conv_w[:, c, w:w + 1], o,
                                                             ALU.mult, ALU.add)
                        if w < CONV - 1:
                            chain(ins)
                    ins.then_inc(cv_done, 1)

                dve.wait_ge(par2, par2_all)
                for b in (0, 1):
                    lo_part(dve, ROW[b][0] + 2)
                    if b == 0:
                        dve.wait_ge(g_a, 2)
                        nc.vector.scalar_tensor_tensor(logf[:], f, 0.0, gexp[:], ALU.min, ALU.subtract
                                                       ).then_inc(g_v, 1)
                    evacuate(b)
                    lo_part(dve, ROW[b][0] + 3)
                for c in range(8):
                    if c % 2:
                        lo_part(dve, B2_CONV + c // 2 + 2)
                    convolve(c)
                for b in (2, 3, 4):
                    lo_part(dve, ROW[b][0] + 2)
                    if b < 4:
                        for t in range(NT):
                            dve.wait_ge(ev_a, 4 * (b - 1) + t + 1)
                            nc.vector.tensor_tensor(value_part(b, t, 1), ps[:, ROW[b][1] + t, :],
                                                    value_part(b, t, 0).bitcast(F32), ALU.subtract
                                                    ).then_inc(ev_v, 1)
                    if b == 2:
                        dve.wait_ge(ev_a, 4)
                        dve.wait_ge(ev_v, 4)
                        for t in range(NT):
                            rotary(t)
                    lo_part(dve, ROW[b][0] + 3)
                dve.wait_ge(sm_t, 2)
                nc.vector.tensor_copy(cum[:].rearrange("p t d h -> p (t d h)"), ps[:, 0, 0:32]).then_inc(g_v, 1)
                dve.wait_ge(g_v, 4)
                chain(nc.vector.tensor_tensor(acol[:], gates[:, :, :, 0, :], cum[:], ALU.subtract))
                for c in range(8):
                    dve.wait_ge(qte_a, c + 1)
                    nc.vector.scalar_tensor_tensor(hTl[:, c, :], ps[:, c, :], 0.125 if c < 4 else 1.0,
                                                   hTh[:, c, :].bitcast(F32), ALU.mult, ALU.subtract
                                                   ).then_inc(qte_v, 1)
                dve.wait_ge(mixpar, 48)
                dve.wait_ge(g_p, 2)
                attend_dve(dve, chain, units2, buf2)
                dve.wait_ge(sm_e, 1)
                nc.vector.tensor_tensor(aTl[0:8, :], ps[0:8, 0, :], aTh[0:8, :].bitcast(F32), ALU.subtract
                                        ).then_inc(al_done, 1)
                for i, c in enumerate((0, 4, 1, 5, 2, 6, 3, 7)):
                    dve.wait_ge(vh_done, i + 1)
                    nc.vector.tensor_tensor(MQKl[:, c, :], MQK[:, c, :], hTl[:, c, :].bitcast(F32), ALU.subtract
                                            ).then_inc(vl_done, 1)
                for r in range(1, 8, 2):
                    dve.wait_ge(sm_t, 3 + r + 1)
                    nc.vector.tensor_copy(AB[:, r, :], ps[:, r, :]).then_inc(ab_v, 1)
                dve.wait_ge(ab_a, 4)
                dve.wait_ge(ab_v, 4)

                def decay(t):
                    for h in range(MH):
                        for d in range(2):
                            dst, src = seg(t, d)
                            mask = masks[:, 0, 384 - P * t:S] if d == 0 else masks[:, 1, 0:S - P * t]
                            last = nc.vector.tensor_tensor_reduce(
                                out=SW[:, t % 2, h, dst], in0=AB[:, MH * d + h, src], in1=mask, scale=1.0,
                                scalar=-3.0e38, op0=ALU.add, op1=ALU.max, accum_out=mmax[:, t, d, h:h + 1])
                    chain(last)
                    chain(nc.vector.tensor_scalar(nmmax[:, t, :, :], mmax[:, t, :, :], -1.0, None, ALU.mult))
                    nc.vector.tensor_tensor(dtmp[:, t, :, :], nmmax[:, t, :, :], cum[:, t, :, :], ALU.subtract
                                            ).then_inc(m1_done, 1)

                def weigh(t):
                    dve.wait_ge(mw2_done, t + 1)
                    for h in range(MH):
                        dve.wait_ge(ms_done, MH * t + h + 1)
                        for d in range(2):
                            dst, src = seg(t, d)
                            w = SW[:, t % 2, h, dst]
                            last = nc.vector.tensor_tensor_reduce(
                                out=w, in0=ps[:, h, src], in1=w, scale=P ** -0.5, scalar=0.0,
                                op0=ALU.mult, op1=ALU.add, accum_out=den[:, t, d, h:h + 1])
                        last.then_inc(m2_done, 1)
                    dve.wait_ge(m2_done, MH * (t + 1))
                    chain(nc.vector.tensor_scalar(drec[:, t, :, :], den[:, t, :, :], -1.0, None, ALU.mult))
                    chain(nc.vector.tensor_tensor(drec[:, t, :, :], drec[:, t, :, :], den[:, t, :, :], ALU.max))
                    chain(nc.vector.tensor_tensor(drec[:, t, :, :], drec[:, t, :, :], mexp[:, t, :, :], ALU.max))
                    chain(nc.vector.reciprocal(drec[:, t, :, :], drec[:, t, :, :]))
                    for h in range(MH):
                        for d in range(2):
                            w = SW[:, t % 2, h, seg(t, d)[0]]
                            last = nc.vector.tensor_scalar(w, w, drec[:, t, d, h:h + 1], None, ALU.mult)
                        chain(last)
                        w = SW[:, t % 2, h, :]
                        nc.vector.tensor_tensor(w[:, t * P:(t + 1) * P], w[:, t * P:(t + 1) * P],
                                                w[:, (t + 1) * P:(t + 2) * P], ALU.add).then_inc(mg_done, 1)
                        if h >= 2:
                            low(t, h - 2)

                def low(t, h):
                    dve.wait_ge(mpt_done, MH * t + h + 1)
                    nc.vector.tensor_tensor(PT2l[:, h % 2, :, :].rearrange("p b n -> p (b n)"), ps[:, 4 + h % 2, :],
                                            PT2h[:, h % 2, :, :].rearrange("p b n -> p (b n)").bitcast(F32),
                                            ALU.subtract).then_inc(mptl_done, 1)

                def cell(t):
                    dve.wait_ge(g_p, 2 + t + 1)
                    for h in range(MH):
                        o = 512 + h * P
                        last = nc.vector.scalar_tensor_tensor(
                            P2[:, t, o:o + P], ps[:, 6 + t % 2, h * P:(h + 1) * P], oinv[:, t, h:h + 1],
                            P2[:, t, 1536 + o:1536 + o + P], ALU.mult, ALU.mult)
                    last.then_inc(o_ready, 1)

                decay(0)
                decay(1)
                for t in range(NT):
                    weigh(t)
                    if t:
                        cell(t - 1)
                    low(t, 2)
                    low(t, 3)
                    if t + 2 < NT:
                        dve.wait_ge(mt_done, MH * (t + 1))
                        decay(t + 2)
                cell(NT - 1)
                for pos, t in enumerate(TURN_ORDER):
                    turn_dve(dve, 1, t, pos)
                lo_part(dve, B2_MIXOUT + 2)
                lo_part(dve, B2_MIXOUT + 3)
                end_dve(dve, chain, 1, 2, B2_MIXOUT + 4)
                ffn_dve(dve, 1, B2_IN2, B2_OUT2)
                end_dve(dve, chain, 2, 3, B2_TILES)

            @block.gpsimd
            def _(pool):
                chain = Chain(pool, pchain)
                end_pool(pool, chain, 0, 0.5)
                pool.wait_ge(xn_done, NT)
                nc.gpsimd.memset(pad[:, :, 0:2], 0.0)
                nc.gpsimd.memset(pad[:, :, S + 2:S + 4], 0.0).then_inc(g_p, 1)
                pool.wait_ge(mixpar, 48)
                pool.wait_ge(ev_a, 16)
                for t in range(NT):
                    last = nc.gpsimd.tensor_tensor(P2[:, t, 2048:2560], P2[:, t, 2048:2560], mgain[:], ALU.mult)
                last.then_inc(g_p, 1)
                for t in range(NT):
                    pool.wait_ge(g_a, 2 + t + 1)
                    chain(nc.gpsimd.tensor_scalar(osum[:, t, 0:MH], osum[:, t, 0:MH], 1.0 / P, EPS,
                                                  ALU.mult, ALU.add))
                    nc.gpsimd.tensor_tensor(oinv[:, t, 0:MH], osum[:, t, 0:MH], halfneg[:].to_broadcast([P, MH]),
                                            ALU.pow).then_inc(g_p, 1)
                end_pool(pool, chain, 1, 1.0)
                end_pool(pool, chain, 2, 0.5)
    return nc


def moving_tiles(w):
    L, K, N = w.shape
    b = w.reshape(L, K // P, P, N // 512, 512).transpose(0, 3, 1, 2, 4).reshape(L, -1, 4, P, 512)
    return b.transpose(0, 1, 3, 2, 4).reshape(L, -1, P, TILE)


def stationary_tiles(w):
    L, _, n, _ = w.shape
    return w.reshape(L, NC, P, n // 2, 2, P).transpose(0, 3, 2, 4, 1, 5).reshape(L, n // 2, P, TILE)


def rope_tables(pos, dim, theta):
    inv = (np.float32(theta) ** (-np.arange(0, dim, 2, dtype=np.float32) / np.float32(dim))).astype(np.float32)
    ang = pos.astype(np.float32)[:, None] * inv[None, :]
    return np.cos(ang).astype(np.float32), np.sin(ang).astype(np.float32)


def by_token(t):
    return np.ascontiguousarray(np.moveaxis(t.reshape(NT, P, *t.shape[1:]), 0, 1))


def constants():
    pos = np.arange(S)
    c = {"identity": np.eye(P, dtype=np.float32)}
    cos, sin = rope_tables(pos, 32, 10000.0)
    c["lin_cos"], c["lin_sin"] = by_token(cos), by_token(sin)
    rc, rs = rope_tables(pos // 64, 32, 10000.0)
    cc, cs = rope_tables(pos % 64, 32, 10000.0)
    c["ax_cos"], c["ax_sin"] = by_token(np.stack([rc, cc], 1)), by_token(np.stack([rs, cs], 1))
    cos, sin = rope_tables(pos, 16, 500000.0)
    c["rot_cos"], c["rot_sin"] = by_token(cos), by_token(sin)
    gap = np.abs(pos[:, None] - pos[None, :])
    count = sum(((gap % dil == 0) & (gap // dil <= 64)).astype(np.int64) for dil in (1, 4, 16))
    bias = np.where(count > 0, np.log(np.maximum(count, 1)), NEG).astype(np.float32)
    c["group_bias"] = by_token(bias)
    p, s = np.arange(P)[:, None], np.arange(P)[None, :]
    zero = np.zeros((P, 384), np.float32)
    c["causal"] = np.stack([np.concatenate([zero, np.where(s <= p, 0, NEG).astype(np.float32)], 1),
                            np.concatenate([np.where(s >= p, 0, NEG).astype(np.float32), zero], 1)], 1)
    c["upto"] = np.stack([(p <= s).astype(np.float32), (p >= s).astype(np.float32)], 1)
    li = [0.8 - 0.6 * math.exp(-0.3 * l) for l in range(DEPTH)]
    c["lambda_init"] = np.array([[v, 1.0 - v] for v in li], np.float32)
    return c


def lay_out(x, mem, pre_norm, w_in, diff_lambda, diff_subln, gqa_q_norm, gqa_k_norm, mem_norm, w_mem_kv,
            w_out, post_norm, norm_gain_2, ffn_w_in_2, ffn_w_out_2, mix_w_in_2, conv_w_2, conv_b_2,
            gate_bias_2, mlstm_norm_gain_2, mix_w_out_2):
    L = DEPTH
    cut = lambda w, lo, hi: w[:, :, lo:hi]
    gq = cut(w_in, 1536, 1920).reshape(L, D, 2, 3, HD).transpose(0, 1, 3, 2, 4).reshape(L, D, 384)
    proj = np.concatenate([cut(w_in, 0, 768), gq, cut(w_in, 1920, 2048), cut(w_in, 2560, 2816),
                           cut(w_in, 768, 1152), cut(w_in, 2048, 2176), cut(w_in, 1152, 1536),
                           cut(w_in, 2176, 2560), cut(w_in, 2816, 3072)], 2)
    mem_v = cut(w_mem_kv, 256, 512).reshape(L, NC, P, 256).transpose(0, 2, 1, 3).reshape(L, 1, P, TILE)
    w1 = np.concatenate([moving_tiles(proj), stationary_tiles(cut(w_mem_kv, 0, 256).reshape(L, D, 2, P)), mem_v,
                         moving_tiles(w_out)], 1)

    def ffn(i):
        w = ffn_w_in_2[:, i].reshape(L, D, 2, FC, P).transpose(0, 1, 3, 2, 4).reshape(L, D, 2 * FC, P)
        return [stationary_tiles(w), moving_tiles(ffn_w_out_2[:, i])]

    m = mix_w_in_2
    w2 = np.concatenate(ffn(0) + [moving_tiles(cut(m, 0, 1024)),
                                  stationary_tiles(cut(m, 1536, 2560).reshape(L, D, 8, P)),
                                  moving_tiles(np.concatenate([cut(m, 1024, 1536), cut(m, 2560, 3584)], 2)),
                                  moving_tiles(mix_w_out_2)] + ffn(1), 1)
    weights = np.concatenate([w1.reshape(-1, P, TILE), w2.reshape(-1, P, TILE), np.zeros((2, P, TILE), np.float32)])
    g = norm_gain_2
    pre = [g[:, i:i + 1] for i in (0, 2, 4)]
    post = [g[:, i:i + 1] for i in (1, 3, 5)]
    arrays = {
        "x": x, "mem": mem, "weights": weights, "mem_norm": mem_norm.reshape(L, NC, P).transpose(0, 2, 1),
        "next_gain": np.concatenate([pre_norm, np.concatenate(pre, 1).reshape(-1, D), np.zeros((1, D), np.float32)]),
        "post_gain": np.concatenate([post_norm, np.concatenate(post, 1).reshape(-1, D)]),
        "diff_lambda": diff_lambda.reshape(L, 128), "diff_subln": diff_subln,
        "gqa_q_norm": gqa_q_norm, "gqa_k_norm": gqa_k_norm,
        "w_gate": cut(m, 3584, 3600).reshape(L, NC, P, 16).transpose(0, 2, 1, 3).reshape(L, P, 128),
        "gate_bias": gate_bias_2.reshape(L, 16),
        "conv_w": conv_w_2.reshape(L, CONV, 8, P).transpose(0, 3, 2, 1).reshape(L, P, 40),
        "conv_b": conv_b_2.reshape(L, 8, P).transpose(0, 2, 1),
        "mlstm_gain": mlstm_norm_gain_2,
    }
    return {k: np.ascontiguousarray(v) for k, v in {**arrays, **constants()}.items()}


def kernel(**inputs):
    import concourse.bacc as bacc
    from concourse.bass_utils import run_bass_kernel_spmd

    arrays = lay_out(**{k: np.asarray(v) for k, v in inputs.items()})
    nc = bacc.Bacc("TRN2", target_bir_lowering=False, num_devices=1)
    aps = {k: nc.dram_tensor(f"in_{k}", v.shape, F32, kind="ExternalInput").ap() for k, v in arrays.items()}
    aps["out"] = nc.dram_tensor("out", (1, S, D), F32, kind="ExternalOutput").ap()
    build(nc, aps)
    r = run_bass_kernel_spmd(nc, [{f"in_{k}": v for k, v in arrays.items()}], core_ids=[0])
    return r.results[0]["out"]
```

```python
import math
from contextlib import ExitStack, contextmanager

import numpy as np

import concourse.bass as bass
from concourse import mybir

F32 = mybir.dt.float32
F32R = mybir.dt.float32r
BF16 = mybir.dt.bfloat16
ALU = mybir.AluOpType
ACT = mybir.ActivationFunctionType
AX = mybir.AxisListType

P = 128
S = 512
D = 1024
NT = S // P
NC = D // P
DEPTH = 2
EPS = 1e-6
TILE = 2048
HD = 64
N_DIFF, N_GQA, N_MEMH = 6, 6, 4
N_MEM = 256
FC = 22
MH = 4
CONV = 5
NEG = -1e30

B1_PROJ, B1_KV, B1_OUT, B1_TILES = 0, 12, 14, 18
B2_IN1, B2_OUT1, B2_QK, B2_CONV, B2_ROW, B2_MIXOUT, B2_IN2, B2_OUT2, B2_TILES = 0, 22, 33, 37, 41, 47, 51, 73, 84

AT_X = 16512
AT_HH = AT_X + 16384
AT_HL = AT_HH + 16384
AT_RAW = AT_HL + 16384
AT_WHI = AT_RAW + 16384
AT_WLO = AT_WHI + 16384
AT_GBC = AT_WLO + 16384
AT_SMALL = AT_GBC + 4096
AT_R = AT_SMALL + 8000
END = 229344


class Chain:

    def __init__(self, eng, sem):
        self.eng, self.sem, self.n = eng, sem, 0

    def __call__(self, ins):
        ins.then_inc(self.sem, 1)
        self.n += 1
        self.eng.wait_ge(self.sem, self.n)


def build(nc, a):
    with ExitStack() as ctx:
        def at(name, shape, offset, dt=F32):
            size = int(np.prod(shape[1:])) * (2 if dt == BF16 else 4)
            assert offset % 32 == 0 and offset + size <= END, (name, offset + size)
            return nc.alloc_sbuf_tensor_at(name, shape, dt, offset=offset)

        X = at("X", [P, NT, D], AT_X)
        hTh = at("hTh", [P, NC, S], AT_HH, F32R)
        hTl = at("hTl", [P, NC, S], AT_HL, F32R)
        raw = at("raw", [P, 2, TILE], AT_RAW)
        whi = at("whi", [P, 2, TILE], AT_WHI, F32R)
        wlo = at("wlo", [P, 2, TILE], AT_WLO, F32R)
        gbc = at("gbc", [P, D], AT_GBC)

        small_at = [AT_SMALL]

        def small(name, shape, dt=F32):
            t = at(name, shape, small_at[0], dt)
            small_at[0] += -(-int(np.prod(shape[1:])) * (2 if dt == BF16 else 4) // 32) * 32
            assert small_at[0] <= AT_R, name
            return t

        ident = small("ident", [P, P])
        junk_mem = at("junk_mem", [P, 2, D], AT_R + 77824)
        junk = small("junk", [P, D], BF16)
        halfneg = small("halfneg", [P, 1])
        gcol = small("gcol", [P, NC])
        sums = small("sums", [P, 4 * NT])
        rinv = small("rinv", [P, 4 * NT])
        ysum = small("ysum", [P, 3 * NT])
        yinv = small("yinv", [P, 3 * NT])
        negmax = small("negmax", [P, 2, 2])
        rowmax = small("rowmax", [P, 2, 1])
        esum = small("esum", [P, 2, 2])
        erec = small("erec", [P, 8, 2])
        otmp = small("otmp", [P, 2, HD])
        lamc = small("lamc", [P, 2])
        lam = small("lam", [P, 8])
        hsum = small("hsum", [P, NT, 8])
        hinv = small("hinv", [P, NT, 8])
        oinv = small("oinv", [P, NT, 8])
        osum = small("osum", [P, NT, 8])
        gate_bias = small("gate_bias", [P, 16])
        gates = small("gates", [P, NT, 2, 2, MH])
        gtmp = small("gtmp", [P, NT, 2, MH])
        gexp = small("gexp", [P, NT, 2, MH])
        logf = small("logf", [P, NT, 2, MH])
        cum = small("cum", [P, NT, 2, MH])
        acol = small("acol", [P, NT, 2, MH])
        mmax = small("mmax", [P, NT, 2, MH])
        nmmax = small("nmmax", [P, NT, 2, MH])
        mexp = small("mexp", [P, NT, 2, MH])
        den = small("den", [P, NT, 2, MH])
        dtmp = small("dtmp", [P, NT, 2, MH])
        drec = small("drec", [P, NT, 2, MH])
        gate_raw = small("gate_raw", [P, NC, 16])
        gate_hi = small("gate_hi", [P, NC, 16], F32R)
        gate_lo = small("gate_lo", [P, NC, 16], F32R)
        ones = small("ones", [P, 1])
        conv_w = small("conv_w", [P, 8, CONV])
        conv_b = small("conv_b", [P, 8])
        rot_cos = small("rot_cos", [P, NT, 8])
        rot_sin = small("rot_sin", [P, NT, 8])

        ps = ctx.enter_context(nc.psum_tensor("ps", [P, 8, 512], F32))

        names = []

        def sem(name):
            s = ctx.enter_context(nc.semaphore(name))
            names.append(s)
            return s

        raw_in = [sem("raw_in0"), sem("raw_in1")]
        hi_ready, lo_ready = sem("hi_ready"), sem("lo_ready")
        w_used = sem("w_used")
        par = sem("par")
        par2 = sem("par2")
        gain_in = sem("gain_in")
        sq_done, r_done, xn_done = sem("sq_done"), sem("r_done"), sem("xn_done")
        tr_done, th_done, tl_done = sem("tr_done"), sem("th_done"), sem("tl_done")
        y_done, ysq_done, yr_done, ysc_done, x_done = (sem("y_done"), sem("ysq_done"), sem("yr_done"),
                                                       sem("ysc_done"), sem("x_done"))
        proj_done = sem("proj_done")
        ev_a, ev_v = sem("ev_a"), sem("ev_v")
        x_in = [sem(f"x_in{t}") for t in range(NT)]
        s_done, mx_done, ex_done, t_done, pt_done, ptl_done, pv_done, o_done = (
            sem("s_done"), sem("mx_done"), sem("ex_done"), sem("t_done"),
            sem("pt_done"), sem("ptl_done"), sem("pv_done"), sem("o_done"))
        zero_done, c_done, mix_done = sem("zero_done"), sem("c_done"), sem("mix_done")
        ot_done, sp_done = sem("ot_done"), sem("sp_done")
        vh_done, vl_done = sem("vh_done"), sem("vl_done")
        dchain, pchain, achain = sem("dchain"), sem("pchain"), sem("achain")
        q_ready = sem("q_ready")
        qt_done, qte_a, qte_v = sem("qt_done"), sem("qte_a"), sem("qte_v")
        g_v, g_p, g_a = sem("g_v"), sem("g_p"), sem("g_a")
        o_ready = sem("o_ready")
        io = sem("io")
        gu_done, silu_done, gated, acth_done, actl_done = (sem("gu_done"), sem("silu_done"), sem("gated"),
                                                          sem("acth_done"), sem("actl_done"))
        pad_done, cv_done, cs_done = sem("pad_done"), sem("cv_done"), sem("cs_done")
        m1_done, m2_done, ms_done, mt_done, mpt_done, mptl_done, mg_done, mpv_done = (
            sem("m1_done"), sem("m2_done"), sem("ms_done"), sem("mt_done"), sem("mpt_done"), sem("mptl_done"),
            sem("mg_done"), sem("mpv_done"))
        mw_done, mr_done = sem("mw_done"), sem("mr_done")
        sm_t, sm_e = sem("sm_t"), sem("sm_e")
        al_done, cs_mm, mw2_done, mixpar, ab_a, ab_v, one_done = (sem("al_done"), sem("cs_mm"), sem("mw2_done"), sem("mixpar"), sem("ab_a"),
                                                         sem("ab_v"), sem("one_done"))
        nums = [s.num for s in names]
        assert nums == list(range(nums[0], nums[0] + len(nums)))

        def tile_of(T):
            return a["weights"][bass.ds(T, 1)].rearrange("a p n -> (a p) n")

        def stream(sp, base, tiles):
            with sp.Fori(1, tiles // 2 + 1) as i:
                for slot in range(2):
                    sp.wait_ge(lo_ready, i * 2 + (slot - 1))
                    sp.dma_start(raw[:, slot, :], tile_of(base + i * 2 + slot)).then_inc(raw_in[slot], 16)
            for slot in range(2):
                sp.wait_ge(raw_in[slot], 16 * (tiles // 2 + 1))

        def first_tiles(sp):
            for slot in range(2):
                sp.sem_inc(raw_in[slot], 16)

        def hi_part(act, T, i=0):
            act.wait_ge(raw_in[T % 2], 16 * (T // 2 + 1) + i * 16)
            if T >= 2:
                act.wait_ge(w_used, T - 1 + i * 2)
            nc.scalar.activation(whi[:, T % 2, :], raw[:, T % 2, :], ACT.Copy).then_inc(hi_ready, 1)

        def lo_part(dve, T, i=0):
            dve.wait_ge(hi_ready, T + 1 + i * 2)
            nc.vector.tensor_tensor(wlo[:, T % 2, :], raw[:, T % 2, :], whi[:, T % 2, :].bitcast(F32),
                                    ALU.subtract).then_inc(lo_ready, 1)

        def three(out, l_hi, l_lo, r_hi, r_lo, start, stop):
            nc.tensor.matmul(out, l_hi, r_hi, start=start, stop=False)
            nc.tensor.matmul(out, l_hi, r_lo, start=False, stop=False)
            return nc.tensor.matmul(out, l_lo, r_hi, start=False, stop=stop)

        def moving(T):
            return (whi[:, T % 2, :].rearrange("p (b n) -> p b n", n=512),
                    wlo[:, T % 2, :].rearrange("p (b n) -> p b n", n=512))

        def stationary(T):
            return (whi[:, T % 2, :].rearrange("p (c k n) -> p c k n", c=2, k=NC),
                    wlo[:, T % 2, :].rearrange("p (c k n) -> p c k n", c=2, k=NC))

        XN = at("XN", [P, 2, D], AT_R + 90112)
        grow = at("grow", [P, D], AT_R + 98304)

        def halves(ap):
            return ap.rearrange("p (h n) -> p h n", h=2)

        def y_bank(t):
            return (2 * t + 4) % 8

        def y_of(t):
            return ps[:, y_bank(t):y_bank(t) + 2, :]

        def count(q, pos):
            return NT * q + pos + 3

        def turn_pe(pe, source, t):
            for c in range(NC):
                last = nc.tensor.transpose(ps[:, y_bank(t) + c // 4, (c % 4) * P:(c % 4 + 1) * P],
                                           source[:, c * P:(c + 1) * P], ident[:])
            last.then_inc(tr_done, 1)

        def turned(t):
            return y_of(t).rearrange("p h (c n) -> p (h c) n", c=4)

        def turn_act(act, q, t, pos=None):
            act.wait_ge(tr_done, count(q, t if pos is None else pos))
            nc.scalar.copy(hTh[:, :, t * P:(t + 1) * P], turned(t)).then_inc(th_done, 1)

        def turn_dve(dve, q, t, pos=None):
            dve.wait_ge(th_done, count(q, t if pos is None else pos))
            nc.vector.tensor_tensor(hTl[:, :, t * P:(t + 1) * P], turned(t),
                                    hTh[:, :, t * P:(t + 1) * P].bitcast(F32), ALU.subtract).then_inc(tl_done, 1)

        def square_act(act, n, t):
            if n >= 0:
                act.wait_ge(x_done, NT * n + t + 1)
            if t == 3:
                act.wait_ge(sq_done, count(n, 2))
            c = NT * (n + 1) + t
            nc.scalar.activation(y_of(t), halves(X[:, t, :]), ACT.Square, accum_out=sums[:, c:c + 1]
                                 ).then_inc(sq_done, 1)

        def root_pool(pool, chain, n, t):
            c = slice(NT * (n + 1) + t, NT * (n + 1) + t + 1)
            pool.wait_ge(sq_done, count(n, t))
            chain(nc.gpsimd.tensor_scalar(sums[:, c], sums[:, c], 1.0 / D, EPS, ALU.mult, ALU.add))
            nc.gpsimd.tensor_tensor(rinv[:, c], sums[:, c], halfneg[:], ALU.pow).then_inc(r_done, 1)

        def norm_dve(dve, n, t):
            c = NT * (n + 1) + t
            dve.wait_ge(r_done, count(n, t))
            nc.vector.scalar_tensor_tensor(XN[:, t % 2, :], X[:, t, :], rinv[:, c:c + 1], grow[:],
                                           ALU.mult, ALU.mult).then_inc(xn_done, 1)

        def turn_x_pe(pe, n, t):
            pe.wait_ge(xn_done, count(n, t))
            turn_pe(pe, XN[:, t % 2, :], t)

        def end_pe(pe, n, T0, nk, hi, lo, order, ready):
            T1 = T0 + 2 * nk // 4

            def part(T, t):
                w_hi, w_lo = moving(T)
                for b in range(4):
                    half, k = divmod(4 * (T - T0) + b, nk)
                    last = three(ps[:, y_bank(t) + half, :], hi[:, k, t * P:(t + 1) * P],
                                 lo[:, k, t * P:(t + 1) * P], w_hi[:, b, :], w_lo[:, b, :],
                                 start=k == 0, stop=k == nk - 1)
                return last

            for T in range(T0, T1 - 2):
                pe.wait_ge(lo_ready, T + 1)
                for t in (order if T == T0 else range(NT)):
                    if T == T0:
                        ready(t)
                    last = part(T, t)
                last.then_inc(w_used, 1)
                if T == T0:
                    ready(None)
            A, B = T1 - 2, T1 - 1
            pe.wait_ge(lo_ready, T1 - 1)
            part(A, 0)
            part(A, 1)
            pe.wait_ge(lo_ready, T1)
            part(B, 0).then_inc(y_done, 1)
            part(B, 1).then_inc(y_done, 1)
            part(A, 2)
            part(A, 3).then_inc(w_used, 1)
            turn_x_pe(pe, n, 0)
            part(B, 2).then_inc(y_done, 1)
            turn_x_pe(pe, n, 1)
            part(B, 3).then_inc(w_used, 1)

        def late_pe(pe, n):
            turn_x_pe(pe, n, 2)
            turn_x_pe(pe, n, 3)

        def end_act(act, n, q, T1):
            def square_y(t):
                if t < NT - 1:
                    act.wait_ge(y_done, (NT - 1) * n + t + 1)
                else:
                    act.wait_ge(w_used, T1)
                    act.wait_ge(ysq_done, NT * n + t)
                nc.scalar.activation(halves(junk[:]), y_of(t), ACT.Square,
                                     accum_out=ysum[:, NT * n + t:NT * n + t + 1]).then_inc(ysq_done, 1)

            square_y(0)
            square_act(act, n, 0)
            square_y(1)
            square_act(act, n, 1)
            hi_part(act, T1)
            turn_act(act, q, 0)
            square_y(2)
            turn_act(act, q, 1)
            square_y(3)

        def late_act(act, n, q, T1):
            hi_part(act, T1 + 1)
            square_act(act, n, 2)
            square_act(act, n, 3)
            turn_act(act, q, 2)
            turn_act(act, q, 3)

        def end_pool(pool, chain, n, factor):
            for t in range(NT):
                c = slice(NT * n + t, NT * n + t + 1)
                pool.wait_ge(ysq_done, NT * n + t + 1)
                chain(nc.gpsimd.tensor_scalar(ysum[:, c], ysum[:, c], 1.0 / D, EPS, ALU.mult, ALU.add))
                if factor == 1.0:
                    nc.gpsimd.tensor_tensor(yinv[:, c], ysum[:, c], halfneg[:], ALU.pow).then_inc(yr_done, 1)
                else:
                    chain(nc.gpsimd.tensor_tensor(yinv[:, c], ysum[:, c], halfneg[:], ALU.pow))
                    nc.gpsimd.tensor_scalar(yinv[:, c], yinv[:, c], factor, None, ALU.mult).then_inc(yr_done, 1)
                if t < 2:
                    root_pool(pool, chain, n, t)

        def late_pool(pool, chain, n):
            root_pool(pool, chain, n, 2)
            root_pool(pool, chain, n, 3)

        def end_dve(dve, chain, n, q, T1):
            def add(t):
                dve.wait_ge(yr_done, NT * n + t + 1)
                chain(nc.vector.scalar_tensor_tensor(y_of(t), y_of(t), yinv[:, NT * n + t:NT * n + t + 1],
                                                     halves(gbc[:]), ALU.mult, ALU.mult))
                nc.vector.tensor_tensor(halves(X[:, t, :]), halves(X[:, t, :]), y_of(t), ALU.add
                                        ).then_inc(x_done, 1)

            dve.wait_ge(gain_in, 32 * (n + 1))
            add(0)
            norm_dve(dve, n, 0)
            add(1)
            norm_dve(dve, n, 1)
            lo_part(dve, T1)
            turn_dve(dve, q, 0)
            add(2)
            turn_dve(dve, q, 1)
            add(3)

        def late_dve(dve, n, q, T1):
            lo_part(dve, T1 + 1)
            norm_dve(dve, n, 2)
            norm_dve(dve, n, 3)
            turn_dve(dve, q, 2)
            turn_dve(dve, q, 3)

        def project_pe(pe, T0, b, banks, after=None, bank_free=None):
            order = [(half, t) for half in range(2) for t in range(NT)]
            if after:
                n, q = after
                order.sort(key=lambda half_t: half_t[1] >= 2)
                if q >= 0:
                    pe.wait_ge(tl_done, count(q, 1))
            for i, (half, t) in enumerate(order):
                T = T0 + half
                w_hi, w_lo = moving(T)
                if t == 0:
                    pe.wait_ge(lo_ready, T + 1)
                if after and t >= 2 and half == 0:
                    pe.wait_ge(tl_done, count(q, t))
                if after and (half, t) == (1, 1):
                    late_pe(pe, n)
                if bank_free and half == 0:
                    bank_free(t)
                for kk in range(4):
                    k = 4 * half + kk
                    last = three(ps[:, banks + t, :], hTh[:, k, t * P:(t + 1) * P],
                                 hTl[:, k, t * P:(t + 1) * P], w_hi[:, kk, :], w_lo[:, kk, :],
                                 start=k == 0, stop=k == NC - 1)
                if t == NT - 1:
                    last.then_inc(w_used, 1)
                elif half == 1:
                    last.then_inc(proj_done, 1)

        def projected(eng, T0, b, t):
            if t == NT - 1:
                eng.wait_ge(w_used, T0 + 2)
            else:
                eng.wait_ge(proj_done, (NT - 1) * b + t + 1)

        FILL_STEPS, FILL_EACH = 6, 6

        def fill(filler, n, bank):
            for _ in range(n):
                nc.tensor.matmul(ps[:, bank, :], *filler, start=True, stop=True)

        def attend_pe(pe, units, buf, v_ready, filler):
            E, MS, PTh, PTl = buf
            for s in range(len(units) + 5):
                if s < FILL_STEPS:
                    fill(filler, FILL_EACH, 7)
                if s < len(units):
                    if s >= 2:
                        pe.wait_ge(ex_done, s - 1)
                    if units[s]["spread"]:
                        pe.wait_ge(sp_done, sum(bool(u["spread"]) for u in units[:s + 1]))
                    for j, (q_hi, q_lo, k_hi, k_lo) in enumerate(units[s]["scores"]):
                        last = three(ps[:, 2 * (s % 2) + j, 0:units[s]["keys"]], q_hi, q_lo, k_hi, k_lo,
                                     start=True, stop=True)
                    last.then_inc(s_done, 1)
                if 0 <= s - 3 < len(units):
                    u = s - 3
                    if units[u]["kind"] == "diff":
                        pe.wait_ge(mix_done, diffs(units, u))
                    else:
                        pe.wait_ge(ex_done, u + 1)
                    if u >= 2:
                        pe.wait_ge(ptl_done, u - 1)
                    for b in range(units[u]["keys"] // P):
                        last = nc.tensor.transpose(ps[:, 4 + u % 2, b * P:(b + 1) * P],
                                                   E[:, u % 3, 0, b * P:(b + 1) * P], ident[:])
                    last.then_inc(t_done, 1)
                if s >= 5:
                    u = s - 5
                    if u == 0:
                        v_ready()
                    pe.wait_ge(ptl_done, u + 1)
                    if u >= 2:
                        pe.wait_ge(o_done, u - 1)
                    nb = units[u]["keys"] // P
                    both = ps[:, 6 + u % 2, 0:2 * HD].rearrange("p (two n) -> p two n", two=2)
                    v = units[u]["v"]
                    for b in range(nb):
                        last = nc.tensor.matmul(both, PTh[:, u % 2, b, :], v[b], start=b == 0, stop=b == nb - 1)
                        if b < nb - 1:
                            nc.tensor.matmul(both[:, 0, :], PTl[:, u % 2, b, :], v[b][:, 0, :], start=False, stop=False)
                        if b == nb - 2:
                            nc.tensor.matmul(both[:, 0, :], PTl[:, u % 2, nb - 1, :], v[nb - 1][:, 0, :],
                                             start=False, stop=False)
                    last.then_inc(pv_done, 1)

        def diffs(units, u):
            return sum(x["kind"] == "diff" for x in units[:u + 1])

        def mix_pool(pool, chain, units, buf, u):
            e1, e2 = (buf[0][:, u % 3, j, :] for j in range(2))
            pool.wait_ge(c_done, diffs(units, u))
            chain(nc.gpsimd.tensor_tensor(e2, e2, erec[:, u % 8, 1:2].to_broadcast([P, S]), ALU.mult))
            nc.gpsimd.tensor_tensor(e1, e1, e2, ALU.add).then_inc(mix_done, 1)

        def part_of_pt(PT, u, n):
            return PT[:, u % 2, 0:n // P, :].rearrange("p b n -> p (b n)")

        def attend_act(act, units, buf, beside=None):
            E, MS, PTh, PTl = buf

            def spread(s):
                for dst, src in units[s]["spread"]:
                    last = nc.scalar.copy(dst, src)
                if units[s]["spread"]:
                    last.then_inc(sp_done, 1)

            spread(0)
            spread(1)
            for s in range(len(units) + 4):
                if s >= 4:
                    u = s - 4
                    n = units[u]["keys"]
                    act.wait_ge(t_done, u + 1)
                    if u >= 2:
                        act.wait_ge(pv_done, u - 1)
                    nc.scalar.copy(part_of_pt(PTh, u, n), ps[:, 4 + u % 2, 0:n]).then_inc(pt_done, 1)
                if s < len(units):
                    if s >= 3:
                        act.wait_ge(t_done, s - 2)
                    act.wait_ge(mx_done, s + 1)
                    for j in range(len(units[s]["scores"])):
                        n = units[s]["keys"]
                        last = nc.scalar.activation(
                            E[:, s % 3, j, 0:n],
                            MS[:, s % 2, 0:n] if units[s]["kind"] == "dilated" else ps[:, 2 * (s % 2) + j, 0:n],
                            ACT.Exp, bias=negmax[:, s % 2, j:j + 1], accum_out=esum[:, s % 2, j:j + 1])
                    last.then_inc(ex_done, 1)
                if s + 2 < len(units):
                    spread(s + 2)
                if beside:
                    beside(s)

        def attend_dve(dve, chain, units, buf, beside=None, after=None):
            E, MS, PTh, PTl = buf
            for s in range(len(units) + 6):
                if s < len(units):
                    un, n = units[s], units[s]["keys"]
                    dve.wait_ge(s_done, s + 1)
                    if un["kind"] == "dilated":
                        chain(nc.vector.tensor_tensor_reduce(
                            out=MS[:, s % 2, :], in0=ps[:, 2 * (s % 2), :], in1=un["bias"], scale=1.0,
                            scalar=-3.0e38, op0=ALU.add, op1=ALU.max, accum_out=rowmax[:, s % 2, :]))
                        nc.vector.tensor_scalar(negmax[:, s % 2, 0:1], rowmax[:, s % 2, :], -1.0, None,
                                                ALU.mult).then_inc(mx_done, 1)
                    else:
                        js = len(un["scores"])
                        nc.vector.tensor_reduce(negmax[:, s % 2, 0:js], ps[:, 2 * (s % 2):2 * (s % 2) + js, 0:n],
                                                AX.X, ALU.max, negate=True).then_inc(mx_done, 1)
                if 0 <= s - 4 < len(units):
                    u = s - 4
                    n = units[u]["keys"]
                    dve.wait_ge(pt_done, u + 1)
                    nc.vector.tensor_tensor(part_of_pt(PTl, u, n), ps[:, 4 + u % 2, 0:n],
                                            part_of_pt(PTh, u, n).bitcast(F32), ALU.subtract).then_inc(ptl_done, 1)
                if s >= 6:
                    u = s - 6
                    dve.wait_ge(pv_done, u + 1)
                    nc.vector.tensor_scalar(otmp[:, u % 2, :], ps[:, 6 + u % 2, HD:2 * HD], erec[:, u % 8, 0:1], None,
                                            ALU.mult).then_inc(ot_done, 1)
                if 1 <= s <= len(units):
                    u = s - 1
                    dve.wait_ge(ex_done, u + 1)
                    r = erec[:, u % 8, :]
                    if units[u]["kind"] == "diff":
                        chain(nc.vector.reciprocal(r, esum[:, u % 2, :]))
                        nc.vector.tensor_scalar(r[:, 1:2], r[:, 1:2], esum[:, u % 2, 0:1], lam[:, 5:6],
                                                ALU.mult, ALU.mult).then_inc(c_done, 1)
                    else:
                        nc.vector.reciprocal(r[:, 0:1], esum[:, u % 2, 0:1])
                if s >= 6:
                    u = s - 6
                    dve.wait_ge(ot_done, u + 1)
                    nc.vector.scalar_tensor_tensor(units[u]["out"], ps[:, 6 + u % 2, 0:HD], erec[:, u % 8, 0:1],
                                                   otmp[:, u % 2, :], ALU.mult, ALU.add).then_inc(o_done, 1)
                    if after:
                        after(u)
                if beside:
                    beside(s)

        with nc.Block() as block:
            @block.sync
            def _(sp):
                for t in range(NT):
                    sp.dma_start(X[:, t, :], a["x"][0, t * P:(t + 1) * P, :]).then_inc(x_in[t], 16)
                    if t % 2:
                        sp.dma_start(raw[:, t // 2, :], a["weights"][t // 2]).then_inc(raw_in[t // 2], 16)
                sp.wait_ge(x_in[2], 16)
                sp.wait_ge(x_in[3], 16)
                sp.wait_ge(raw_in[1], 16)

            @block.tensor
            def _(pe):
                pe.wait_ge(par, 32)
                for t in range(2):
                    pe.wait_ge(xn_done, t + 1)
                    turn_pe(pe, XN[:, t, :], t)

            @block.scalar
            def _(act):
                act.dma_start(ident[:], a["identity"]).then_inc(par, 16)
                act.dma_start(grow[:], a["next_gain"][0:1].to_broadcast([P, D])).then_inc(par, 16)
                for t in range(2):
                    act.wait_ge(x_in[t], 16)
                    nc.scalar.activation(y_of(t), halves(X[:, t, :]), ACT.Square, accum_out=sums[:, t:t + 1]
                                         ).then_inc(sq_done, 1)
                act.wait_ge(raw_in[0], 16)
                nc.scalar.activation(whi[:, 0, :], raw[:, 0, :], ACT.Copy).then_inc(hi_ready, 1)
                for t in range(2):
                    act.wait_ge(tr_done, t + 1)
                    nc.scalar.copy(hTh[:, :, t * P:(t + 1) * P], turned(t)).then_inc(th_done, 1)

            @block.vector
            def _(dve):
                dve.wait_ge(par, 32)
                for t in range(2):
                    dve.wait_ge(r_done, t + 1)
                    nc.vector.scalar_tensor_tensor(XN[:, t, :], X[:, t, :], rinv[:, t:t + 1], grow[:],
                                                   ALU.mult, ALU.mult).then_inc(xn_done, 1)
                lo_part(dve, 0)
                for t in range(2):
                    dve.wait_ge(th_done, t + 1)
                    nc.vector.tensor_tensor(hTl[:, :, t * P:(t + 1) * P], turned(t),
                                            hTh[:, :, t * P:(t + 1) * P].bitcast(F32), ALU.subtract)

            @block.gpsimd
            def _(pool):
                chain = Chain(pool, pchain)
                chain(nc.gpsimd.memset(halfneg[:], -0.5))
                for t in range(2):
                    pool.wait_ge(sq_done, t + 1)
                    chain(nc.gpsimd.tensor_scalar(sums[:, t:t + 1], sums[:, t:t + 1], 1.0 / D, EPS, ALU.mult, ALU.add))
                    nc.gpsimd.tensor_tensor(rinv[:, t:t + 1], sums[:, t:t + 1], halfneg[:], ALU.pow).then_inc(r_done, 1)

        def next_round():
            nc.sync.sem_clear(range(nums[0], nums[-1] + 1))
            nc.all_engine_barrier()

        @contextmanager
        def layers():
            with nc.Fori(0, DEPTH) as layer:
                with nc.Block() as block:
                    yield layer, block
                next_round()

        next_round()

        P1 = at("P1", [P, NT, 3072], AT_R)
        P1r = at("P1r", [P, NT, 3072], AT_R, F32R)
        QK = at("QK", [P, 2, NC, S], AT_HH, F32R)
        QX = at("QX", [P, 2, 4, S], AT_R + 57344, F32R)
        QD = at("QD", [P, 4, 2, P], AT_R + 98304, F32R)
        QG = at("QG", [P, 2, 2, P], AT_R + 75520, F32R)
        memX = at("memX", [P, 2, D], AT_R + 49152)
        memTh = at("memTh", [P, NC, N_MEM], AT_R + 49152 + 8192, F32R)
        memTl = at("memTl", [P, NC, N_MEM], AT_R + 49152 + 16384, F32R)
        mkh = at("mkh", [P, 2, N_MEM], AT_R + 49152, F32R)
        mkl = at("mkl", [P, 2, N_MEM], AT_R + 51200, F32R)
        mv = at("mv", [P, 2, 2, N_MEM], AT_R + 53248, F32R)
        lin_cos = at("lin_cos", [P, NT, 16], AT_R + 86016)
        lin_sin = at("lin_sin", [P, NT, 16], AT_R + 86272)
        ax_cos = at("ax_cos", [P, NT, 2, 16], AT_R + 86528)
        ax_sin = at("ax_sin", [P, NT, 2, 16], AT_R + 87040)
        qk_gain = at("qk_gain", [P, 2, HD], AT_R + 87552)
        subln = at("subln", [P, HD], AT_R + 73728)
        lamin = at("lamin", [P, 4, 32], AT_R + 88064)
        lamt = at("lamt", [P, 2, 32], AT_R + 88576)
        rA = at("rA", [P, 768], AT_R + 77824)
        rB = at("rB", [P, 768], AT_R + 77824 + 3072)
        osq = at("osq", [P, 384], AT_R + 73984)
        buf1 = (at("E1", [P, 3, 2, S], AT_R + 77824), None, at("PTh1", [P, 2, 4, P], AT_R + 90112, F32R),
                at("PTl1", [P, 2, 4, P], AT_R + 94208, F32R))
        BANK1 = [4, 0, 4, 0, 0, 4]

        filler1 = (mkh[:, 0, 0:P], mv[:, 0, :, :].rearrange("p a n -> p (a n)"))

        def turned1(c, rows=slice(0, P), cols=slice(0, S)):
            both = turned_parts(c, rows, cols)
            return both[:, 0, :], both[:, 1, :]

        def turned_parts(c, rows, cols):
            return QK[rows, :, c, cols] if c < NC else QX[rows, :, c - NC, cols]

        def values1(b, col):
            return P1r[:, b, 1024:2048].rearrange("p (two n) -> p two n", two=2)[:, :, col - 1536:col - 1536 + HD]
        TURN_ORDER = [0, 2, 1, 3]
        par_all = 16 * 11

        def scores1():
            units = []
            for t in range(NT):
                tk = slice(t * P, (t + 1) * P)
                for h in range(N_DIFF):
                    sc, sp = [], []
                    for j in range(2):
                        c, r = divmod(2 * h + j, 4)
                        rows = slice(32 * r, 32 * r + 32)
                        sp.append((QD[rows, r, :, :], turned_parts(c, rows, tk)))
                        sc.append((QD[:, r, 0, :], QD[:, r, 1, :]) + turned1(3 + c))
                    units.append(dict(kind="diff", spread=sp, t=t, keys=S, scores=sc, out=P1[:, t, HD * h:HD * (h + 1)],
                                      v=[values1(b, 1536 + HD * h) for b in range(NT)]))
                for h in (0, 3, 1, 4, 2, 5):
                    kv, c = divmod(h, 3)
                    rows = slice(HD * kv, HD * kv + HD)
                    o = 384 + HD * h
                    units.append(dict(kind="gqa", t=t, keys=S,
                                      spread=[(QG[rows, kv, :, :], turned_parts(6 + c, rows, tk))],
                                      scores=[(QG[:, kv, 0, :], QG[:, kv, 1, :]) + turned1(9)],
                                      out=P1[:, t, o:o + HD],
                                      v=[values1(b, 1920 + HD * kv) for b in range(NT)]))
                for h in range(N_MEMH):
                    c, r = divmod(h, 2)
                    rows = slice(HD * r, HD * r + HD)
                    o = 768 + HD * h
                    units.append(dict(kind="mem", spread=[], t=t, keys=N_MEM, out=P1[:, t, o:o + HD],
                                      scores=[turned1(10 + c, rows, tk) + (mkh[rows, c, :], mkl[rows, c, :])],
                                      v=[mv[:, b, :, HD * h:HD * (h + 1)] for b in range(2)]))
            return units

        units1 = scores1()
        scale1 = [32 ** -0.5] * 3 + [None] * 3 + [0.125] * 3 + [None] + [0.125] * 2

        with layers() as (layer, block):
            one = lambda name: a[name][bass.ds(layer, 1)]

            @block.sync
            def _(sp):
                first_tiles(sp)
                sp.dma_start(memX[:], a["mem"].rearrange("b (t p) d -> p (b t) d", p=P)).then_inc(par, 16)
                sp.dma_start(gcol[:], one("mem_norm").rearrange("a p c -> (a p) c")).then_inc(par, 16)
                for dst, name in ((lin_cos, "lin_cos"), (lin_sin, "lin_sin")):
                    sp.dma_start(dst[:], a[name]).then_inc(par, 16)
                for dst, name in ((ax_cos, "ax_cos"), (ax_sin, "ax_sin")):
                    sp.dma_start(dst[:], a[name]).then_inc(par, 16)
                for dst, name in ((qk_gain[:, 0, :], "gqa_q_norm"), (qk_gain[:, 1, :], "gqa_k_norm"),
                                  (subln[:], "diff_subln")):
                    sp.dma_start(dst, one(name).to_broadcast([P, HD])).then_inc(par, 16)
                sp.dma_start(lamin[:].rearrange("p a b -> p (a b)"),
                             one("diff_lambda").to_broadcast([P, 128])).then_inc(par, 16)
                sp.dma_start(lamc[:], one("lambda_init").to_broadcast([P, 2])).then_inc(par, 16)
                sp.dma_start(gbc[:], a["post_gain"][bass.ds(layer, 1)].to_broadcast([P, D])).then_inc(gain_in, 16)
                stream(sp, layer * B1_TILES, B1_TILES)

            @block.tensor
            def _(pe):
                def bank_free(t):
                    if t % 2:
                        pe.wait_ge(ev_v, 6 + (t + 1) // 2)
                    else:
                        pe.wait_ge(ev_a, 6 + t // 2 + 1)

                for b in range(6):
                    if b in (2, 3, 4):
                        pe.wait_ge(ev_a, 2 * (b - 1))
                        pe.wait_ge(ev_v, 2 * (b - 1))
                    if b == 4:
                        pe.wait_ge(g_v, 2)
                        for c in range(NC):
                            for t in range(2):
                                last = nc.tensor.transpose(ps[:, 4 + c // 2, (2 * (c % 2) + t) * P:
                                                              (2 * (c % 2) + t + 1) * P],
                                                           memX[:, t, c * P:(c + 1) * P], ident[:])
                            if c % 2:
                                last.then_inc(sm_t, 1)
                    if b == 5:
                        pe.wait_ge(mw_done, NC)
                    project_pe(pe, B1_PROJ + 2 * b, b, BANK1[b], after=None if b else (-1, -1),
                               bank_free=bank_free if b == 4 else None)
                w_hi, w_lo = stationary(B1_KV)
                pe.wait_ge(ev_a, 12)
                pe.wait_ge(lo_ready, B1_KV + 1)
                for c in range(2):
                    for k in range(NC):
                        last = three(ps[:, c, 0:N_MEM], w_hi[:, c, k, :], w_lo[:, c, k, :],
                                     memTh[:, k, :], memTl[:, k, :], k == 0, k == NC - 1)
                    last.then_inc(sm_t if c == 0 else w_used, 1)
                v_hi = whi[:, 1, :].rearrange("p (k n) -> p k n", k=NC)
                v_lo = wlo[:, 1, :].rearrange("p (k n) -> p k n", k=NC)
                pe.wait_ge(lo_ready, B1_KV + 2)
                for t in range(2):
                    for k in range(NC):
                        last = three(ps[:, 2 + t, 0:N_MEM], memTh[:, k, t * P:(t + 1) * P],
                                     memTl[:, k, t * P:(t + 1) * P], v_hi[:, k, :], v_lo[:, k, :],
                                     k == 0, k == NC - 1)
                    last.then_inc(sm_t if t == 0 else w_used, 1)
                pe.wait_ge(ev_a, 8 + 8)
                pe.wait_ge(q_ready, NT)
                for c in range(12):
                    if c == 4:
                        pe.wait_ge(mw_done, NC + 4)
                    if c >= 8:
                        pe.wait_ge(qte_v, c - 7)
                    if c >= 4:
                        fill(filler1, 2, (c + 4) % 8)
                    for t in range(NT):
                        last = nc.tensor.transpose(ps[:, (c + 4) % 8, t * P:(t + 1) * P], P1[:, t, c * P:(c + 1) * P],
                                                   ident[:])
                    last.then_inc(qt_done, 1)
                pe.wait_ge(qte_v, 5)
                fill(filler1, 8, 0)
                pe.wait_ge(qte_v, 12)
                attend_pe(pe, units1, buf1, lambda: pe.wait_ge(vl_done, NT), filler1)
                for t in TURN_ORDER:
                    if y_bank(t) == 6:
                        pe.wait_ge(o_done, len(units1))
                    pe.wait_ge(o_ready, t + 1)
                    turn_pe(pe, P1[:, t, 0:D], t)
                end_pe(pe, 0, B1_OUT, NC, hTh, hTl, TURN_ORDER,
                       lambda t: t is not None and pe.wait_ge(tl_done, count(0, TURN_ORDER.index(t))))

            @block.scalar
            def _(act):
                act.sem_inc(hi_ready, 1)
                late_act(act, -1, -1, 0)
                act.wait_ge(par, par_all)
                for t in range(2):
                    nc.scalar.activation(junk_mem[:, t, :], memX[:, t, :], ACT.Square,
                                         accum_out=osum[:, t, 0:1]).then_inc(g_a, 1)
                act.wait_ge(g_v, 3)
                nc.scalar.activation(lam[:, 2:4], lam[:, 0:2], ACT.Exp).then_inc(g_a, 1)
                for b in range(6):
                    hi_part(act, B1_PROJ + 2 * b + 2)
                    for t in range(NT):
                        if b >= 4:
                            projected(act, B1_PROJ + 2 * b, b, t)
                            nc.scalar.activation(P1[:, t, 512 * b:512 * (b + 1)], ps[:, BANK1[b] + t, :],
                                                 ACT.Silu).then_inc(ev_a, 1)
                        elif t % 2 == 0:
                            projected(act, B1_PROJ + 2 * b, b, t)
                            nc.scalar.copy(P1[:, t, 512 * b:512 * (b + 1)], ps[:, BANK1[b] + t, :]
                                           ).then_inc(ev_a, 1)
                    hi_part(act, B1_PROJ + 2 * b + 3)
                    if b == 3:
                        for c in range(NC):
                            act.wait_ge(sm_t, c // 2 + 1)
                            nc.scalar.activation(memTh[:, c, :], ps[:, 4 + c // 2, 256 * (c % 2):256 * (c % 2 + 1)],
                                                 ACT.Copy, scale=gcol[:, c:c + 1]).then_inc(sm_e, 1)
                for c in range(2):
                    act.wait_ge(*((sm_t, NC // 2 + 1), (w_used, B1_KV + 1))[c])
                    nc.scalar.copy(mkh[:, c, :], ps[:, c, 0:N_MEM]).then_inc(sm_e, 1)
                hi_part(act, B1_KV + 2)
                for t in range(2):
                    act.wait_ge(*((sm_t, NC // 2 + 2), (w_used, B1_KV + 2))[t])
                    nc.scalar.copy(mv[:, t, 0, :], ps[:, 2 + t, 0:N_MEM]).then_inc(sm_e, 1)
                hi_part(act, B1_KV + 3)
                for c in range(12):
                    act.wait_ge(qt_done, c + 1)
                    nc.scalar.activation(turned1(c)[0], ps[:, (c + 4) % 8, :], ACT.Copy, scale=scale1[c] or 1.0
                                         ).then_inc(qte_a, 1)

                def value_high(s):
                    if s < NT:
                        nc.scalar.copy(P1r[:, s, 1024:1536], P1[:, s, 1536:2048]).then_inc(vh_done, 1)

                act.wait_ge(qte_v, 12)
                act.wait_ge(zero_done, 1)
                attend_act(act, units1, buf1, value_high)
                for pos, t in enumerate(TURN_ORDER):
                    turn_act(act, 0, t, pos)
                act.dma_start(grow[:], a["next_gain"][bass.ds(layer + 1, 1)].to_broadcast([P, D])
                              ).then_inc(gain_in, 16)
                hi_part(act, B1_OUT + 2)
                hi_part(act, B1_OUT + 3)
                end_act(act, 0, 1, B1_TILES)

            @block.vector
            def _(dve):
                chain = Chain(dve, dchain)
                dve.sem_inc(lo_ready, 1)
                late_dve(dve, -1, -1, 0)
                for t in range(2):
                    dve.wait_ge(g_p, t + 1)
                    nc.vector.tensor_scalar(memX[:, t, :], memX[:, t, :], oinv[:, t, 0:1], None, ALU.mult
                                            ).then_inc(g_v, 1)
                dve.wait_ge(par, par_all)
                for j in range(2):
                    chain(nc.vector.tensor_tensor_reduce(
                        out=lamt[:, j, :], in0=lamin[:, 2 * j, :], in1=lamin[:, 2 * j + 1, :], scale=1.0, scalar=0.0,
                        op0=ALU.mult, op1=ALU.add, accum_out=lam[:, j:j + 1]))
                nc.vector.tensor_scalar(subln[:], subln[:], lamc[:, 1:2], None, ALU.mult).then_inc(g_v, 1)
                dve.wait_ge(g_a, 3)
                chain(nc.vector.tensor_tensor(lam[:, 4:5], lam[:, 3:4], lam[:, 2:3], ALU.subtract))
                chain(nc.vector.tensor_tensor(lam[:, 5:6], lam[:, 4:5], lamc[:, 0:1], ALU.subtract))

                def rotate(x, n, cos, sin, out_inc=None):
                    A = rA[:, 0:32 * n].rearrange("p (n r d) -> p n r d", r=2, d=16)
                    B = rB[:, 0:32 * n].rearrange("p (n r d) -> p n r d", r=2, d=16)
                    xs = x.rearrange("p n (r d) -> p n r d", r=2)
                    c4 = cos.unsqueeze(1).unsqueeze(1).to_broadcast([P, n, 2, 16])
                    s3 = sin.unsqueeze(1).to_broadcast([P, n, 16])
                    nc.vector.tensor_tensor(A, xs, c4, ALU.mult)
                    nc.vector.scalar_tensor_tensor(B[:, :, 0, :], xs[:, :, 1, :], -1.0, s3, ALU.mult, ALU.mult)
                    chain(nc.vector.tensor_tensor(B[:, :, 1, :], xs[:, :, 0, :], s3, ALU.mult))
                    return nc.vector.tensor_tensor(x, A.rearrange("p n r d -> p n (r d)"),
                                                   B.rearrange("p n r d -> p n (r d)"), ALU.add)

                def rope(t):
                    gq = P1[:, t, 768:1280].rearrange("p (h d) -> p h d", d=HD)
                    sq = rA[:, 0:512].rearrange("p (h d) -> p h d", d=HD)
                    chain(nc.vector.tensor_tensor(sq, gq, gq, ALU.mult))
                    nc.vector.tensor_reduce(hsum[:, t, :], sq, AX.X, ALU.add).then_inc(g_v, 1)
                    dve.wait_ge(g_v, 3 + t + 1)
                    chain(rotate(P1[:, t, 0:768].rearrange("p (n d) -> p n d", d=32), 24, lin_cos[:, t, :],
                                 lin_sin[:, t, :]))
                    dve.wait_ge(g_p, 2 + t + 1)
                    chain(nc.vector.tensor_tensor(gq, gq, hinv[:, t, :].unsqueeze(2).to_broadcast([P, 8, HD]),
                                                  ALU.mult))
                    nc.vector.tensor_tensor(gq[:, 0:6, :], gq[:, 0:6, :],
                                            qk_gain[:, 0:1, :].to_broadcast([P, 6, HD]), ALU.mult)
                    chain(nc.vector.tensor_tensor(gq[:, 6:8, :], gq[:, 6:8, :],
                                                  qk_gain[:, 1:2, :].to_broadcast([P, 2, HD]), ALU.mult))
                    for axis in range(2):
                        last = rotate(gq[:, :, 32 * axis:32 * axis + 32], 8, ax_cos[:, t, axis, :],
                                      ax_sin[:, t, axis, :])
                        if axis == 0:
                            chain(last)
                    last.then_inc(q_ready, 1)
                    dve.wait_ge(q_ready, t + 1)

                for b in range(6):
                    if b == 3:
                        dve.wait_ge(ev_a, 6)
                        dve.wait_ge(ev_v, 6)
                        rope(0)
                    if b == 4:
                        for c in range(NC):
                            dve.wait_ge(sm_e, c // 2 * 2 + 2)
                            nc.vector.scalar_tensor_tensor(
                                memTl[:, c, :], ps[:, 4 + c // 2, 256 * (c % 2):256 * (c % 2 + 1)],
                                gcol[:, c:c + 1], memTh[:, c, :].bitcast(F32), ALU.mult, ALU.subtract
                                ).then_inc(mw_done, 1)
                        rope(1)
                    if b == 5:
                        rope(3)
                    lo_part(dve, B1_PROJ + 2 * b + 2)
                    if b < 4:
                        for t in (1, 3):
                            projected(dve, B1_PROJ + 2 * b, b, t)
                            nc.vector.tensor_copy(P1[:, t, 512 * b:512 * (b + 1)], ps[:, BANK1[b] + t, :]
                                                  ).then_inc(ev_v, 1)
                    if b == 4:
                        rope(2)
                    lo_part(dve, B1_PROJ + 2 * b + 3)
                for i in range(2):
                    for c in range(2):
                        low, high = (mv[:, c, 1, :], mv[:, c, 0, :]) if i else (mkl[:, c, :], mkh[:, c, :])
                        dve.wait_ge(sm_e, NC + 2 * i + c + 1)
                        nc.vector.tensor_tensor(low, ps[:, 2 * i + c, 0:N_MEM], high.bitcast(F32), ALU.subtract
                                                ).then_inc(mw_done, 1)
                    lo_part(dve, B1_KV + 2 + i)
                for c in range(12):
                    dve.wait_ge(qte_a, c + 1)
                    nc.vector.scalar_tensor_tensor(turned1(c)[1], ps[:, (c + 4) % 8, :], scale1[c] or 1.0,
                                                   turned1(c)[0].bitcast(F32), ALU.mult, ALU.subtract
                                                   ).then_inc(qte_v, 1)

                def value_low(s):
                    if s < NT:
                        dve.wait_ge(vh_done, s + 1)
                        nc.vector.tensor_tensor(P1r[:, s, 1536:2048], P1[:, s, 1536:2048],
                                                P1r[:, s, 1024:1536].bitcast(F32), ALU.subtract).then_inc(vl_done, 1)

                def after(u):
                    t, i = divmod(u, 16)
                    if i == 9:
                        dve.wait_ge(g_p, 6 + t + 1)
                        nc.vector.tensor_reduce(osum[:, t, 0:6], osq[:].rearrange("p (h d) -> p h d", d=HD), AX.X,
                                                ALU.add).then_inc(g_v, 1)

                attend_dve(dve, chain, units1, buf1, value_low, after)
                for pos, t in enumerate(TURN_ORDER):
                    turn_dve(dve, 0, t, pos)
                lo_part(dve, B1_OUT + 2)
                lo_part(dve, B1_OUT + 3)
                end_dve(dve, chain, 0, 1, B1_TILES)

            @block.gpsimd
            def _(pool):
                chain = Chain(pool, pchain)

                def inverse_root(src, dst, width, n, done):
                    chain(nc.gpsimd.tensor_scalar(src, src, 1.0 / width, EPS, ALU.mult, ALU.add))
                    nc.gpsimd.tensor_tensor(dst, src, halfneg[:].to_broadcast([P, n]), ALU.pow).then_inc(done, 1)

                late_pool(pool, chain, -1)
                pool.wait_ge(xn_done, count(-1, 3))
                nc.gpsimd.memset(QD[:].bitcast(F32), 0.0)
                nc.gpsimd.memset(QG[:].bitcast(F32), 0.0).then_inc(zero_done, 1)
                for t in range(2):
                    pool.wait_ge(g_a, t + 1)
                    inverse_root(osum[:, t, 0:1], oinv[:, t, 0:1], D, 1, g_p)
                for t in range(NT):
                    pool.wait_ge(g_v, 3 + t + 1)
                    inverse_root(hsum[:, t, :], hinv[:, t, :], HD, 8, g_p)
                def gate_memory(t):
                    pool.wait_ge(o_done, 16 * (t + 1))
                    nc.gpsimd.tensor_tensor(P1[:, t, 768:D], P1[:, t, 768:D], P1[:, t, 2816:3072], ALU.mult
                                            ).then_inc(o_ready, 1)

                for t in range(NT):
                    for h in range(N_DIFF):
                        mix_pool(pool, chain, units1, buf1, 16 * t + h)
                        if t and h == 4:
                            gate_memory(t - 1)
                    oa = P1[:, t, 0:384].rearrange("p (h d) -> p h d", d=HD)
                    pool.wait_ge(o_done, 16 * t + 6)
                    nc.gpsimd.tensor_tensor(osq[:], P1[:, t, 0:384], P1[:, t, 0:384], ALU.mult).then_inc(g_p, 1)
                    pool.wait_ge(g_v, 7 + t + 1)
                    chain(nc.gpsimd.tensor_scalar(osum[:, t, 0:6], osum[:, t, 0:6], 1.0 / HD, EPS,
                                                  ALU.mult, ALU.add))
                    chain(nc.gpsimd.tensor_tensor(oinv[:, t, 0:6], osum[:, t, 0:6], halfneg[:].to_broadcast([P, 6]),
                                                  ALU.pow))
                    chain(nc.gpsimd.tensor_tensor(oa, oa, oinv[:, t, 0:6].unsqueeze(2).to_broadcast([P, 6, HD]),
                                                  ALU.mult))
                    chain(nc.gpsimd.tensor_tensor(oa, oa, subln[:].unsqueeze(1).to_broadcast([P, 6, HD]),
                                                  ALU.mult))
                    pool.wait_ge(o_done, 16 * t + 12)
                    nc.gpsimd.tensor_tensor(P1[:, t, 0:768], P1[:, t, 0:768], P1[:, t, 2048:2816], ALU.mult)
                gate_memory(NT - 1)
                end_pool(pool, chain, 0, 1.0)

        P2 = at("P2", [P, NT, 2560], AT_R)
        P2r = at("P2r", [P, NT, 2560], AT_R, F32R)
        MQK = at("MQK", [P, 8, S], AT_R + 40960)
        MQKl = at("MQKl", [P, 8, S], AT_R + 40960, F32R)
        VA = at("VA", [P, NT, 2, 512], AT_R + 57344, F32R)

        filler2 = (VA[:, 0, 0, 0:P], VA[:, 0, 0, :])

        def value_part(b, t, part):
            return VA[:, t, part, :] if b == 2 else P2r[:, t, 1536 - 512 * part:2048 - 512 * part]
        AB = at("AB", [P, 8, S], AT_HH)
        masks = at("masks", [P, 2, S], AT_R + 73728)
        BM = at("BM", [P, NT, S], AT_R + 77824)
        acc = at("acc", [P, 2, S], AT_R + 86016)
        mgain = at("mgain", [P, S], AT_R + 94208)
        pad = at("pad", [P, 2, S + 4], AT_R + 98304)
        upto = at("upto", [P, 2, P], AT_R + 93184)
        rt = at("rt", [P, 2, 3, 128], AT_R + 90112)
        SW = at("SW", [P, 2, MH, 640], AT_R + 77824)
        aTh = at("aTh", [P, S], AT_R + 86016, F32R)
        aTl = at("aTl", [P, S], AT_R + 88064, F32R)
        identr = at("identr", [P, P], AT_R + 90112, F32R)
        PT2h = at("PT2h", [P, 2, NT, P], AT_R + 57344, F32R)
        PT2l = at("PT2l", [P, 2, NT, P], AT_R + 61440, F32R)
        acth = at("acth", [P, FC, S], AT_R, F32R)
        actl = at("actl", [P, FC, S], AT_R + 45056, F32R)
        sil = at("sil", [P, 2, S], AT_R + 90112)
        afull = at("afull", [P, 2, S], AT_R + 94208)
        buf2 = (at("E2", [P, 3, 1, S], AT_R + 86016), at("MS", [P, 2, S], AT_R + 96256),
                at("PTh2", [P, 2, 4, P], AT_R + 92160, F32R), at("PTl2", [P, 2, 4, P], AT_GBC, F32R))
        par2_all = 16 * 6

        units2 = []
        for t in range(NT):
            for h in range(8):
                c, r = divmod(h, 2)
                rows = slice(HD * r, HD * r + HD)
                units2.append(dict(kind="dilated", spread=[], t=t, keys=S, bias=BM[:, t, :],
                                   scores=[(hTh[rows, c, t * P:(t + 1) * P], hTl[rows, c, t * P:(t + 1) * P],
                                            hTh[rows, 4 + c, :], hTl[rows, 4 + c, :])],
                                   out=P2[:, t, HD * h:HD * (h + 1)],
                                   v=[VA[:, b, :, HD * h:HD * (h + 1)] for b in range(NT)]))

        def ffn_pe(pe, f, n, q, T_in, T_out):
            def chunk(T, p, c, cols=slice(0, S)):
                w_hi, w_lo = stationary(T)
                for k in range(NC):
                    last = three(ps[:, 4 + 2 * p + c, cols], w_hi[:, c, k, :], w_lo[:, c, k, :],
                                 hTh[:, k, cols], hTl[:, k, cols], k == 0, k == NC - 1)
                return last

            pe.wait_ge(gated, FC * f + 2)
            if q >= 0:
                pe.wait_ge(tl_done, count(q, 1))
            for p in range(2):
                pe.wait_ge(lo_ready, T_in + p + 1)
                for c in range(2):
                    if (p, c) == (1, 1):
                        late_pe(pe, n - 1)
                    chunk(T_in + p, p, c, slice(0, 2 * P))
            pe.wait_ge(tl_done, count(q, 3))
            for p in range(2):
                for c in range(2):
                    last = chunk(T_in + p, p, c, slice(2 * P, S))
                last.then_inc(w_used, 1)
            with pe.Fori(1, FC // 2) as i:
                for p in range(2):
                    pe.wait_ge(lo_ready, T_in + p + 1 + i * 2)
                    pe.wait_ge(gated, FC * f + p + 1 + i * 2)
                    chunk(T_in + p, p, 0)
                    chunk(T_in + p, p, 1).then_inc(w_used, 1)

            def ready(t):
                if t == 2:
                    pe.wait_ge(actl_done, FC * f + 4)
                elif t == 0:
                    pe.wait_ge(gated, FC * (f + 1) + 2)
                elif t is None:
                    pe.wait_ge(actl_done, FC * (f + 1))

            end_pe(pe, n, T_out, FC, acth, actl, [2, 3, 0, 1], ready)

        def ffn_act(act, f, T_in, T_out):
            with act.Fori(0, FC // 2) as i:
                for p in range(2):
                    act.wait_ge(w_used, T_in + p + 1 + i * 2)
                    nc.scalar.activation(sil[:, p, :], ps[:, 4 + 2 * p, :], ACT.Silu).then_inc(silu_done, 1)
                    hi_part(act, T_in + p + 2, i)
                    act.wait_ge(gated, FC * f + p + 3 + i * 2)
                    nc.scalar.copy(acth[:, bass.ds(i * 2 + p, 1), :].rearrange("p a n -> p (a n)"), afull[:, p, :]
                                   ).then_inc(acth_done, 1)
            for T in range(T_out + 2, T_out + 11):
                hi_part(act, T)

        def ffn_dve(dve, f, T_in, T_out):
            with dve.Fori(0, FC // 2) as i:
                for p in range(2):
                    dve.wait_ge(silu_done, FC * f + p + 1 + i * 2)
                    nc.vector.tensor_tensor(afull[:, p, :], sil[:, p, :], ps[:, 5 + 2 * p, :], ALU.mult
                                            ).then_inc(gated, 1)
                    lo_part(dve, T_in + p + 2, i)
                    dve.wait_ge(acth_done, FC * f + p + 1 + i * 2)
                    j = bass.ds(i * 2 + p, 1)
                    nc.vector.tensor_tensor(actl[:, j, :].rearrange("p a n -> p (a n)"), afull[:, p, :],
                                            acth[:, j, :].rearrange("p a n -> p (a n)").bitcast(F32),
                                            ALU.subtract).then_inc(actl_done, 1)
            for T in range(T_out + 2, T_out + 11):
                lo_part(dve, T)

        def seg(t, d):
            wf = (t + 1) * P
            return (slice(0, wf), slice(0, wf)) if d == 0 else (slice(wf, 640), slice(t * P, S))

        ROW = [(B2_QK, 4), (B2_QK + 2, 0), (B2_ROW, 4), (B2_ROW + 2, 0), (B2_ROW + 4, 4)]

        with layers() as (layer, block):
            one = lambda name: a[name][bass.ds(layer, 1)]

            def gains(eng, n):
                eng.dma_start(gbc[:], a["post_gain"][bass.ds(layer * 3 + (n + 2), 1)].to_broadcast([P, D])
                              ).then_inc(gain_in, 16)
                if n == 0:
                    eng.wait_ge(xn_done, 2)
                eng.dma_start(grow[:], a["next_gain"][bass.ds(layer * 3 + (n + 3), 1)].to_broadcast([P, D])
                              ).then_inc(gain_in, 16)

            @block.sync
            def _(sp):
                first_tiles(sp)
                sp.dma_start(gate_raw[:].rearrange("p a c -> p (a c)"), one("w_gate").rearrange("a p c -> (a p) c")
                             ).then_inc(par2, 16)
                sp.dma_start(gate_bias[:], one("gate_bias").to_broadcast([P, 16])).then_inc(par2, 16)
                sp.dma_start(conv_w[:].rearrange("p a c -> p (a c)"), one("conv_w").rearrange("a p c -> (a p) c")
                             ).then_inc(par2, 16)
                sp.dma_start(conv_b[:], one("conv_b").rearrange("a p c -> (a p) c")).then_inc(par2, 16)
                sp.dma_start(rot_cos[:], a["rot_cos"]).then_inc(par2, 16)
                sp.dma_start(rot_sin[:], a["rot_sin"]).then_inc(par2, 16)
                gains(sp, 0)
                stream(sp, layer * B2_TILES + DEPTH * B1_TILES, B2_TILES)
                for t in range(NT):
                    sp.wait_ge(x_done, 2 * NT + t + 1)
                    sp.dma_start(a["out"][0, t * P:(t + 1) * P, :], X[:, t, :]).then_inc(io, 16)
                sp.wait_ge(io, 16 * NT)

            @block.tensor
            def _(pe):
                ffn_pe(pe, 0, 0, -1, B2_IN1, B2_OUT1)
                project_pe(pe, ROW[0][0], 0, ROW[0][1], after=(0, 0))
                pe.wait_ge(mw_done, 1)
                for t in range(NT):
                    for k in range(NC):
                        last = three(ps[:, 3, 16 * t:16 * (t + 1)], hTh[:, k, t * P:(t + 1) * P],
                                     hTl[:, k, t * P:(t + 1) * P], gate_hi[:, k, :], gate_lo[:, k, :],
                                     k == 0, k == NC - 1)
                last.then_inc(sm_t, 1)
                project_pe(pe, ROW[1][0], 1, ROW[1][1],
                           bank_free=lambda t: t == 3 and pe.wait_ge(g_v, 1))
                for c in range(8):
                    T = B2_CONV + c // 2
                    if c % 4 == 0:
                        pe.wait_ge(ev_a, 2 * (c // 4 + 1))
                        pe.wait_ge(ev_v, 2 * (c // 4 + 1))
                    w_hi, w_lo = stationary(T)
                    pe.wait_ge(lo_ready, T + 1)
                    for k in range(NC):
                        last = three(ps[:, (c + 4) % 8, :], w_hi[:, c % 2, k, :], w_lo[:, c % 2, k, :], hTh[:, k, :],
                                     hTl[:, k, :], k == 0, k == NC - 1)
                    last.then_inc(w_used if c % 2 else cs_mm, 1)
                for b in (2, 3, 4):
                    if b == 4:
                        pe.wait_ge(ev_v, 8)
                    else:
                        pe.wait_ge(pad_done, 4 * (b - 1))
                    project_pe(pe, ROW[b][0], b, ROW[b][1])
                pe.wait_ge(ev_v, 12)
                pe.wait_ge(g_v, 3)
                pe.wait_ge(mixpar, 64)
                for t in range(NT):
                    for d in range(2):
                        others = range(t) if d == 0 else range(t + 1, NT)
                        out = ps[:, 0, 8 * t + 4 * d:8 * t + 4 * d + 4]
                        last = nc.tensor.matmul(out, upto[:, d, :], logf[:, t, d, :], start=True, stop=not len(others))
                        for o in others:
                            last = nc.tensor.matmul(out, ones[:].to_broadcast([P, P]), logf[:, o, d, :],
                                                    start=False, stop=o == others[-1])
                last.then_inc(sm_t, 1)
                pe.wait_ge(g_v, 4)
                pe.wait_ge(q_ready, NT)
                for c in range(8):
                    if c == 4:
                        pe.wait_ge(ev_a, 16)
                    for t in range(NT):
                        last = nc.tensor.transpose(ps[:, c, t * P:(t + 1) * P], P2[:, t, c * P:(c + 1) * P], ident[:])
                    last.then_inc(qt_done, 1)
                pe.wait_ge(qte_v, 8)
                attend_pe(pe, units2, buf2, lambda: pe.wait_ge(ev_v, 12), filler2)
                pe.wait_ge(o_done, len(units2))
                for t in range(NT):
                    last = nc.tensor.transpose(ps[0:8, 0, t * P:(t + 1) * P],
                                               acol[:, t, :, :].rearrange("p d h -> p (d h)"), ident[:])
                last.then_inc(sm_t, 1)
                pe.wait_ge(al_done, 1)
                for r in range(8):
                    row = identr[0:8, r:r + 1].to_broadcast([8, P])
                    nc.tensor.matmul(ps[:, r, :], row, aTh[0:8, :], start=True, stop=False)
                    nc.tensor.matmul(ps[:, r, :], row, aTl[0:8, :], start=False, stop=True).then_inc(sm_t, 1)
                pe.wait_ge(ab_a, 4)
                pe.wait_ge(ab_v, 4)

                def similar(t):
                    for h in range(MH):
                        if t:
                            pe.wait_ge(m2_done, MH * (t - 1) + h + 1)
                        three(ps[:, h, :], hTl[:, h, t * P:(t + 1) * P], MQKl[:, h, t * P:(t + 1) * P],
                              hTl[:, MH + h, :], MQKl[:, MH + h, :], True, True).then_inc(ms_done, 1)

                def values(t, h):
                    pe.wait_ge(mptl_done, MH * t + h + 1)
                    for b in range(NT):
                        last = three(ps[:, 6 + t % 2, h * P:(h + 1) * P], PT2h[:, h % 2, b, :], PT2l[:, h % 2, b, :],
                                     value_part(3, b, 0)[:, h * P:(h + 1) * P], value_part(3, b, 1)[:, h * P:(h + 1) * P],
                                     start=b == 0, stop=b == NT - 1)
                    if h == MH - 1:
                        last.then_inc(mpv_done, 1)

                pe.wait_ge(vl_done, 8)
                similar(0)
                for t in range(NT):
                    if t + 1 < NT:
                        similar(t + 1)
                    if t >= 2:
                        pe.wait_ge(o_ready, t - 1)
                    for h in range(MH):
                        pe.wait_ge(mg_done, MH * t + h + 1)
                        for b in range(NT):
                            col = b * P if b <= t else (b + 1) * P
                            last = nc.tensor.transpose(ps[:, 4 + h % 2, b * P:(b + 1) * P],
                                                       SW[:, t % 2, h, col:col + P], ident[:])
                        last.then_inc(mt_done, 1)
                        if h:
                            values(t, h - 1)
                    values(t, MH - 1)
                for t in TURN_ORDER:
                    pe.wait_ge(o_ready, NT if y_bank(t) == 6 else t + 1)
                    turn_pe(pe, P2[:, t, 0:D], t)
                end_pe(pe, 1, B2_MIXOUT, NC, hTh, hTl, TURN_ORDER,
                       lambda t: t is not None and pe.wait_ge(tl_done, count(1, TURN_ORDER.index(t))))
                ffn_pe(pe, 1, 2, 2, B2_IN2, B2_OUT2)

            @block.scalar
            def _(act):
                act.sem_inc(hi_ready, 1)
                late_act(act, -1, -1, 0)
                act.wait_ge(par2, par2_all)
                nc.scalar.copy(gate_hi[:], gate_raw[:]).then_inc(mr_done, 1)
                ffn_act(act, 0, B2_IN1, B2_OUT1)
                end_act(act, 0, 0, B2_OUT1 + 11)
                late_act(act, 0, 0, B2_OUT1 + 11)
                act.dma_start(BM[:], a["group_bias"]).then_inc(mixpar, 16)
                act.dma_start(masks[:], a["causal"]).then_inc(mixpar, 16)
                act.dma_start(mgain[:], one("mlstm_gain").to_broadcast([P, S])).then_inc(mixpar, 16)
                act.dma_start(upto[:], a["upto"]).then_inc(mixpar, 16)

                def evacuate(b):
                    T0, bank = ROW[b]
                    for t in (0, 2):
                        projected(act, T0, b, t)
                        nc.scalar.copy(P2[:, t, 512 * b:512 * (b + 1)], ps[:, bank + t, :]).then_inc(ev_a, 1)

                def conv_silu(c):
                    act.wait_ge(cv_done, c + 1)
                    nc.scalar.activation(MQK[:, c, :], acc[:, c % 2, :], ACT.Silu, bias=conv_b[:, c:c + 1]
                                         ).then_inc(cs_done, 1)

                for b in (0, 1):
                    hi_part(act, ROW[b][0] + 2)
                    if b == 1:
                        act.wait_ge(g_v, 2)
                        nc.scalar.activation(gexp[:], gtmp[:], ACT.Exp).then_inc(g_a, 1)
                        act.wait_ge(g_a, 1)
                        nc.scalar.activation(gexp[:], gexp[:], ACT.Ln, bias=1.0).then_inc(g_a, 1)
                    evacuate(b)
                    hi_part(act, ROW[b][0] + 3)
                act.wait_ge(g_p, 1)
                for c in range(8):
                    T = B2_CONV + c // 2
                    if c % 2:
                        hi_part(act, T + 2)
                        act.wait_ge(w_used, T + 1)
                    else:
                        act.wait_ge(cs_mm, c // 2 + 1)
                    if c >= 2:
                        act.wait_ge(cv_done, c - 1)
                    nc.scalar.copy(pad[:, c % 2, 2:S + 2], ps[:, (c + 4) % 8, :]).then_inc(pad_done, 1)
                    if c:
                        conv_silu(c - 1)
                conv_silu(7)
                for b in (2, 3, 4):
                    hi_part(act, ROW[b][0] + 2)
                    if b < 4:
                        for t in range(NT):
                            projected(act, ROW[b][0], b, t)
                            nc.scalar.copy(value_part(b, t, 0), ps[:, ROW[b][1] + t, :]).then_inc(ev_a, 1)
                    else:
                        for t in range(NT):
                            projected(act, ROW[b][0], b, t)
                            nc.scalar.activation(P2[:, t, 512 * b:512 * (b + 1)], ps[:, ROW[b][1] + t, :],
                                                 ACT.Sigmoid).then_inc(ev_a, 1)
                    hi_part(act, ROW[b][0] + 3)
                for c in range(8):
                    act.wait_ge(qt_done, c + 1)
                    nc.scalar.activation(hTh[:, c, :], ps[:, c, :], ACT.Copy, scale=0.125 if c < 4 else 1.0
                                         ).then_inc(qte_a, 1)
                attend_act(act, units2, buf2)
                act.wait_ge(sm_t, 3)
                nc.scalar.copy(identr[:], ident[:])
                nc.scalar.copy(aTh[0:8, :], ps[0:8, 0, :]).then_inc(sm_e, 1)
                for c in (0, 4, 1, 5, 2, 6, 3, 7):
                    nc.scalar.copy(hTl[:, c, :], MQK[:, c, :]).then_inc(vh_done, 1)
                for r in range(0, 8, 2):
                    act.wait_ge(sm_t, 3 + r + 1)
                    nc.scalar.copy(AB[:, r, :], ps[:, r, :]).then_inc(ab_a, 1)

                def weights(t):
                    act.wait_ge(m1_done, t + 1)
                    for h in range(MH):
                        for d in range(2):
                            w = SW[:, t % 2, h, seg(t, d)[0]]
                            nc.scalar.activation(w, w, ACT.Exp, bias=nmmax[:, t, d, h:h + 1])
                    nc.scalar.activation(mexp[:, t, :, :], dtmp[:, t, :, :], ACT.Exp).then_inc(mw2_done, 1)

                def cell_squares(t):
                    act.wait_ge(mpv_done, t + 1)
                    for h in range(MH):
                        last = nc.scalar.activation(junk[:, h * P:(h + 1) * P], ps[:, 6 + t % 2, h * P:(h + 1) * P], ACT.Square,
                                                    accum_out=osum[:, t, h:h + 1])
                    last.then_inc(g_a, 1)

                weights(0)
                weights(1)
                for t in range(NT):
                    for h in range(MH):
                        act.wait_ge(mt_done, MH * t + h + 1)
                        nc.scalar.copy(PT2h[:, h % 2, :, :].rearrange("p b n -> p (b n)"), ps[:, 4 + h % 2, :]
                                       ).then_inc(mpt_done, 1)
                    if t + 2 < NT:
                        weights(t + 2)
                    cell_squares(t)
                for pos, t in enumerate(TURN_ORDER):
                    turn_act(act, 1, t, pos)
                gains(act, 1)
                hi_part(act, B2_MIXOUT + 2)
                hi_part(act, B2_MIXOUT + 3)
                end_act(act, 1, 2, B2_MIXOUT + 4)
                late_act(act, 1, 2, B2_MIXOUT + 4)
                gains(act, 2)
                ffn_act(act, 1, B2_IN2, B2_OUT2)
                end_act(act, 2, 3, B2_TILES)

            @block.vector
            def _(dve):
                chain = Chain(dve, dchain)
                nc.vector.memset(ones[:], 1.0).then_inc(one_done, 1)
                dve.sem_inc(lo_ready, 1)
                dve.sem_inc(gated, 2)
                late_dve(dve, -1, -1, 0)
                dve.wait_ge(mr_done, 1)
                nc.vector.tensor_tensor(gate_lo[:], gate_raw[:], gate_hi[:].bitcast(F32), ALU.subtract
                                        ).then_inc(mw_done, 1)
                ffn_dve(dve, 0, B2_IN1, B2_OUT1)
                end_dve(dve, chain, 0, 0, B2_OUT1 + 11)
                late_dve(dve, 0, 0, B2_OUT1 + 11)
                f = gates[:, :, :, 1, :]

                def gates_in():
                    dve.wait_ge(sm_t, 1)
                    nc.vector.tensor_tensor(gates[:].rearrange("p t d g h -> p t (d g h)"),
                                            ps[:, 3, 0:64].rearrange("p (t g) -> p t g", t=NT),
                                            gate_bias[:].unsqueeze(1).to_broadcast([P, NT, 16]), ALU.add
                                            ).then_inc(g_v, 1)
                    dve.wait_ge(g_v, 1)
                    chain(nc.vector.tensor_scalar(gtmp[:], f, -1.0, None, ALU.mult))
                    nc.vector.tensor_tensor(gtmp[:], gtmp[:], f, ALU.min).then_inc(g_v, 1)

                def evacuate(b):
                    T0, bank = ROW[b]
                    for t in (1, 3):
                        projected(dve, T0, b, t)
                        nc.vector.tensor_copy(P2[:, t, 512 * b:512 * (b + 1)], ps[:, bank + t, :]).then_inc(ev_v, 1)

                def rotary(t):
                    x = P2[:, t, 0:1024].rearrange("p (n d) -> p n d", d=HD)
                    x1, x2 = x[:, :, 0:8], x[:, :, 8:16]
                    c3 = rot_cos[:, t, :].unsqueeze(1).to_broadcast([P, 16, 8])
                    s3 = rot_sin[:, t, :].unsqueeze(1).to_broadcast([P, 16, 8])
                    A, B, C = (rt[:, t % 2, j, :].rearrange("p (n d) -> p n d", d=8) for j in range(3))
                    nc.vector.tensor_tensor(A, x1, s3, ALU.mult)
                    nc.vector.tensor_tensor(B, x2, s3, ALU.mult)
                    chain(nc.vector.tensor_tensor(C, x2, c3, ALU.mult))
                    chain(nc.vector.tensor_tensor(x1, x1, c3, ALU.mult))
                    nc.vector.tensor_tensor(x2, C, A, ALU.add)
                    nc.vector.tensor_tensor(x1, x1, B, ALU.subtract).then_inc(q_ready, 1)

                def convolve(c):
                    dve.wait_ge(pad_done, c + 1)
                    if c >= 2:
                        dve.wait_ge(cs_done, c - 1)
                    o, x = acc[:, c % 2, :], pad[:, c % 2, :]
                    chain(nc.vector.tensor_scalar(o, x[:, 0:S], conv_w[:, c, 0:1], None, ALU.mult))
                    for w in range(1, CONV):
                        ins = nc.vector.scalar_tensor_tensor(o, x[:, w:w + S], conv_w[:, c, w:w + 1], o,
                                                             ALU.mult, ALU.add)
                        if w < CONV - 1:
                            chain(ins)
                    ins.then_inc(cv_done, 1)

                dve.wait_ge(par2, par2_all)
                for b in (0, 1):
                    lo_part(dve, ROW[b][0] + 2)
                    evacuate(b)
                    lo_part(dve, ROW[b][0] + 3)
                    if b == 0:
                        gates_in()
                    else:
                        dve.wait_ge(g_a, 2)
                        nc.vector.scalar_tensor_tensor(logf[:], f, 0.0, gexp[:], ALU.min, ALU.subtract
                                                       ).then_inc(g_v, 1)
                for c in range(8):
                    if c % 2:
                        lo_part(dve, B2_CONV + c // 2 + 2)
                    convolve(c)
                for b in (2, 3, 4):
                    lo_part(dve, ROW[b][0] + 2)
                    if b < 4:
                        for t in range(NT):
                            dve.wait_ge(ev_a, 4 * (b - 1) + t + 1)
                            nc.vector.tensor_tensor(value_part(b, t, 1), ps[:, ROW[b][1] + t, :],
                                                    value_part(b, t, 0).bitcast(F32), ALU.subtract
                                                    ).then_inc(ev_v, 1)
                    if b == 2:
                        dve.wait_ge(ev_a, 4)
                        dve.wait_ge(ev_v, 4)
                        for t in range(NT):
                            rotary(t)
                    lo_part(dve, ROW[b][0] + 3)
                dve.wait_ge(sm_t, 2)
                nc.vector.tensor_copy(cum[:].rearrange("p t d h -> p (t d h)"), ps[:, 0, 0:32]).then_inc(g_v, 1)
                dve.wait_ge(g_v, 4)
                chain(nc.vector.tensor_tensor(acol[:], gates[:, :, :, 0, :], cum[:], ALU.subtract))
                for c in range(8):
                    dve.wait_ge(qte_a, c + 1)
                    nc.vector.scalar_tensor_tensor(hTl[:, c, :], ps[:, c, :], 0.125 if c < 4 else 1.0,
                                                   hTh[:, c, :].bitcast(F32), ALU.mult, ALU.subtract
                                                   ).then_inc(qte_v, 1)
                dve.wait_ge(mixpar, 64)
                dve.wait_ge(g_p, 2)
                attend_dve(dve, chain, units2, buf2)
                dve.wait_ge(sm_e, 1)
                nc.vector.tensor_tensor(aTl[0:8, :], ps[0:8, 0, :], aTh[0:8, :].bitcast(F32), ALU.subtract
                                        ).then_inc(al_done, 1)
                for i, c in enumerate((0, 4, 1, 5, 2, 6, 3, 7)):
                    dve.wait_ge(vh_done, i + 1)
                    nc.vector.tensor_tensor(MQKl[:, c, :], MQK[:, c, :], hTl[:, c, :].bitcast(F32), ALU.subtract
                                            ).then_inc(vl_done, 1)
                for r in range(1, 8, 2):
                    dve.wait_ge(sm_t, 3 + r + 1)
                    nc.vector.tensor_copy(AB[:, r, :], ps[:, r, :]).then_inc(ab_v, 1)
                dve.wait_ge(ab_a, 4)
                dve.wait_ge(ab_v, 4)

                def decay(t):
                    for h in range(MH):
                        for d in range(2):
                            dst, src = seg(t, d)
                            mask = masks[:, 0, 384 - P * t:S] if d == 0 else masks[:, 1, 0:S - P * t]
                            last = nc.vector.tensor_tensor_reduce(
                                out=SW[:, t % 2, h, dst], in0=AB[:, MH * d + h, src], in1=mask, scale=1.0,
                                scalar=-3.0e38, op0=ALU.add, op1=ALU.max, accum_out=mmax[:, t, d, h:h + 1])
                    chain(last)
                    chain(nc.vector.tensor_scalar(nmmax[:, t, :, :], mmax[:, t, :, :], -1.0, None, ALU.mult))
                    nc.vector.tensor_tensor(dtmp[:, t, :, :], nmmax[:, t, :, :], cum[:, t, :, :], ALU.subtract
                                            ).then_inc(m1_done, 1)

                def weigh(t):
                    dve.wait_ge(mw2_done, t + 1)
                    for h in range(MH):
                        dve.wait_ge(ms_done, MH * t + h + 1)
                        for d in range(2):
                            dst, src = seg(t, d)
                            w = SW[:, t % 2, h, dst]
                            last = nc.vector.tensor_tensor_reduce(
                                out=w, in0=ps[:, h, src], in1=w, scale=P ** -0.5, scalar=0.0,
                                op0=ALU.mult, op1=ALU.add, accum_out=den[:, t, d, h:h + 1])
                        last.then_inc(m2_done, 1)
                    dve.wait_ge(m2_done, MH * (t + 1))
                    chain(nc.vector.tensor_scalar(drec[:, t, :, :], den[:, t, :, :], -1.0, None, ALU.mult))
                    chain(nc.vector.tensor_tensor(drec[:, t, :, :], drec[:, t, :, :], den[:, t, :, :], ALU.max))
                    chain(nc.vector.tensor_tensor(drec[:, t, :, :], drec[:, t, :, :], mexp[:, t, :, :], ALU.max))
                    chain(nc.vector.reciprocal(drec[:, t, :, :], drec[:, t, :, :]))
                    for h in range(MH):
                        for d in range(2):
                            w = SW[:, t % 2, h, seg(t, d)[0]]
                            last = nc.vector.tensor_scalar(w, w, drec[:, t, d, h:h + 1], None, ALU.mult)
                        chain(last)
                        w = SW[:, t % 2, h, :]
                        nc.vector.tensor_tensor(w[:, t * P:(t + 1) * P], w[:, t * P:(t + 1) * P],
                                                w[:, (t + 1) * P:(t + 2) * P], ALU.add).then_inc(mg_done, 1)
                        if h >= 2:
                            low(t, h - 2)

                def low(t, h):
                    dve.wait_ge(mpt_done, MH * t + h + 1)
                    nc.vector.tensor_tensor(PT2l[:, h % 2, :, :].rearrange("p b n -> p (b n)"), ps[:, 4 + h % 2, :],
                                            PT2h[:, h % 2, :, :].rearrange("p b n -> p (b n)").bitcast(F32),
                                            ALU.subtract).then_inc(mptl_done, 1)

                def cell(t):
                    dve.wait_ge(g_p, 2 + t + 1)
                    for h in range(MH):
                        o = 512 + h * P
                        last = nc.vector.scalar_tensor_tensor(
                            P2[:, t, o:o + P], ps[:, 6 + t % 2, h * P:(h + 1) * P], oinv[:, t, h:h + 1],
                            P2[:, t, 1536 + o:1536 + o + P], ALU.mult, ALU.mult)
                    last.then_inc(o_ready, 1)

                decay(0)
                decay(1)
                for t in range(NT):
                    weigh(t)
                    if t:
                        cell(t - 1)
                    low(t, 2)
                    low(t, 3)
                    if t + 2 < NT:
                        dve.wait_ge(mt_done, MH * (t + 1))
                        decay(t + 2)
                cell(NT - 1)
                for pos, t in enumerate(TURN_ORDER):
                    turn_dve(dve, 1, t, pos)
                lo_part(dve, B2_MIXOUT + 2)
                lo_part(dve, B2_MIXOUT + 3)
                end_dve(dve, chain, 1, 2, B2_MIXOUT + 4)
                late_dve(dve, 1, 2, B2_MIXOUT + 4)
                ffn_dve(dve, 1, B2_IN2, B2_OUT2)
                end_dve(dve, chain, 2, 3, B2_TILES)

            @block.gpsimd
            def _(pool):
                chain = Chain(pool, pchain)
                late_pool(pool, chain, -1)
                end_pool(pool, chain, 0, 0.5)
                late_pool(pool, chain, 0)
                pool.wait_ge(xn_done, count(0, 3))
                nc.gpsimd.memset(pad[:, :, 0:2], 0.0)
                nc.gpsimd.memset(pad[:, :, S + 2:S + 4], 0.0).then_inc(g_p, 1)
                pool.wait_ge(mixpar, 64)
                pool.wait_ge(ev_a, 16)
                for t in range(NT):
                    last = nc.gpsimd.tensor_tensor(P2[:, t, 2048:2560], P2[:, t, 2048:2560], mgain[:], ALU.mult)
                last.then_inc(g_p, 1)
                for t in range(NT):
                    pool.wait_ge(g_a, 2 + t + 1)
                    chain(nc.gpsimd.tensor_scalar(osum[:, t, 0:MH], osum[:, t, 0:MH], 1.0 / P, EPS,
                                                  ALU.mult, ALU.add))
                    nc.gpsimd.tensor_tensor(oinv[:, t, 0:MH], osum[:, t, 0:MH], halfneg[:].to_broadcast([P, MH]),
                                            ALU.pow).then_inc(g_p, 1)
                end_pool(pool, chain, 1, 1.0)
                late_pool(pool, chain, 1)
                end_pool(pool, chain, 2, 0.5)
    return nc


def moving_tiles(w):
    L, K, N = w.shape
    b = w.reshape(L, K // P, P, N // 512, 512).transpose(0, 3, 1, 2, 4).reshape(L, -1, 4, P, 512)
    return b.transpose(0, 1, 3, 2, 4).reshape(L, -1, P, TILE)


def stationary_tiles(w):
    L, _, n, _ = w.shape
    return w.reshape(L, NC, P, n // 2, 2, P).transpose(0, 3, 2, 4, 1, 5).reshape(L, n // 2, P, TILE)


def rope_tables(pos, dim, theta):
    inv = (np.float32(theta) ** (-np.arange(0, dim, 2, dtype=np.float32) / np.float32(dim))).astype(np.float32)
    ang = pos.astype(np.float32)[:, None] * inv[None, :]
    return np.cos(ang).astype(np.float32), np.sin(ang).astype(np.float32)


def by_token(t):
    return np.ascontiguousarray(np.moveaxis(t.reshape(NT, P, *t.shape[1:]), 0, 1))


def constants():
    pos = np.arange(S)
    c = {"identity": np.eye(P, dtype=np.float32)}
    cos, sin = rope_tables(pos, 32, 10000.0)
    c["lin_cos"], c["lin_sin"] = by_token(cos), by_token(sin)
    rc, rs = rope_tables(pos // 64, 32, 10000.0)
    cc, cs = rope_tables(pos % 64, 32, 10000.0)
    c["ax_cos"], c["ax_sin"] = by_token(np.stack([rc, cc], 1)), by_token(np.stack([rs, cs], 1))
    cos, sin = rope_tables(pos, 16, 500000.0)
    c["rot_cos"], c["rot_sin"] = by_token(cos), by_token(sin)
    gap = np.abs(pos[:, None] - pos[None, :])
    count = sum(((gap % dil == 0) & (gap // dil <= 64)).astype(np.int64) for dil in (1, 4, 16))
    bias = np.where(count > 0, np.log(np.maximum(count, 1)), NEG).astype(np.float32)
    c["group_bias"] = by_token(bias)
    p, s = np.arange(P)[:, None], np.arange(P)[None, :]
    zero = np.zeros((P, 384), np.float32)
    c["causal"] = np.stack([np.concatenate([zero, np.where(s <= p, 0, NEG).astype(np.float32)], 1),
                            np.concatenate([np.where(s >= p, 0, NEG).astype(np.float32), zero], 1)], 1)
    c["upto"] = np.stack([(p <= s).astype(np.float32), (p >= s).astype(np.float32)], 1)
    li = [0.8 - 0.6 * math.exp(-0.3 * l) for l in range(DEPTH)]
    c["lambda_init"] = np.array([[v, 1.0 - v] for v in li], np.float32)
    return c


def lay_out(x, mem, pre_norm, w_in, diff_lambda, diff_subln, gqa_q_norm, gqa_k_norm, mem_norm, w_mem_kv,
            w_out, post_norm, norm_gain_2, ffn_w_in_2, ffn_w_out_2, mix_w_in_2, conv_w_2, conv_b_2,
            gate_bias_2, mlstm_norm_gain_2, mix_w_out_2):
    L = DEPTH
    cut = lambda w, lo, hi: w[:, :, lo:hi]
    gq = cut(w_in, 1536, 1920).reshape(L, D, 2, 3, HD).transpose(0, 1, 3, 2, 4).reshape(L, D, 384)
    proj = np.concatenate([cut(w_in, 0, 768), gq, cut(w_in, 1920, 2048), cut(w_in, 2560, 2816),
                           cut(w_in, 768, 1152), cut(w_in, 2048, 2176), cut(w_in, 1152, 1536),
                           cut(w_in, 2176, 2560), cut(w_in, 2816, 3072)], 2)
    mem_v = cut(w_mem_kv, 256, 512).reshape(L, NC, P, 256).transpose(0, 2, 1, 3).reshape(L, 1, P, TILE)
    w1 = np.concatenate([moving_tiles(proj), stationary_tiles(cut(w_mem_kv, 0, 256).reshape(L, D, 2, P)), mem_v,
                         moving_tiles(w_out)], 1)

    def ffn(i):
        w = ffn_w_in_2[:, i].reshape(L, D, 2, FC, P).transpose(0, 1, 3, 2, 4).reshape(L, D, 2 * FC, P)
        return [stationary_tiles(w), moving_tiles(ffn_w_out_2[:, i])]

    m = mix_w_in_2
    w2 = np.concatenate(ffn(0) + [moving_tiles(cut(m, 0, 1024)),
                                  stationary_tiles(cut(m, 1536, 2560).reshape(L, D, 8, P)),
                                  moving_tiles(np.concatenate([cut(m, 1024, 1536), cut(m, 2560, 3584)], 2)),
                                  moving_tiles(mix_w_out_2)] + ffn(1), 1)
    weights = np.concatenate([w1.reshape(-1, P, TILE), w2.reshape(-1, P, TILE), np.zeros((2, P, TILE), np.float32)])
    g = norm_gain_2
    pre = [g[:, i:i + 1] for i in (0, 2, 4)]
    post = [g[:, i:i + 1] for i in (1, 3, 5)]
    arrays = {
        "x": x, "mem": mem, "weights": weights, "mem_norm": mem_norm.reshape(L, NC, P).transpose(0, 2, 1),
        "next_gain": np.concatenate([pre_norm, np.concatenate(pre, 1).reshape(-1, D), np.zeros((1, D), np.float32)]),
        "post_gain": np.concatenate([post_norm, np.concatenate(post, 1).reshape(-1, D)]),
        "diff_lambda": diff_lambda.reshape(L, 128), "diff_subln": diff_subln,
        "gqa_q_norm": gqa_q_norm, "gqa_k_norm": gqa_k_norm,
        "w_gate": cut(m, 3584, 3600).reshape(L, NC, P, 16).transpose(0, 2, 1, 3).reshape(L, P, 128),
        "gate_bias": gate_bias_2.reshape(L, 16),
        "conv_w": conv_w_2.reshape(L, CONV, 8, P).transpose(0, 3, 2, 1).reshape(L, P, 40),
        "conv_b": conv_b_2.reshape(L, 8, P).transpose(0, 2, 1),
        "mlstm_gain": mlstm_norm_gain_2,
    }
    return {k: np.ascontiguousarray(v) for k, v in {**arrays, **constants()}.items()}


def kernel(**inputs):
    import concourse.bacc as bacc
    from concourse.bass_utils import run_bass_kernel_spmd

    arrays = lay_out(**{k: np.asarray(v) for k, v in inputs.items()})
    nc = bacc.Bacc("TRN2", target_bir_lowering=False, num_devices=1)
    aps = {k: nc.dram_tensor(f"in_{k}", v.shape, F32, kind="ExternalInput").ap() for k, v in arrays.items()}
    aps["out"] = nc.dram_tensor("out", (1, S, D), F32, kind="ExternalOutput").ap()
    build(nc, aps)
    r = run_bass_kernel_spmd(nc, [{f"in_{k}": v for k, v in arrays.items()}], core_ids=[0])
    return r.results[0]["out"]
```
